# Optimizing a Trainium2 kernel written in Bass

```python
import math
import jax, jax.numpy as jnp
from jax import lax
import numpy as np

D_MODEL = 1024
BATCH = 1
SEQ = 1024
DEPTH = 1

N_FOX_HEADS = 8
FOX_HEAD_DIM = 64
FOX_WIDTH = N_FOX_HEADS * FOX_HEAD_DIM
N_DIFF_HEADS = 4
DIFF_QK_DIM = 64
DIFF_V_DIM = 2 * DIFF_QK_DIM
DIFF_QK_WIDTH = N_DIFF_HEADS * 2 * DIFF_QK_DIM
DIFF_WIDTH = N_DIFF_HEADS * DIFF_V_DIM
MIX_WIDTH = FOX_WIDTH + DIFF_WIDTH
IN_SIZES = (FOX_WIDTH, FOX_WIDTH, FOX_WIDTH, N_FOX_HEADS,
            DIFF_QK_WIDTH, DIFF_QK_WIDTH, DIFF_WIDTH)
IN_WIDTH = sum(IN_SIZES)
IN_SPLITS = tuple(int(v) for v in np.cumsum(IN_SIZES)[:-1])
ROPE_THETA = 500000.0
ROPE_DIM = DIFF_QK_DIM // 4
D_FF = 2816
FFN_RESIDUAL_WEIGHT = 0.5
Q_BLOCK = 128
RMS_EPS = 1e-6


def rms_norm(x, g):
    xf = x.astype(jnp.float32)
    y = xf * lax.rsqrt(jnp.mean(xf * xf, axis=-1, keepdims=True) + RMS_EPS)
    return (y * g.astype(jnp.float32)).astype(x.dtype)

def swiglu(x, w_gate, w_up, w_down):
    return (jax.nn.silu(x @ w_gate) * (x @ w_up)) @ w_down

def to_heads(t, n_heads):
    b, s, _ = t.shape
    return t.reshape(b, s, n_heads, -1).transpose(0, 2, 1, 3)

def from_heads(t):
    b, h, s, d = t.shape
    return t.transpose(0, 2, 1, 3).reshape(b, s, h * d)

def partial_rope(t, pos):
    half = ROPE_DIM // 2
    inv_freq = ROPE_THETA ** (-jnp.arange(0, ROPE_DIM, 2, dtype=jnp.float32) / ROPE_DIM)
    ang = pos.astype(jnp.float32)[:, None] * inv_freq[None, :]
    cos, sin = jnp.cos(ang), jnp.sin(ang)
    tf = t.astype(jnp.float32)
    x1, x2, rest = tf[..., :half], tf[..., half:ROPE_DIM], tf[..., ROPE_DIM:]
    out = jnp.concatenate([x1 * cos - x2 * sin, x2 * cos + x1 * sin, rest], axis=-1)
    return out.astype(t.dtype)

def causal_block_attention(q, k, v, log_decay_cum=None):
    seq = q.shape[2]
    scale = q.shape[-1] ** -0.5
    outs = []
    for i in range(seq // Q_BLOCK):
        q0, q1 = i * Q_BLOCK, (i + 1) * Q_BLOCK
        s = jnp.einsum('bhqd,bhkd->bhqk', q[:, :, q0:q1], k[:, :, :q1]).astype(jnp.float32) * scale
        if log_decay_cum is not None:
            s = s + log_decay_cum[:, :, q0:q1, None] - log_decay_cum[:, :, None, :q1]
        mask = jnp.arange(q1)[None, :] <= jnp.arange(q0, q1)[:, None]
        s = jnp.where(mask, s, jnp.finfo(jnp.float32).min)
        p = jax.nn.softmax(s, axis=-1).astype(v.dtype)
        outs.append(jnp.einsum('bhqk,bhkd->bhqd', p, v[:, :, :q1]))
    return jnp.concatenate(outs, axis=2)

def token_mixer(h, w_in, fox_forget_b, lam_q1, lam_k1, lam_q2, lam_k2, subln_g, w_out, layer):
    b, s, _ = h.shape
    pos = jnp.arange(s)
    proj = h @ w_in
    fq, fk, fv, fgate, dq, dk, dv = jnp.split(proj, IN_SPLITS, axis=-1)

    log_f = jax.nn.log_sigmoid(fgate.astype(jnp.float32) + fox_forget_b.astype(jnp.float32))
    c = jnp.cumsum(log_f, axis=1).transpose(0, 2, 1)
    fox_o = causal_block_attention(to_heads(fq, N_FOX_HEADS), to_heads(fk, N_FOX_HEADS),
                                   to_heads(fv, N_FOX_HEADS), c)
    fox_o = from_heads(fox_o)

    dq = dq.reshape(b, s, N_DIFF_HEADS, 2, DIFF_QK_DIM)
    dk = dk.reshape(b, s, N_DIFF_HEADS, 2, DIFF_QK_DIM)
    hd = lambda t: partial_rope(t.transpose(0, 2, 1, 3), pos)
    q1, q2 = hd(dq[..., 0, :]), hd(dq[..., 1, :])
    k1, k2 = hd(dk[..., 0, :]), hd(dk[..., 1, :])
    v = to_heads(dv, N_DIFF_HEADS)
    lam_init = 0.8 - 0.6 * math.exp(-0.3 * layer)
    lam = (jnp.exp(jnp.sum(lam_q1.astype(jnp.float32) * lam_k1.astype(jnp.float32)))
           - jnp.exp(jnp.sum(lam_q2.astype(jnp.float32) * lam_k2.astype(jnp.float32)))
           + lam_init)
    a1 = causal_block_attention(q1, k1, v)
    a2 = causal_block_attention(q2, k2, v)
    diff_o = a1 - lam.astype(a1.dtype) * a2
    diff_o = rms_norm(diff_o, subln_g) * (1.0 - lam_init)
    diff_o = from_heads(diff_o)

    return jnp.concatenate([fox_o, diff_o], axis=-1) @ w_out

def first_inputs(seed: int = 0) -> dict:
    key = jax.random.key(seed)
    ks = jax.random.split(key, 24)
    L = DEPTH
    nrm = lambda k, shape, scale: jax.random.normal(k, shape, jnp.float32) * scale
    gain = lambda k, n: 1.0 + 0.02 * jax.random.normal(k, (L, n), jnp.float32)
    return {
        "x": jax.random.normal(ks[0], (BATCH, SEQ, D_MODEL), jnp.float32),
        "ffn1_pre_g": gain(ks[1], D_MODEL),
        "ffn1_post_g": gain(ks[2], D_MODEL),
        "ffn1_w_gate": nrm(ks[3], (L, D_MODEL, D_FF), D_MODEL ** -0.5),
        "ffn1_w_up": nrm(ks[4], (L, D_MODEL, D_FF), D_MODEL ** -0.5),
        "ffn1_w_down": nrm(ks[5], (L, D_FF, D_MODEL), D_FF ** -0.5),
        "mix_pre_g": gain(ks[6], D_MODEL),
        "mix_post_g": gain(ks[7], D_MODEL),
        "w_in": nrm(ks[8], (L, D_MODEL, IN_WIDTH), D_MODEL ** -0.5),
        "fox_forget_b": nrm(ks[9], (L, N_FOX_HEADS), 0.02),
        "diff_lambda_q1": nrm(ks[10], (L, DIFF_QK_DIM), 0.1),
        "diff_lambda_k1": nrm(ks[11], (L, DIFF_QK_DIM), 0.1),
        "diff_lambda_q2": nrm(ks[12], (L, DIFF_QK_DIM), 0.1),
        "diff_lambda_k2": nrm(ks[13], (L, DIFF_QK_DIM), 0.1),
        "diff_subln_g": gain(ks[14], DIFF_V_DIM),
        "w_out": nrm(ks[15], (L, MIX_WIDTH, D_MODEL), MIX_WIDTH ** -0.5),
        "ffn2_pre_g": gain(ks[16], D_MODEL),
        "ffn2_post_g": gain(ks[17], D_MODEL),
        "ffn2_w_gate": nrm(ks[18], (L, D_MODEL, D_FF), D_MODEL ** -0.5),
        "ffn2_w_up": nrm(ks[19], (L, D_MODEL, D_FF), D_MODEL ** -0.5),
        "ffn2_w_down": nrm(ks[20], (L, D_FF, D_MODEL), D_FF ** -0.5),
    }

def first_block(x, ffn1_pre_g, ffn1_post_g, ffn1_w_gate, ffn1_w_up, ffn1_w_down,
              mix_pre_g, mix_post_g, w_in, fox_forget_b,
              diff_lambda_q1, diff_lambda_k1, diff_lambda_q2, diff_lambda_k2, diff_subln_g,
              w_out, ffn2_pre_g, ffn2_post_g, ffn2_w_gate, ffn2_w_up, ffn2_w_down):
    for l in range(DEPTH):
        f1 = swiglu(rms_norm(x, ffn1_pre_g[l]), ffn1_w_gate[l], ffn1_w_up[l], ffn1_w_down[l])
        x = x + FFN_RESIDUAL_WEIGHT * rms_norm(f1, ffn1_post_g[l])
        m = token_mixer(rms_norm(x, mix_pre_g[l]), w_in[l], fox_forget_b[l],
                        diff_lambda_q1[l], diff_lambda_k1[l], diff_lambda_q2[l], diff_lambda_k2[l],
                        diff_subln_g[l], w_out[l], l)
        x = x + rms_norm(m, mix_post_g[l])
        f2 = swiglu(rms_norm(x, ffn2_pre_g[l]), ffn2_w_gate[l], ffn2_w_up[l], ffn2_w_down[l])
        x = x + FFN_RESIDUAL_WEIGHT * rms_norm(f2, ffn2_post_g[l])
    return x


DEPTH_2 = 2

CHUNK = 64
N_META = 16
EPS = 1e-6
N_EVEN = (DEPTH_2 + 1) // 2
N_ODD = DEPTH_2 // 2
CONV_W = 4

LRU_WIDTH = D_MODEL
LRU_BLOCKS = 4
LRU_BLOCK = LRU_WIDTH // LRU_BLOCKS
RG_LRU_C = 8.0

SSD_WIDTH = D_MODEL
SSD_HEAD_DIM = 64
SSD_HEADS = SSD_WIDTH // SSD_HEAD_DIM
SSD_GROUPS = 2
SSD_HPG = SSD_HEADS // SSD_GROUPS
SSD_STATE = 128
SSD_CHUNK = CHUNK
SSD_CONV_DIM = SSD_WIDTH + 2 * SSD_GROUPS * SSD_STATE

EVEN_SPLITS = (LRU_WIDTH, 2 * LRU_WIDTH, 2 * LRU_WIDTH + SSD_WIDTH,
               2 * LRU_WIDTH + SSD_WIDTH + SSD_CONV_DIM)
EVEN_IN = 2 * LRU_WIDTH + SSD_WIDTH + SSD_CONV_DIM + SSD_HEADS
EVEN_MIX = LRU_WIDTH + SSD_WIDTH

SB_HEADS = 16
SB_HEAD_DIM = D_MODEL // SB_HEADS
SB_WIDTH = SB_HEADS * SB_HEAD_DIM
SB_BLOCK = 128
ODD_IN = 4 * SB_WIDTH


def rmsnorm(x, w):
    xf = x.astype(jnp.float32)
    y = xf * lax.rsqrt(jnp.mean(xf * xf, axis=-1, keepdims=True) + EPS)
    return (y * w.astype(jnp.float32)).astype(x.dtype)

def causal_dwconv(u, w, b):
    out = lax.conv_general_dilated(
        u, w[:, None, :].astype(u.dtype), window_strides=(1,),
        padding=[(CONV_W - 1, 0)], dimension_numbers=('NWC', 'WIO', 'NWC'),
        feature_group_count=u.shape[-1])
    return out + b

def linear_scan(a, b):
    def combine(left, right):
        al, bl = left
        ar, br = right
        return al * ar, ar * bl + br
    _, h = lax.associative_scan(combine, (a, b), axis=1)
    return h

def rg_lru(u, w_a, b_a, w_x, b_x, lam):
    bsz, L, _ = u.shape
    uf = u.astype(jnp.float32)
    ub = uf.reshape(bsz, L, LRU_BLOCKS, LRU_BLOCK)
    r = jax.nn.sigmoid(jnp.einsum('blgi,gij->blgj', ub, w_a).reshape(bsz, L, LRU_WIDTH) + b_a)
    i = jax.nn.sigmoid(jnp.einsum('blgi,gij->blgj', ub, w_x).reshape(bsz, L, LRU_WIDTH) + b_x)
    log_a = -RG_LRU_C * r * jax.nn.softplus(-lam)
    a = jnp.exp(log_a)
    mult = jnp.sqrt(-jnp.expm1(2.0 * log_a))
    return linear_scan(a, mult * i * uf)

def ssd_scan(xh, dt, a, bmat, cmat):
    bsz, L, _, _ = xh.shape
    pad = (-L) % SSD_CHUNK
    def padf(t):
        return jnp.pad(t, [(0, 0), (pad, 0)] + [(0, 0)] * (t.ndim - 2))
    f32 = jnp.float32
    xdt = padf((xh * dt[..., None]).astype(f32))
    adt = padf((dt * a).astype(f32))
    bm = padf(bmat.astype(f32))
    cm = padf(cmat.astype(f32))
    nc = (L + pad) // SSD_CHUNK
    X = xdt.reshape(bsz, nc, SSD_CHUNK, SSD_GROUPS, SSD_HPG, SSD_HEAD_DIM)
    A = adt.reshape(bsz, nc, SSD_CHUNK, SSD_GROUPS, SSD_HPG).transpose(0, 3, 4, 1, 2)
    Bc = bm.reshape(bsz, nc, SSD_CHUNK, SSD_GROUPS, SSD_STATE)
    Cc = cm.reshape(bsz, nc, SSD_CHUNK, SSD_GROUPS, SSD_STATE)
    a_cum = jnp.cumsum(A, axis=-1)
    tri = jnp.tril(jnp.ones((SSD_CHUNK, SSD_CHUNK), bool))
    seg = a_cum[..., :, None] - a_cum[..., None, :]
    decay = jnp.exp(jnp.where(tri, seg, -jnp.inf))
    cb = jnp.einsum('bclgn,bcsgn->bcgls', Cc, Bc)
    y_diag = jnp.einsum('bcgls,bgecls,bcsgep->bclgep', cb, decay, X)
    decay_states = jnp.exp(a_cum[..., -1:] - a_cum)
    states = jnp.einsum('bclgn,bgecl,bclgep->bcgepn', Bc, decay_states, X)
    chunk_tot = jnp.pad(a_cum[..., -1], [(0, 0), (0, 0), (0, 0), (1, 0)])
    cs = jnp.cumsum(chunk_tot, axis=-1)
    tri_c = jnp.tril(jnp.ones((nc + 1, nc + 1), bool))
    decay_chunk = jnp.exp(jnp.where(tri_c, cs[..., :, None] - cs[..., None, :], -jnp.inf))
    states = jnp.concatenate([jnp.zeros_like(states[:, :1]), states], axis=1)
    states = jnp.einsum('bgezc,bcgepn->bzgepn', decay_chunk, states)[:, :-1]
    y_off = jnp.einsum('bclgn,bcgepn,bgecl->bclgep', Cc, states, jnp.exp(a_cum))
    y = (y_diag + y_off).reshape(bsz, L + pad, SSD_HEADS, SSD_HEAD_DIM)
    return y[:, pad:]

def gated_group_rmsnorm(y, z, w):
    bsz, L, W = y.shape
    g = (y * jax.nn.silu(z.astype(jnp.float32))).reshape(bsz, L, SSD_GROUPS, W // SSD_GROUPS)
    g = g * lax.rsqrt(jnp.mean(g * g, axis=-1, keepdims=True) + EPS)
    return g.reshape(bsz, L, W) * w.astype(jnp.float32)

def rglru_ssd_layer(h, norm_w, w_in, lru_conv_w, lru_conv_b, lru_w_a, lru_b_a,
                    lru_w_x, lru_b_x, lru_lambda, ssd_conv_w, ssd_conv_b,
                    ssd_dt_bias, ssd_a_log, ssd_d, ssd_norm, w_out):
    bsz, L, _ = h.shape
    u = rmsnorm(h, norm_w)
    proj = u @ w_in
    lru_x, lru_g, ssd_z, ssd_xbc, ssd_dt = jnp.split(proj, EVEN_SPLITS, axis=-1)
    lx = causal_dwconv(lru_x, lru_conv_w, lru_conv_b)
    y_a = rg_lru(lx, lru_w_a, lru_b_a, lru_w_x, lru_b_x, lru_lambda) * jax.nn.silu(lru_g.astype(jnp.float32))
    xbc = jax.nn.silu(causal_dwconv(ssd_xbc, ssd_conv_w, ssd_conv_b))
    xs, bm, cm = jnp.split(xbc, (SSD_WIDTH, SSD_WIDTH + SSD_GROUPS * SSD_STATE), axis=-1)
    dt = jax.nn.softplus(ssd_dt.astype(jnp.float32) + ssd_dt_bias)
    a = -jnp.exp(ssd_a_log.astype(jnp.float32))
    xh = xs.reshape(bsz, L, SSD_HEADS, SSD_HEAD_DIM)
    y = ssd_scan(xh, dt, a,
                 bm.reshape(bsz, L, SSD_GROUPS, SSD_STATE),
                 cm.reshape(bsz, L, SSD_GROUPS, SSD_STATE))
    y = y + xh.astype(jnp.float32) * ssd_d[:, None]
    y_b = gated_group_rmsnorm(y.reshape(bsz, L, SSD_WIDTH), ssd_z, ssd_norm)
    mixed = jnp.concatenate([y_a, y_b], axis=-1).astype(h.dtype)
    return h + mixed @ w_out

def stick_breaking_block(q_blk, k_ctx, v_ctx, q0):
    tq = q_blk.shape[1]
    s_len = k_ctx.shape[1]
    z = jnp.einsum('bthd,bshd->bhts', q_blk.astype(jnp.float32),
                   k_ctx.astype(jnp.float32)) * (SB_HEAD_DIM ** -0.5)
    before = jnp.arange(s_len)[None, :] < (q0 + jnp.arange(tq))[:, None]
    log_keep = jnp.where(before, jax.nn.log_sigmoid(-z), 0.0)
    csum = jnp.cumsum(log_keep, axis=-1)
    weights = jnp.where(before, jnp.exp(jax.nn.log_sigmoid(z) + csum[..., -1:] - csum), 0.0)
    return jnp.einsum('bhts,bshd->bthd', weights, v_ctx.astype(jnp.float32))

def stick_breaking_layer(h, norm_w, w_in, w_out):
    bsz, L, _ = h.shape
    u = rmsnorm(h, norm_w)
    q, k, v, g = jnp.split(u @ w_in, 4, axis=-1)
    q = q.reshape(bsz, L, SB_HEADS, SB_HEAD_DIM)
    k = k.reshape(bsz, L, SB_HEADS, SB_HEAD_DIM)
    v = v.reshape(bsz, L, SB_HEADS, SB_HEAD_DIM)
    bounds = [0] + list(range(N_META, L, SB_BLOCK)) + [L]
    outs = [stick_breaking_block(q[:, s:e], k[:, :e], v[:, :e], s)
            for s, e in zip(bounds[:-1], bounds[1:])]
    o = jnp.concatenate(outs, axis=1).reshape(bsz, L, SB_WIDTH)
    o = (o * jax.nn.silu(g.astype(jnp.float32))).astype(h.dtype)
    return h + o @ w_out

def second_inputs(seed: int = 0) -> dict:
    key = jax.random.key(seed)
    ks = jax.random.split(key, 24)
    f32 = jnp.float32

    def nrm(k, shape, fan_in):
        return jax.random.normal(k, shape, f32) * (fan_in ** -0.5)

    def gain(k, shape):
        return 1.0 + 0.05 * jax.random.normal(k, shape, f32)

    def bias(k, shape, s=0.05):
        return s * jax.random.normal(k, shape, f32)

    x = jax.random.normal(ks[0], (BATCH, SEQ, D_MODEL), f32)
    meta = jax.random.normal(ks[1], (N_META, D_MODEL), f32)
    even_norm = gain(ks[2], (N_EVEN, D_MODEL))
    even_w_in = nrm(ks[3], (N_EVEN, D_MODEL, EVEN_IN), D_MODEL)
    lru_conv_w = nrm(ks[4], (N_EVEN, CONV_W, LRU_WIDTH), CONV_W)
    lru_conv_b = bias(ks[5], (N_EVEN, LRU_WIDTH))
    lru_w_a = nrm(ks[6], (N_EVEN, LRU_BLOCKS, LRU_BLOCK, LRU_BLOCK), LRU_BLOCK)
    lru_b_a = bias(ks[7], (N_EVEN, LRU_WIDTH), 0.1)
    lru_w_x = nrm(ks[8], (N_EVEN, LRU_BLOCKS, LRU_BLOCK, LRU_BLOCK), LRU_BLOCK)
    lru_b_x = bias(ks[9], (N_EVEN, LRU_WIDTH), 0.1)
    a_c = jax.random.uniform(ks[10], (N_EVEN, LRU_WIDTH), f32, minval=0.9, maxval=0.999)
    a0 = a_c ** (1.0 / RG_LRU_C)
    lru_lambda = jnp.log(a0) - jnp.log1p(-a0)
    ssd_conv_w = nrm(ks[11], (N_EVEN, CONV_W, SSD_CONV_DIM), CONV_W)
    ssd_conv_b = bias(ks[12], (N_EVEN, SSD_CONV_DIM))
    dt0 = jnp.exp(jax.random.uniform(ks[13], (N_EVEN, SSD_HEADS), f32,
                                     minval=float(np.log(1e-3)), maxval=float(np.log(1e-1))))
    ssd_dt_bias = dt0 + jnp.log(-jnp.expm1(-dt0))
    ssd_a_log = jnp.log(jax.random.uniform(ks[14], (N_EVEN, SSD_HEADS), f32, minval=1.0, maxval=16.0))
    ssd_d = gain(ks[15], (N_EVEN, SSD_HEADS))
    ssd_norm = gain(ks[16], (N_EVEN, SSD_WIDTH))
    even_w_out = nrm(ks[17], (N_EVEN, EVEN_MIX, D_MODEL), EVEN_MIX)
    odd_norm = gain(ks[18], (N_ODD, D_MODEL))
    odd_w_in = nrm(ks[19], (N_ODD, D_MODEL, ODD_IN), D_MODEL)
    odd_w_out = nrm(ks[20], (N_ODD, SB_WIDTH, D_MODEL), SB_WIDTH)
    final_norm = gain(ks[21], (D_MODEL,))
    return {'x': x, 'meta': meta, 'even_norm': even_norm, 'even_w_in': even_w_in,
            'lru_conv_w': lru_conv_w, 'lru_conv_b': lru_conv_b,
            'lru_w_a': lru_w_a, 'lru_b_a': lru_b_a, 'lru_w_x': lru_w_x, 'lru_b_x': lru_b_x,
            'lru_lambda': lru_lambda, 'ssd_conv_w': ssd_conv_w, 'ssd_conv_b': ssd_conv_b,
            'ssd_dt_bias': ssd_dt_bias, 'ssd_a_log': ssd_a_log, 'ssd_d': ssd_d,
            'ssd_norm': ssd_norm, 'even_w_out': even_w_out, 'odd_norm': odd_norm,
            'odd_w_in': odd_w_in, 'odd_w_out': odd_w_out, 'final_norm': final_norm}

def second_block(x, meta, even_norm, even_w_in, lru_conv_w, lru_conv_b, lru_w_a, lru_b_a,
              lru_w_x, lru_b_x, lru_lambda, ssd_conv_w, ssd_conv_b, ssd_dt_bias,
              ssd_a_log, ssd_d, ssd_norm, even_w_out, odd_norm, odd_w_in, odd_w_out,
              final_norm):
    bsz = x.shape[0]
    meta_b = jnp.broadcast_to(meta[None].astype(x.dtype), (bsz, N_META, D_MODEL))
    h = jnp.concatenate([meta_b, x], axis=1)
    for layer in range(DEPTH_2):
        j = layer // 2
        if layer % 2 == 0:
            h = rglru_ssd_layer(h, even_norm[j], even_w_in[j], lru_conv_w[j], lru_conv_b[j],
                                lru_w_a[j], lru_b_a[j], lru_w_x[j], lru_b_x[j], lru_lambda[j],
                                ssd_conv_w[j], ssd_conv_b[j], ssd_dt_bias[j], ssd_a_log[j],
                                ssd_d[j], ssd_norm[j], even_w_out[j])
        else:
            h = stick_breaking_layer(h, odd_norm[j], odd_w_in[j], odd_w_out[j])
    return rmsnorm(h, final_norm)[:, N_META:].astype(x.dtype)


def setup_inputs(seed=0):
    out = dict(first_inputs(seed))
    for name, value in second_inputs(seed + 1).items():
        if name != "x":
            out[name + "_2"] = value
    return out


def reference(
    x, ffn1_pre_g, ffn1_post_g, ffn1_w_gate, ffn1_w_up, ffn1_w_down, mix_pre_g, mix_post_g,
    w_in, fox_forget_b, diff_lambda_q1, diff_lambda_k1, diff_lambda_q2, diff_lambda_k2,
    diff_subln_g, w_out, ffn2_pre_g, ffn2_post_g, ffn2_w_gate, ffn2_w_up, ffn2_w_down, meta_2,
    even_norm_2, even_w_in_2, lru_conv_w_2, lru_conv_b_2, lru_w_a_2, lru_b_a_2, lru_w_x_2,
    lru_b_x_2, lru_lambda_2, ssd_conv_w_2, ssd_conv_b_2, ssd_dt_bias_2, ssd_a_log_2, ssd_d_2,
    ssd_norm_2, even_w_out_2, odd_norm_2, odd_w_in_2, odd_w_out_2, final_norm_2,
):
    x = first_block(
        x, ffn1_pre_g, ffn1_post_g, ffn1_w_gate, ffn1_w_up, ffn1_w_down, mix_pre_g, mix_post_g,
        w_in, fox_forget_b, diff_lambda_q1, diff_lambda_k1, diff_lambda_q2, diff_lambda_k2,
        diff_subln_g, w_out, ffn2_pre_g, ffn2_post_g, ffn2_w_gate, ffn2_w_up, ffn2_w_down,
    )
    return second_block(
        x, meta_2, even_norm_2, even_w_in_2, lru_conv_w_2, lru_conv_b_2, lru_w_a_2, lru_b_a_2,
        lru_w_x_2, lru_b_x_2, lru_lambda_2, ssd_conv_w_2, ssd_conv_b_2, ssd_dt_bias_2,
        ssd_a_log_2, ssd_d_2, ssd_norm_2, even_w_out_2, odd_norm_2, odd_w_in_2, odd_w_out_2,
        final_norm_2,
    )


_drawn_inputs = setup_inputs


def setup_inputs(seed=0):
    import zlib

    import numpy as np

    out = dict(_drawn_inputs(seed))
    spreads = {}
    factors = {'ffn1_post_g': 3.858,
     'mix_post_g': 3.456,
     'fox_forget_b': 8.0,
     'diff_lambda_q1': 8.0,
     'diff_subln_g': 4.391,
     'ffn2_pre_g': 5.502,
     'ffn2_post_g': 7.944,
     'lru_b_a_2': 8.0,
     'lru_b_x_2': 5.633,
     'ssd_d_2': 4.597,
     'ssd_norm_2': 2.852,
     'odd_norm_2': 3.24}
    for name, (base, spread) in spreads.items():
        noise = np.random.default_rng([zlib.crc32(name.encode()), seed]).standard_normal(out[name].shape)
        drawn = base * np.exp(spread * noise) if base else spread * noise
        out[name] = __import__('jax').numpy.asarray(drawn.astype(out[name].dtype))
    for name, factor in factors.items():
        out[name] = (out[name] * factor).astype(out[name].dtype)
    return out
```

```python
import math

import concourse.bass as bass
from concourse import mybir
import numpy as np

D = 1024
T1 = 1024
META = 16
T2 = T1 + META
FF = 2816
EPS = 1e-6
NEG = -1e30
FFN_CHUNKS = [(0, 512), (512, 1024)]
CHUNKS = [(0, 352), (352, 704), (704, 1040)]

UNITS = []
for _f in (1, 2):
    UNITS += [f"G{_f}.{j}" for j in range(22)]
    UNITS += [f"U{_f}.{j}" for j in range(22)]
    UNITS += [f"D{_f}.{b}.{c}" for b in range(11) for c in range(2)]
UNITS += [f"IN.{i}" for i in range(25)]
UNITS += [f"OUT.{i}" for i in range(8)]
UNITS += [f"E.{i}" for i in range(37)]
UNITS += [f"L.{g}" for g in range(4)]
UNITS += [f"EO.{g}.{c}" for g in range(4) for c in range(2)]
UNITS += [f"EB.{i}" for i in range(8)]
UNITS += [f"Q.{i}" for i in range(32)]
UNITS += [f"QO.{i}" for i in range(8)]
UNIT_AT = {name: n for n, name in enumerate(UNITS)}

VEC = {}
_n = 0
for _name, _w in [("ffn1_pre_g", 8), ("ffn1_post_g", 8), ("mix_pre_g", 8), ("mix_post_g", 8),
                  ("ffn2_pre_g", 8), ("ffn2_post_g", 8), ("even_norm_2", 8), ("odd_norm_2", 8),
                  ("final_norm_2", 8), ("lru_conv_w_2", 32), ("lru_conv_b_2", 8), ("lru_b_a_2", 8),
                  ("lru_b_x_2", 8), ("lru_lambda_2", 8), ("ssd_conv_w_2", 48), ("ssd_conv_b_2", 12),
                  ("ssd_norm_2", 8), ("fox_forget_b", 1), ("ssd_dt_bias_2", 1),
                  ("ssd_a_log_2", 16), ("ssd_d_2", 16)]:
    VEC[_name] = _n
    _n += _w
NVEC = _n
MATS = ["ident", "ones", "rot"]
MATS2 = ["triu", "low", "ntri", "nones"]


class Prog:

    ENG = ("pe", "act", "dve", "pool", "sp")

    def __init__(self):
        self.q = {e: [] for e in self.ENG}
        self.n = {e: 0 for e in self.ENG}
        self.waited = {}
        self.dman = {}

    def wait(self, eng, toks):
        for t in toks:
            if t is None:
                continue
            if isinstance(t, list):
                self.wait(eng, t)
                continue
            sem, v = t
            if self.waited.get((eng, sem), 0) < v:
                self.waited[(eng, sem)] = v
                self.q[eng].append(("wait", sem, v))

    def do(self, eng, fn, *toks):
        self.wait(eng, toks)
        self.n[eng] += 1
        self.q[eng].append(("ins", fn, eng, 1))
        return (eng, self.n[eng])

    def act(self, fn, *toks):
        return self.do("act", fn, *toks)

    def dve(self, fn, *toks):
        return self.do("dve", fn, *toks)

    def pool(self, fn, *toks):
        return self.do("pool", fn, *toks)

    def act_raw(self, fn):
        self.q["act"].append(("ins", fn, None, 0))

    def pe(self, fns, *toks):
        self.wait("pe", toks)
        for fn in fns[:-1]:
            self.q["pe"].append(("ins", fn, None, 0))
        self.n["pe"] += 1
        self.q["pe"].append(("ins", fns[-1], "pe", 1))
        return ("pe", self.n["pe"])

    def dma(self, eng, sem, fn, *toks):
        self.wait(eng, toks)
        self.dman[sem] = self.dman.get(sem, 0) + 16
        self.q[eng].append(("ins", fn, sem, 16))
        return (sem, self.dman[sem])


class Weights:

    NRAW, NSPL = 2, 3

    def __init__(self, P, order, dram, raw, hi, lo, COPY, SUB):
        self.P, self.order, self.dram = P, order, dram
        self.raw, self.hi, self.lo = raw, hi, lo
        self.COPY, self.SUB = COPY, SUB
        self.asked = []
        self.nload = self.nsplit = 0
        self.loaded, self.parted, self.free = {}, {}, {}

    def _load(self, i):
        s = i % self.NRAW
        src = self.dram[UNIT_AT[self.order[i]]]
        dst = self.raw[s][:, :]
        self.loaded[i] = self.P.dma("sp", f"w{s}", lambda e: e.dma_start(dst, src),
                                    self.parted.get(i - self.NRAW))

    def _split(self, i):
        s, r = i % self.NSPL, i % self.NRAW
        raw, hi, lo, COPY, SUB = self.raw[r], self.hi[s], self.lo[s], self.COPY, self.SUB
        n = {"D": 1024, "L": 1024}.get(self.order[i][0], 1024)
        a = self.P.act(lambda e: e.activation(hi[:, 0:n], raw[:, 0:n], COPY),
                       self.loaded[i], self.free.get(i - self.NSPL))
        b = self.P.pool(lambda e: e.tensor_tensor(lo[:, 0:n], raw[:, 0:n], hi[:, 0:n], SUB),
                        self.loaded[i], self.free.get(i - self.NSPL), a)
        self.parted[i] = [a, b]

    def get(self, name):
        i = len(self.asked)
        self.asked.append(name)
        if self.order is None:
            return i, self.hi[0], self.lo[0], []
        assert self.order[i] == name
        while self.nsplit <= min(i + 1, len(self.order) - 1):
            while self.nload <= min(self.nsplit + 1, len(self.order) - 1):
                if self.nload >= self.NRAW and (self.nload - self.NRAW) not in self.parted:
                    break
                self._load(self.nload)
                self.nload += 1
            self._split(self.nsplit)
            self.nsplit += 1
        while self.nload < len(self.order) and (self.nload - self.NRAW) in self.parted:
            self._load(self.nload)
            self.nload += 1
        return i, self.hi[i % self.NSPL], self.lo[i % self.NSPL], self.parted[i]

    def done(self, i, tok):
        self.free[i] = tok


def emit(nc, A, S, order):
    ALU = mybir.AluOpType
    ACT = mybir.ActivationFunctionType
    AX = mybir.AxisListType
    P = Prog()
    W = Weights(P, order, A["w"], S["raw"], S["whi"], S["wlo"], ACT.Copy, ALU.subtract)
    PS = S["ps"]
    bankfree = {b: [] for b in range(8)}
    RES, XH, XL = S["res"], S["xh"], S["xl"]
    TT = S["t"]
    vec, mat = S["vec"], S["mat"]

    def v(name, i=0):
        c = VEC[name] + i
        return vec[:, c:c + 1]

    def m(name):
        if name in MATS2:
            i = MATS2.index(name)
            return S["mat2"][:, i * 128:(i + 1) * 128]
        i = MATS.index(name)
        return mat[:, i * 128:(i + 1) * 128]

    def bank(b, n=512, p0=0, p1=128):
        return PS[p0:p1, b * 512:b * 512 + n]

    def load(eng, sem, dst, src, *toks):
        return P.dma(eng, sem, lambda e: e.dma_start(dst, src), *toks)

    tc = [load("act", "cst", vec[:, :], A["vec"]), load("act", "cst", mat[:, :], A["mat"]),
          load("act", "cst", TT[0][:, 0:256], A["masks"])]
    tc = tc[-1]
    idb, cmb, smb = S["idb"], S["cmb"], S["smb"]
    tb = [P.dve(lambda e: e.tensor_copy(idb[:, :], m("ident")), tc),
          P.dve(lambda e: e.tensor_copy(cmb[:, :], TT[0][:, 0:128]), tc),
          P.dve(lambda e: e.tensor_copy(smb[:, :], TT[0][:, 128:256]), tc)][-1]

    def mm3(out, whi, wlo, xhi, xlo, first, last):
        return [lambda e: e.matmul(out, whi, xhi, start=first, stop=False),
                lambda e: e.matmul(out, wlo, xhi, start=False, stop=False),
                lambda e: e.matmul(out, whi, xlo, start=False, stop=last)]

    def group(b, n, parts, *toks):
        fns = []
        for k, (wh, wl, xh, xl) in enumerate(parts):
            fns += mm3(bank(b, n), wh, wl, xh, xl, k == 0, k == len(parts) - 1)
        t = P.pe(fns, bankfree[b], *toks)
        bankfree[b] = [t]
        return t

    def unit8(wh, wl, c0, c1, XHt=None, XLt=None, K=8):
        XHt, XLt = XHt or XH, XLt or XL
        return [(wh[:, k * 128:(k + 1) * 128], wl[:, k * 128:(k + 1) * 128],
                 XHt[:, k, c0:c1], XLt[:, k, c0:c1]) for k in range(K)]

    tfree = {i: [] for i in range(4)}
    tfree[0] = [tb]

    def msq(src, KT, c0, c1, srctoks, b, sq=0, t1=1, r=2, dim=D):
        n = c1 - c0
        SQ, R = TT[sq][:, 0:n], TT[r][:, 0:n]
        pend = None
        for k in range(KT):
            x = src(k, c0, c1)
            if k == 0:
                pend = P.act(lambda e, x=x: e.activation(SQ, x, ACT.Square), tfree[sq], srctoks)
            else:
                tt = TT[t1 if k % 2 else 3][:, 0:n]
                slot = t1 if k % 2 else 3
                a = P.act(lambda e, tt=tt, x=x: e.activation(tt, x, ACT.Square), tfree[slot], srctoks)
                pend = P.dve(lambda e, tt=tt: e.tensor_tensor(SQ, SQ, tt, ALU.add), a, pend)
                tfree[slot] = [pend]
        g = P.pe([lambda e: e.matmul(bank(b, n), m("ones"), SQ, start=True, stop=True)],
                 pend, bankfree[b], tc)
        V, N = SQ, TT[t1][:, 0:n]
        d = P.dve(lambda e: e.tensor_scalar(V, bank(b, n), 1.0 / dim, EPS, ALU.mult, ALU.add), g)
        bankfree[b] = [d]
        a = P.act(lambda e: e.activation(R, V, ACT.Ln), d, tfree[r])
        a = P.act(lambda e: e.activation(R, R, ACT.Exp, scale=-0.5), a)
        d = P.dve(lambda e: e.scalar_tensor_tensor(N, R, 1.0, V, ALU.mult, ALU.mult), a, tfree[t1])
        d = P.dve(lambda e: e.scalar_tensor_tensor(N, N, -0.5, R, ALU.mult, ALU.mult), d)
        tfree[sq] = [d]
        d = P.dve(lambda e: e.tensor_scalar(N, N, 1.5, None, ALU.add), d)
        d2 = P.dve(lambda e: e.tensor_tensor(R, R, N, ALU.mult), d)
        tfree[r] = tfree[t1] = [d2]
        return d2

    def norm_split(src, KT, chunks, gname, srctoks, free, b0=0, k0=0, dim=D):
        toks = []
        for ci, (c0, c1) in enumerate(chunks):
            n = c1 - c0
            R = TT[2][:, 0:n]
            tr = msq(src, KT, c0, c1, srctoks[ci], b0, dim=dim)
            for k in range(KT):
                slot = 3 if k % 2 else 1
                tmp = TT[slot][:, 0:n]
                x = src(k, c0, c1)
                gk = v(gname, k0 + k)
                xh, xl = XH[:, k0 + k, c0:c1], XL[:, k0 + k, c0:c1]
                d = P.dve(lambda e, x=x, gk=gk, tmp=tmp, R=R: e.scalar_tensor_tensor(
                    tmp, x, gk, R, ALU.mult, ALU.mult), tr, tfree[slot], tc)
                a = P.act(lambda e, xh=xh, tmp=tmp: e.activation(xh, tmp, ACT.Copy), d, free)
                p = P.dve(lambda e, xl=xl, xh=xh, tmp=tmp: e.tensor_tensor(
                    xl, tmp, xh, ALU.subtract), a, free)
                tfree[slot] = [p]
            tfree[2] = [d]
            toks.append([a, p])
        return toks

    def post_norm(acc, gname, factor, acctoks, chunks, free=None):
        toks = []
        for ci, (c0, c1) in enumerate(chunks):
            n = c1 - c0
            R = TT[2][:, 0:n]
            src = lambda k, a, b: acc[:, k, a:b]
            tr = msq(src, 8, c0, c1, acctoks[ci], 0)
            for k in range(8):
                slot = 3 if k % 2 else 1
                tmp = TT[slot][:, 0:n]
                x, gk, y = acc[:, k, c0:c1], v(gname, k), RES[:, k, META + c0:META + c1]
                d = P.dve(lambda e, x=x, gk=gk, tmp=tmp, R=R: e.scalar_tensor_tensor(
                    tmp, x, gk, R, ALU.mult, ALU.mult), tr, tfree[slot])
                d = P.dve(lambda e, y=y, tmp=tmp: e.scalar_tensor_tensor(
                    y, tmp, factor, y, ALU.mult, ALU.add), d)
                tfree[slot] = [d]
            tfree[2] = [d]
            toks.append([d])
        return toks

    res_src = lambda k, a, b: RES[:, k, META + a:META + b]
    h_src = lambda k, a, b: RES[:, k, a:b]

    def ffn(f, restoks, xfree):
        ACC, H_H, H_L = S["acc"], S["hh"], S["hl"]
        T = FFN_CHUNKS
        xt = norm_split(res_src, 8, T, f"ffn{f}_pre_g", restoks, xfree)
        hfree = {s: [] for s in range(4)}
        hready = {}
        acctok = [None, None]
        nb = [0]

        def gate_up(j):
            ig, gh, gl, gt = W.get(f"G{f}.{j}")
            iu, uh, ul, ut = W.get(f"U{f}.{j}")
            s = j % 4
            for c, (c0, c1) in enumerate(T):
                b = 2 * ((2 * j + c) % 2)
                tg = group(b, 512, unit8(gh, gl, c0, c1), gt, xt[c])
                tu = group(b + 1, 512, unit8(uh, ul, c0, c1), ut)
                ta, tb_, = (0, 1) if c == 0 else (2, 3)
                ea, eb = TT[ta][:, :], TT[tb_][:, :]
                g_, u_ = bank(b), bank(b + 1)
                hh, hl = H_H[:, s, c0:c1], H_L[:, s, c0:c1]
                d1 = P.act(lambda e, ea=ea, g_=g_: e.activation(ea, g_, ACT.Silu), tg, tfree[ta])
                d2 = P.dve(lambda e, ea=ea, eb=eb, u_=u_: e.tensor_tensor(eb, u_, ea, ALU.mult),
                           d1, tu, tfree[tb_])
                bankfree[b], bankfree[b + 1] = [d1], [d2]
                a = P.act(lambda e, hh=hh, eb=eb: e.activation(hh, eb, ACT.Copy), d2, hfree[s])
                p = P.pool(lambda e, hh=hh, hl=hl, eb=eb: e.tensor_tensor(hl, eb, hh, ALU.subtract), a)
                tfree[ta], tfree[tb_] = [d2], [p]
                hready[j, c] = [a, p]
            W.done(ig, tg)
            W.done(iu, tu)

        def down(b):
            tl = None
            for h in range(2):
                iw, wh, wl, wt = W.get(f"D{f}.{b}.{h}")
                for fi in range(4):
                    ft = 4 * h + fi
                    for c, (c0, c1) in enumerate(T):
                        pb = 4 + nb[0] % 4
                        nb[0] += 1
                        parts = []
                        for k in range(2):
                            o = k * 512 + fi * 128
                            s = (2 * b + k) % 4
                            parts.append((wh[:, o:o + 128], wl[:, o:o + 128],
                                          H_H[:, s, c0:c1], H_L[:, s, c0:c1]))
                        tl = group(pb, 512, parts, wt, hready[2 * b, c], hready[2 * b + 1, c])
                        acc, pp = ACC[:, ft, c0:c1], bank(pb)
                        if b == 0:
                            d = P.dve(lambda e, acc=acc, pp=pp: e.tensor_copy(acc, pp), tl)
                        else:
                            d = P.dve(lambda e, acc=acc, pp=pp: e.tensor_tensor(acc, acc, pp, ALU.add), tl)
                        bankfree[pb] = [d]
                        acctok[c] = [d]
                W.done(iw, tl)
            for k in range(2):
                hfree[(2 * b + k) % 4] = [tl]

        for b in range(11):
            gate_up(2 * b)
            if b:
                down(b - 1)
            gate_up(2 * b + 1)
        xdone = ("pe", P.n["pe"])
        down(10)
        rt = post_norm(ACC, f"ffn{f}_post_g", 0.5, acctok, T)
        return rt, [xdone]

    def act_(out, in_, func, **kw):
        return lambda e: e.activation(out, in_, func, **kw)

    def tt_(out, a, b, op):
        return lambda e: e.tensor_tensor(out, a, b, op)

    def ts_(out, a, s1, s2, op0, op1=ALU.bypass):
        return lambda e: e.tensor_scalar(out, a, s1, s2, op0, op1)

    def stt_(out, a, s1, b, op0, op1):
        return lambda e: e.scalar_tensor_tensor(out, a, s1, b, op0, op1)

    def cp_(out, a):
        return lambda e: e.tensor_copy(out, a)

    def mm_(out, lhsT, rhs, start=True, stop=True, skip=False):
        return lambda e: e.matmul(out, lhsT, rhs, start=start, stop=stop, skip_group_check=skip)

    def tr_(out, in_, n=128):
        return lambda e: e.transpose(out, in_, m("ident")[0:n, 0:n])

    def exp_ln_tables():
        P.act_raw(lambda e: e.preload_act_table_set("natural_log_exp_and_others"))

    def softplus(out, tmp, src, srctok, tmpfree, outfree):
        d = P.dve(ts_(tmp, src, 40.0, None, ALU.min), srctok, tmpfree)
        a = P.act(act_(tmp, tmp, ACT.Exp), d)
        a = P.act(act_(tmp, tmp, ACT.Ln, bias=1.0), a)
        return P.dve(tt_(out, src, tmp, ALU.max), a, outfree)

    def mixer(restoks, xfree):
        M = S["mix"]
        OT, QT, KT_, VT = S["ot"], M["q"], M["k"], M["vt"]
        NCB, NC8, COS, SIN = M["ncb"], M["nc8"], M["cos"], M["sin"]
        PT, PP, OTM, SM, LAM = M["pt"], M["p"], M["otm"], M["sm"], M["lam"]
        T = FFN_CHUNKS
        exp_ln_tables()
        tlam = load("act", "lam", LAM[:, :], A["lam"], restoks[1])
        xt = norm_split(res_src, 8, T, "mix_pre_g", restoks, xfree)
        SUBG = LAM[:, 256:384]
        sm = lambda i, n=1: SM[:, i:i + n]
        d = []
        for i in range(2):
            q, k = LAM[:, 128 * i:128 * i + 64], LAM[:, 128 * i + 64:128 * i + 128]
            d1 = P.dve(lambda e, q=q, k=k, i=i: e.scalar_tensor_tensor(
                q, q, 1.0, k, ALU.mult, ALU.mult, accum_out=sm(i)), tlam)
            d.append(P.act(act_(sm(i), sm(i), ACT.Exp), d1))
        d1 = P.dve(tt_(sm(0), sm(0), sm(1), ALU.subtract), d)
        tnl = P.dve(ts_(sm(0), sm(0), 0.2, -1.0, ALU.add, ALU.mult), d1)
        tsg = P.dve(ts_(SUBG, SUBG, 0.8, None, ALU.mult), tlam)
        NLAM = sm(0)
        i24, wh, wl, wt = W.get("IN.24")
        tg = []
        for c, (c0, c1) in enumerate(T):
            tg.append(group(c, 512, unit8(wh, wl, c0, c1), wt, xt[c]))
        W.done(i24, tg[1])
        z8 = PT[0][0:8, 0:1024]
        e8 = PT[1][0:8, 0:1024]
        fb = v("fox_forget_b")[0:8, :]
        for c, (c0, c1) in enumerate(T):
            d = P.dve(ts_(z8[:, c0:c1], bank(c, 512, 0, 8), fb, -1.0, ALU.add, ALU.mult), tg[c], tc)
            bankfree[c] = [d]
        d = softplus(z8, e8, z8, d, None, None)
        dz = P.dve(lambda e: e.memset(e8, 0.0), d)
        dn = P.dve(lambda e: e.tensor_tensor_scan(NC8[0:8, :], z8, e8, 0.0, ALU.add, ALU.add), dz, d)
        CT = sm(64, 64)
        tct = P.pe([mm_(PS[:, 8 * b:8 * b + 8], NC8[0:8, 128 * b:128 * b + 128], m("ident")[0:8, 0:8])
                    for b in range(8)], dn, bankfree[0])
        dct = P.dve(cp_(CT, PS[:, 0:64]), tct)
        bankfree[0] = [dct]
        ptfree = [[dn], [dn]]
        pfree = [tfree[0] + tfree[1], tfree[2] + tfree[3]]
        qfree, kfree, vfree, ncfree, otmfree = [], [], [], [dn], []
        rope_free = []
        trope = None
        smfree = {}
        pend = []

        def project(unit, dst, scale, free, b0):
            iw, wh, wl, wt = W.get(unit)
            out = []
            for c, (c0, c1) in enumerate(T):
                t = group(b0 + c, 512, unit8(wh, wl, c0, c1), wt, xt[c])
                a = P.act(act_(dst[:, c0:c1], bank(b0 + c), ACT.Copy, scale=scale), t, free)
                bankfree[b0 + c] = [a]
                out.append(a)
            W.done(iw, t)
            return out

        def rope(X, toks):
            for c, (c0, c1) in enumerate(T):
                t = P.pe([mm_(bank(2 + c), m("rot"), X[:, c0:c1])], toks[c], bankfree[2 + c])
                tmp = PT[1][:, c0:c1]
                d1 = P.dve(tt_(tmp, bank(2 + c), SIN[:, c0:c1], ALU.mult), t, ptfree[1], trope)
                bankfree[2 + c] = [d1]
                d2 = P.dve(tt_(X[:, c0:c1], X[:, c0:c1], COS[:, c0:c1], ALU.mult), toks[c], t)
                toks[c] = P.dve(tt_(X[:, c0:c1], X[:, c0:c1], tmp, ALU.add), d1, d2)
            ptfree[1] = [toks[1]]
            return toks

        state = {}

        def stage_a(n, t, qb, i):
            nk = 128 * (qb + 1)
            pb = n % 2
            b0 = 2 * pb
            fns = []
            for c0 in range(0, nk, 512):
                c1 = min(nk, c0 + 512)
                o = PS[:, b0 * 512 + c0:b0 * 512 + c1]
                last = c1 == nk
                fns.append(mm_(o, QT[64 * i:64 * i + 64, 128 * qb:128 * qb + 128],
                               KT_[64 * i:64 * i + 64, c0:c1], True, not last))
            fns.append(mm_(PS[:, b0 * 512 + nk - 128:b0 * 512 + nk], idb[:, :], cmb[:, :], False, True))
            ts = P.pe(fns, state["q"], state["k"], bankfree[b0], bankfree[b0 + 1], tb)
            state["sdone"] = ts
            pp = PP[pb][:, 0:nk]
            src = PS[:, b0 * 512:b0 * 512 + nk]
            j = 4 * (n % 3)
            mx, bias, rs, ri = sm(8 + j), sm(9 + j), sm(10 + j), sm(11 + j)
            if t < 4:
                nc_ = NCB[i][:, 0:nk]
                d = P.dve(lambda e, sc=src: e.tensor_tensor_reduce(
                    out=pp, in0=sc, in1=nc_, scale=1.0, scalar=-3e38, op0=ALU.add, op1=ALU.max,
                    accum_out=mx), ts, pfree[pb], state["nc"], smfree.get(n % 3))
                bankfree[b0] = bankfree[b0 + 1] = [d]
                src = pp
                c = CT[:, 8 * qb + 2 * t + i:8 * qb + 2 * t + i + 1]
                d = P.dve(tt_(mx, mx, c, ALU.subtract), d, dct)
                db = P.dve(stt_(bias, mx, -1.0, c, ALU.mult, ALU.subtract), d)
            else:
                d = P.dve(lambda e: e.tensor_reduce(mx, src, AX.X, ALU.max), ts, smfree.get(n % 3))
                db = P.dve(ts_(bias, mx, -1.0, None, ALU.mult), d)
            a = P.act(act_(pp, src, ACT.Exp, bias=bias, accum_out=rs), db, pfree[pb])
            if t >= 4:
                bankfree[b0] = bankfree[b0 + 1] = [a]
            dr = P.dve(lambda e: e.reciprocal(ri, rs), a)
            return a, dr

        def stage_b(n, t, qb, i, ta):
            nk = 128 * (qb + 1)
            pb = n % 2
            fns = [tr_(PS[:, 2048 + 128 * k:2176 + 128 * k], PP[pb][:, 128 * k:128 * k + 128])
                   for k in range(qb + 1)]
            tp = P.pe(fns, ta, bankfree[4], bankfree[5], tc)
            pfree[pb] = [tp]
            s = n % 2
            dst, src = PT[s][:, 0:nk], PS[:, 2048:2048 + nk]
            te = P.act(act_(dst, src, ACT.Copy), tp, ptfree[s]) if n % 2 else \
                P.dve(cp_(dst, src), tp, ptfree[s])
            bankfree[4] = bankfree[5] = [te]
            return te

        def stage_c(n, t, qb, i, te, dr):
            s = n % 2
            w = 64 if t < 4 else 128
            o = i * 64 if t < 4 else 0
            out = PS[:, 3072:3072 + w]
            fns = [mm_(out, PT[s][:, 128 * k:128 * k + 128], VT[:, k, o:o + w], k == 0, k == qb)
                   for k in range(qb + 1)]
            tp = P.pe(fns, te, bankfree[6], state["v"])
            ptfree[s] = [tp]
            state["vdone"] = tp
            j = 4 * (n % 3)
            rs, ri = sm(10 + j), sm(11 + j)
            if t < 4:
                d = P.dve(ts_(OTM[:, o:o + w], out, ri, None, ALU.mult), tp, dr, otmfree)
            elif i == 0:
                d = P.dve(ts_(OTM[:, :], out, ri, None, ALU.mult), tp, dr, otmfree)
                state["o1"] = d
            else:
                d = P.dve(tt_(ri, ri, NLAM, ALU.mult), dr, tnl)
                d = P.dve(stt_(OTM[:, :], out, ri, OTM[:, :], ALU.mult, ALU.add), tp, d, state["o1"])
            bankfree[6] = [d]
            smfree[n % 3] = [d]
            if i == 0:
                return
            if t >= 4:
                x, y, z, sq = sm(20), sm(21), sm(22), PS[:, 3712:3840]
                d = P.dve(lambda e: e.scalar_tensor_tensor(sq, OTM[:, :], 1.0, OTM[:, :], ALU.mult,
                                                           ALU.mult, accum_out=x), d, bankfree[7])
                bankfree[7] = [d]
                d = P.dve(ts_(x, x, 1.0 / 128, EPS, ALU.mult, ALU.add), d)
                a = P.act(act_(y, x, ACT.Ln), d)
                a = P.act(act_(y, y, ACT.Exp, scale=-0.5), a)
                d = P.dve(tt_(z, y, y, ALU.mult), a)
                d = P.dve(tt_(z, z, x, ALU.mult), d)
                d = P.dve(ts_(z, z, -0.5, 1.5, ALU.mult, ALU.add), d)
                d = P.dve(tt_(y, y, z, ALU.mult), d)
                d = P.dve(stt_(OTM[:, :], OTM[:, :], y, SUBG, ALU.mult, ALU.mult), d, tsg)
            tp = P.pe([tr_(PS[:, 3584:3712], OTM[:, :])], d, bankfree[7], tc)
            otmfree[:] = [tp]
            a = P.act(act_(OT[:, t, 128 * qb:128 * qb + 128], PS[:, 3584:3712], ACT.Copy), tp)
            bankfree[7] = [a]
            state["ot"] = a

        def step(item):
            if item is not None:
                n = item[0]
                ta, dr = stage_a(*item)
                pend.append([item, ta, dr, None])
            k = len(pend) - (1 if item is not None else 0)
            ready = pend[:k]
            late = [p for p in ready if p[3] is not None]
            for p in ready:
                if p[3] is None:
                    p[3] = stage_b(*p[0], p[1])
                    break
            for p in late[:1]:
                stage_c(*p[0], p[3], p[2])
                pend.remove(p)

        n = 0
        for t in range(8):
            o = 0 if t < 4 else 12
            u = t % 4
            if t == 4:
                trope = P.dma("pool", "rope", lambda e: e.dma_start(M["cs"][:, :, :], A["rope"]), ncfree)
            sd = state.get("sdone")
            tq = project(f"IN.{o + u}", QT, 0.125, sd, 0)
            tk = project(f"IN.{o + 4 + u}", KT_, 1.0, sd, 2)
            while pend:
                step(None)
            if t >= 4:
                tq = rope(QT, tq)
                tk = rope(KT_, tk)
            vr = PT[0]
            tv = project(f"IN.{o + 8 + u}", vr, 1.0, ptfree[0], 0)
            tp = P.pe([tr_(PS[:, 2048 + 128 * k:2176 + 128 * k], vr[:, 128 * k:128 * k + 128])
                       for k in range(8)], tv, bankfree[4], bankfree[5], tc)
            ptfree[0] = [tp]
            a = P.act(act_(VT[:, :, :], PS[:, 2048:3072].rearrange("p (a b) -> p a b", a=8), ACT.Copy),
                      tp, state.get("vdone"))
            bankfree[4] = bankfree[5] = [a]
            state["q"], state["k"], state["v"] = tq, tk, a
            if t < 4:
                toks = []
                for i in range(2):
                    h = 2 * t + i
                    sel = m("ident")[0:8, h:h + 1].to_broadcast([8, 128])
                    for c, (c0, c1) in enumerate(T):
                        b = 6 + c
                        tp = P.pe([mm_(bank(b), sel, NC8[0:8, c0:c1])], bankfree[b], dn)
                        dd = P.dve(cp_(NCB[i][:, c0:c1], bank(b)), tp, state.get("sexp"))
                        bankfree[b] = [dd]
                        toks.append(dd)
                state["nc"] = toks
            for qb in range(8):
                for i in range(2):
                    step((n, t, qb, i))
                    n += 1
            ncfree = [("dve", P.n["dve"]), ("pe", P.n["pe"])]
        xdone = [("pe", P.n["pe"])]
        while pend:
            step(None)
        tfree[0] = tfree[1] = list(pfree[0])
        tfree[2] = tfree[3] = list(pfree[1])
        toks = []
        for k in range(8):
            for c, (c0, c1) in enumerate(T):
                x, xh, xl = OT[:, k, c0:c1], XH[:, k, c0:c1], XL[:, k, c0:c1]
                a = P.act(act_(xh, x, ACT.Copy), state["ot"], xdone)
                p = P.dve(tt_(xl, x, xh, ALU.subtract), a)
                toks.append([a, p])
        osplit = toks[-1]
        acctok = [None, None]
        for f in range(8):
            iw, wh, wl, wt = W.get(f"OUT.{f}")
            for c, (c0, c1) in enumerate(T):
                b = (2 * f + c) % 8
                t = group(b, 512, unit8(wh, wl, c0, c1), wt, osplit)
                d = P.dve(cp_(S["acc"][:, f, c0:c1], bank(b)), t, osplit)
                bankfree[b] = [d]
                acctok[c] = [d]
            W.done(iw, t)
        xd = [("pe", P.n["pe"])]
        return post_norm(S["acc"], "mix_post_g", 1.0, acctok, T), xd

    def evac3(unit, fn, xt, b0, *toks):
        iw, wh, wl, wt = W.get(unit)
        for c, (c0, c1) in enumerate(CHUNKS):
            b = b0 + c
            t = group(b, c1 - c0, unit8(wh, wl, c0, c1), wt, xt[c], *toks)
            bankfree[b] = [fn(c, c0, c1, bank(b, c1 - c0), t)]
        W.done(iw, t)

    def conv4(out, x, wname, nw, bname, tile, srctoks, free):
        d = P.dve(ts_(out, x[:, 0:T2], v(wname, tile), v(bname, tile), ALU.mult, ALU.add), srctoks, free)
        for k in range(1, 4):
            d = P.dve(stt_(out, x[:, k:k + T2], v(wname, nw * k + tile), out, ALU.mult, ALU.add), d)
        return d

    def even(h0, xfree):
        V = S["lru"]
        XIN, U, TB = V["xin"], V["u"], V["tb"]
        UH, UL, YH, YL = S["uh"], S["ul"], S["yh"], S["yl"]
        tm2 = load("act", "mat2", S["mat2"][:, :], A["mat2"], h0)
        exp_ln_tables()
        xt = norm_split(h_src, 8, CHUNKS, "even_norm_2", [h0] * 3, xfree)
        sm = V["sm"]
        L, E1, Z, Z2, AC, N8 = [sm[:, 8 * i:8 * i + 8] for i in range(6)]
        lam = vec[:, VEC["lru_lambda_2"]:VEC["lru_lambda_2"] + 8]
        d = P.dve(ts_(L, lam, -1.0, None, ALU.mult), tc)
        d = P.dve(tt_(E1, L, lam, ALU.min), d)
        a = P.act(act_(E1, E1, ACT.Exp), d)
        d = P.dve(ts_(Z, E1, 2.0, None, ALU.add), a)
        d = P.dve(lambda e: e.reciprocal(Z, Z), d)
        d = P.dve(tt_(Z, Z, E1, ALU.mult), d)
        d = P.dve(tt_(Z2, Z, Z, ALU.mult), d)
        d = P.dve(ts_(AC, Z2, 1.0 / 17, 1.0 / 15, ALU.mult, ALU.add), d)
        for q in (13, 11, 9, 7, 5, 3, 1):
            d = P.dve(tt_(AC, AC, Z2, ALU.mult), d)
            d = P.dve(ts_(AC, AC, 1.0 / q, None, ALU.add), d)
        d = P.dve(tt_(AC, AC, Z, ALU.mult), d)
        d = P.dve(ts_(L, L, 0.0, 8.0, ALU.max, ALU.mult), d)
        d = P.dve(stt_(AC, AC, 16.0, L, ALU.mult, ALU.add), d)
        ts8 = P.dve(ts_(N8, AC, -1.0, None, ALU.mult), d)
        S8 = AC
        tz = P.pool(lambda e, x=XIN: e.memset(x[:, 0:3], 0.0), h0)
        R_, I_, A_, L_ = TB
        xinfree, ufree = [], [[], []]
        uhfree, yfree = [], []
        tbfree = {0: [], 1: [], 2: [], 3: []}
        ynb = [0]
        restok = list(h0)
        for g in range(4):
            ut = []
            for ti in range(2):
                tile = 2 * g + ti
                toks = []

                def to_xin(c, c0, c1, b, t):
                    a = P.act(act_(XIN[:, 3 + c0:3 + c1], b, ACT.Copy), t, xinfree, tz)
                    toks.append(a)
                    return a
                evac3(f"E.{tile}", to_xin, xt, 0 if ti == 0 else 3)
                d = conv4(U[ti], XIN, "lru_conv_w_2", 8, "lru_conv_b_2", tile, toks, ufree[ti])
                xinfree = [d]
                a = P.act(act_(UH[:, ti, :], U[ti], ACT.Copy), d, uhfree)
                p = P.pool(tt_(UL[:, ti, :], U[ti], UH[:, ti, :], ALU.subtract), a)
                ut += [a, p]
            il, lh, ll, lt = W.get(f"L.{g}")
            for tj in range(2):
                tile = 2 * g + tj
                st = {0: [], 1: [], 2: []}
                for which, dst, bname in ((0, R_, "lru_b_a_2"), (1, I_, "lru_b_x_2")):
                    for c, (c0, c1) in enumerate(CHUNKS):
                        b = 3 * which + c
                        parts = []
                        for ki in range(2):
                            o = which * 512 + ki * 256 + tj * 128
                            parts.append((lh[:, o:o + 128], ll[:, o:o + 128],
                                          UH[:, ki, c0:c1], UL[:, ki, c0:c1]))
                        t = group(b, c1 - c0, parts, lt, ut)
                        a = P.act(act_(dst[:, c0:c1], bank(b, c1 - c0), ACT.Sigmoid,
                                       bias=v(bname, tile)), t, tbfree[which])
                        bankfree[b] = [a]
                        st[which].append(a)
                uhfree = [t]
                G_ = XIN[:, 3:3 + T2]

                def to_g(c, c0, c1, b, t):
                    a = P.act(act_(G_[:, c0:c1], b, ACT.Sigmoid), t, xinfree)
                    d = P.dve(tt_(G_[:, c0:c1], b, G_[:, c0:c1], ALU.mult), a)
                    st[2].append(d)
                    return d
                if tj == 1:
                    W.done(il, t)
                evac3(f"E.{8 + tile}", to_g, xt, 0)
                s8, n8 = S8[:, tile:tile + 1], N8[:, tile:tile + 1]
                at = P.act(act_(L_, R_, ACT.Tanh, scale=s8), st[0], ts8, tbfree[3])
                exp_ln_tables()
                aa = P.act(act_(A_, R_, ACT.Exp, scale=n8), ts8, tbfree[2])
                d = P.dve(ts_(L_, L_, 1e-18, None, ALU.max), at)
                a1 = P.act(act_(R_, L_, ACT.Ln, scale=2.0), d, aa)
                a2 = P.act(act_(L_, L_, ACT.Ln, bias=1.0), a1)
                d = P.dve(tt_(R_, R_, L_, ALU.subtract), a1, a2)
                a3 = P.act(act_(R_, R_, ACT.Exp, scale=0.5), d)
                d = P.pool(tt_(I_, I_, U[tj], ALU.mult), st[1], ut)
                ufree[tj] = [d]
                d = P.dve(tt_(I_, I_, R_, ALU.mult), d, a3)
                tbfree[0] = [d]
                d = P.dve(lambda e: e.tensor_tensor_scan(L_, A_, I_, 0.0, ALU.mult, ALU.add), d, aa)
                tbfree[1] = tbfree[2] = [d]
                d = P.dve(tt_(L_, L_, G_, ALU.mult), d, st[2])
                xinfree = [d]
                a = P.act(act_(YH[:, tj, :], L_, ACT.Copy), d, yfree)
                p = P.pool(tt_(YL[:, tj, :], L_, YH[:, tj, :], ALU.subtract), a)
                tbfree[3] = [p]
            yt = [a, p]
            for hh in range(2):
                iw, wh, wl, wt = W.get(f"EO.{g}.{hh}")
                for fi in range(4):
                    f = 4 * hh + fi
                    for c, (c0, c1) in enumerate(CHUNKS):
                        b = 6 + ynb[0] % 2
                        ynb[0] += 1
                        parts = [(wh[:, k * 512 + fi * 128:k * 512 + fi * 128 + 128],
                                  wl[:, k * 512 + fi * 128:k * 512 + fi * 128 + 128],
                                  YH[:, k, c0:c1], YL[:, k, c0:c1]) for k in range(2)]
                        t = group(b, c1 - c0, parts, wt, yt)
                        r = RES[:, f, c0:c1]
                        d = P.dve(tt_(r, r, bank(b, c1 - c0), ALU.add), t, restok)
                        bankfree[b] = [d]
                W.done(iw, t)
            yfree = [t]
            restok = [d]
        lru_end = [d, t, a, p, ("pool", P.n["pool"]), ("act", P.n["act"])]
        tsp = P.dma("pool", "spill", lambda e: e.dma_start(A["rs"], RES[:, :, :]), d)
        V = S["ssd"]
        X, BC, BT, DT = V["x"], V["bc"], V["bt"], V["dt"]
        XIN, CV = V["xin"], V["cv"]
        tz = P.pool(lambda e, x=XIN: e.memset(x[:, 0:3], 0.0), lru_end)
        cvfree, xinfree = list(lru_end), list(lru_end)
        zdone = None
        for k in range(8):
            toks = []

            def to_z(c, c0, c1, b, t):
                a = P.act(act_(CV[:, c0:c1], b, ACT.Silu), t, cvfree)
                toks.append(a)
                return a
            evac3(f"E.{16 + k}", to_z, xt, 3 * (k % 2))
            zdone = P.dma("pool", "zs", lambda e, k=k: e.dma_start(A["zs"][k], CV), toks)
            cvfree = [zdone]
        nblk = 9
        blk = [(128 * c, min(128, T2 - 128 * c)) for c in range(nblk)]
        xtok = None
        for k in range(12):
            toks = []

            def to_x(c, c0, c1, b, t):
                a = P.act(act_(XIN[:, 3 + c0:3 + c1], b, ACT.Copy), t, xinfree, tz)
                toks.append(a)
                return a
            evac3(f"E.{24 + k}", to_x, xt, 0)
            d = conv4(CV, XIN, "ssd_conv_w_2", 12, "ssd_conv_b_2", k, toks, cvfree)
            xinfree = [d]
            dst = CV if k < 8 else BC[:, k - 8, :]
            a = P.act(act_(dst, CV, ACT.Silu), d, lru_end)
            cvfree = [a]
            if k < 10:
                src = dst
                for part in range(3):
                    bs = blk[4 * part:4 * part + 4]
                    b = 3 + part
                    t = P.pe([tr_(PS[0:n, b * 512 + 128 * j:b * 512 + 128 * j + 128], src[:, t0:t0 + n])
                              for j, (t0, n) in enumerate(bs)], a, bankfree[b], tc)
                    n = bs[0][1]
                    o = BT[0:n, 4 * part:4 * part + len(bs), (k - 8) * 128:(k - 7) * 128] if k >= 8 else \
                        X[0:n, 4 * part:4 * part + len(bs), k * 128:(k + 1) * 128]
                    i_ = PS[0:n, b * 512:b * 512 + 128 * len(bs)].rearrange("p (a b) -> p a b", a=len(bs))
                    xtok = P.dve(cp_(o, i_), t, lru_end)
                    bankfree[b] = [xtok]
                cvfree = [a, t]
        bctok = a
        exp_ln_tables()
        dtf, dte = XIN[0:16, 0:T2], CV[0:16, 0:T2]
        db = v("ssd_dt_bias_2")[0:16, :]
        toks = []

        def to_dt(c, c0, c1, b, t):
            d = P.dve(ts_(dtf[:, c0:c1], b[0:16, :], db, None, ALU.add), t, xinfree)
            toks.append(d)
            return d
        evac3("E.36", to_dt, xt, 0)
        xdone = [("pe", P.n["pe"])]
        d = softplus(dtf, dte, dtf, toks, cvfree, None)
        t = P.pe([mm_(PS[0:n, 1536 + 16 * c:1552 + 16 * c], dtf[:, t0:t0 + n], m("ident")[0:16, 0:16])
                  for c, (t0, n) in enumerate(blk)], d, bankfree[3])
        dd = [P.dve(cp_(DT[:, 0:8, :], PS[:, 1536:1664].rearrange("p (a b) -> p a b", a=8)), t, lru_end),
              P.dve(cp_(DT[0:16, 8, :], PS[0:16, 1664:1680]), t)]
        bankfree[3] = [dd[1]]
        dtt = dd[1]
        Q = S["scan"]
        ANEG = Q["aneg"]
        a = P.act(act_(ANEG, vec[:, VEC["ssd_a_log_2"]:VEC["ssd_a_log_2"] + 16], ACT.Exp), xdone)
        ta = P.dve(ts_(ANEG, ANEG, -1.0, None, ALU.mult), a)
        DD = vec[:, VEC["ssd_d_2"]:VEC["ssd_d_2"] + 16]
        ST = Q["state"]
        YT = RES
        sttok = [None, None]
        stread = [None, None]
        fr = {}

        def bc3(ap, w):
            p, h = ap.shape
            return ap.unsqueeze(2).to_broadcast([p, h, w])

        def bh(ap, h):
            p, w = ap.shape
            return ap.unsqueeze(1).to_broadcast([p, h, w])

        def r3(ap, h):
            return ap.rearrange("p (a b) -> p a b", a=h)

        ytok = None
        for c, (t0, n) in enumerate(blk):
            s2 = c % 2
            AD, EX, DDT, Y = Q["ad"][s2], Q["ex"][s2], Q["ddt"][s2], Q["y"][s2]
            d = P.dve(tt_(AD[0:n, :], DT[0:n, c, :], ANEG[0:n, :], ALU.mult), ta, dtt, fr.get(("ad", s2)))
            tad = d
            t = P.pe([mm_(PS[0:n, 0:16], m("triu")[0:n, 0:n], AD[0:n, :]),
                      mm_(PS[0:n, 16:32], m("low")[0:n, 0:n], AD[0:n, :]),
                      mm_(PS[:, 32:48], m("ones")[0:n, :], AD[0:n, :])], d, bankfree[0], tm2)
            a0 = P.act(act_(EX[0:n, 0:32], PS[0:n, 0:32], ACT.Exp), t, fr.get(("ex", s2)))
            a1 = P.act(act_(EX[:, 32:48], PS[:, 32:48], ACT.Exp), t)
            bankfree[0] = [a1]
            dq = P.dve(tt_(DDT[0:n, :], DT[0:n, c, :], EX[0:n, 16:32], ALU.mult), a0, fr.get(("ddt", s2)))
            ydone = []
            for g in range(2):
                k2 = g
                GT, M_, CBM, XD, XS, TX = (Q[q][k2] for q in ("gt", "m", "cbm", "xd", "xs", "tx"))
                hs = slice(8 * g, 8 * g + 8)
                xg = r3(X[0:n, c, 512 * g:512 * g + 512], 8)
                gt3 = r3(GT[0:n, 0:8 * n], 8)
                p = P.pool(tt_(gt3, bh(m("triu")[0:n, 0:n], 8), bc3(AD[0:n, hs], n), ALU.mult),
                           tad, fr.get(("gt", k2)), tm2)
                w = 4 * n
                t = P.pe([mm_(PS[0:n, 512:512 + w], m("low")[0:n, 0:n], GT[0:n, 0:w]),
                          mm_(PS[0:n, 1024:1024 + w], m("low")[0:n, 0:n], GT[0:n, w:2 * w])],
                         p, bankfree[1], bankfree[2])
                fr[("gt", k2)] = [t]
                a = None
                for q in range(2):
                    a = P.act(act_(M_[0:n, q * w:q * w + w], PS[0:n, 512 + 512 * q:512 + 512 * q + w], ACT.Exp),
                              t, fr.get(("m", k2)))
                bankfree[1] = bankfree[2] = [a]
                tcb = P.pe([mm_(PS[0:n, 2560:2560 + n], BC[:, g, t0:t0 + n], BC[:, 2 + g, t0:t0 + n])],
                           bctok, bankfree[5])
                d = P.dve(tt_(CBM[0:n, 0:n], PS[0:n, 2560:2560 + n], m("triu")[0:n, 0:n], ALU.mult),
                          tcb, fr.get(("cbm", k2)), tm2)
                bankfree[5] = [d]
                m3 = r3(M_[0:n, 0:8 * n], 8)
                dm = P.dve(tt_(m3, m3, bh(CBM[0:n, 0:n], 8), ALU.mult), a, d)
                fr[("cbm", k2)] = [dm]
                ps_ = P.pool(tt_(r3(XS[0:n, :], 8), xg, bc3(DT[0:n, c, hs], 64), ALU.mult),
                             xtok, dtt, fr.get(("xs", k2)))
                pd_ = P.pool(tt_(r3(XD[0:n, :], 8), xg, bc3(DDT[0:n, hs], 64), ALU.mult),
                             dq, fr.get(("xd", k2)))
                px_ = P.pool(tt_(r3(TX[0:n, :], 8), xg, bc3(DD[0:n, hs], 64), ALU.mult),
                             fr.get(("tx", k2)))
                ty = P.pe([mm_(PS[0:n, 1536 + 64 * h:1600 + 64 * h], M_[0:n, h * n:h * n + n],
                               XS[0:n, 64 * h:64 * h + 64]) for h in range(8)], dm, ps_, bankfree[3])
                fr[("m", k2)] = [ty]
                fr[("xs", k2)] = [ty]
                yv = Y[0:n, 512 * g:512 * g + 512]
                if c:
                    to = P.pe([mm_(PS[0:n, 2048:2560], BC[:, 2 + g, t0:t0 + n], ST[g])],
                              sttok[g], bankfree[4])
                    stread[g] = to
                    d = P.dve(tt_(r3(yv, 8), r3(PS[0:n, 2048:2560], 8), bc3(EX[0:n, hs], 64), ALU.mult),
                              to, a0, fr.get(("y", s2)))
                    bankfree[4] = [d]
                    d = P.dve(tt_(yv, yv, PS[0:n, 1536:2048], ALU.add), ty, d)
                    bankfree[3] = [d]
                    d = P.dve(tt_(yv, yv, TX[0:n, :], ALU.add), px_, d)
                else:
                    d = P.dve(tt_(yv, TX[0:n, :], PS[0:n, 1536:2048], ALU.add), ty, px_)
                    bankfree[3] = [d]
                fr[("tx", k2)] = [d]
                ydone.append(d)
                if c < nblk - 1:
                    tb_ = P.pe([mm_(PS[:, 2560:3072], BT[0:n, c, 128 * g:128 * g + 128], XD[0:n, :])],
                               pd_, xtok, bankfree[5])
                    fr[("xd", k2)] = [tb_]
                    if c:
                        d = P.dve(tt_(r3(ST[g], 8), r3(ST[g], 8), bc3(EX[:, 32 + 8 * g:40 + 8 * g], 64),
                                      ALU.mult), stread[g], a1, sttok[g])
                        d = P.dve(tt_(ST[g], ST[g], PS[:, 2560:3072], ALU.add), d, tb_)
                    else:
                        d = P.dve(cp_(ST[g], PS[:, 2560:3072]), tb_, xdone)
                    bankfree[5] = [d]
                    sttok[g] = d
            fr[("ad", s2)] = [t, p]
            fr[("ex", s2)] = [d, ydone]
            fr[("ddt", s2)] = [pd_]
            for half in range(2):
                b = 6 + half
                t = P.pe([tr_(PS[:, b * 512 + 128 * j:b * 512 + 128 * j + n],
                              Y[0:n, 512 * half + 128 * j:512 * half + 128 * j + 128], n) for j in range(4)],
                         ydone, bankfree[b], tc)
                src = PS[:, b * 512:b * 512 + 512].rearrange("p (a b) -> p a b", a=4)[:, :, 0:n]
                ytok = P.act(act_(YT[:, 4 * half:4 * half + 4, t0:t0 + n], src, ACT.Copy), t, tsp)
                bankfree[b] = [ytok]
            fr[("y", s2)] = [t]
        scan_end = [("pe", P.n["pe"]), ("dve", P.n["dve"]), ("pool", P.n["pool"]), ("act", P.n["act"])]
        gt = []
        for k in range(8):
            dst = V["zin"][k % 2]
            tl = P.dma("pool", f"zin{k % 2}", lambda e, k=k, dst=dst: e.dma_start(dst, A["zs"][k]),
                       zdone, scan_end, gt[k - 2:k - 1])
            gt.append(P.dve(tt_(YT[:, k, :], YT[:, k, :], dst, ALU.mult), tl, ytok))
        tfr = scan_end + [gt[-1]]
        for i in range(4):
            tfree[i] = list(tfr)
        yt = []
        for grp in range(2):
            yt.append(norm_split(lambda k, a, b, grp=grp: YT[:, 4 * grp + k, a:b], 4, CHUNKS, "ssd_norm_2",
                                 [[gt[4 * grp + 3]]] * 3, scan_end, k0=4 * grp, dim=512))
        yn = [yt[0][c] + yt[1][c] for c in range(3)]
        nend = [("dve", P.n["dve"]), ("act", P.n["act"])]
        tback = P.dma("pool", "back", lambda e: e.dma_start(RES[:, :, :], A["rs"]), nend, tsp)
        d = add_gemm("EB", yn, tback)
        return d, [("pe", P.n["pe"])]

    def add_gemm(prefix, yn, restok):
        nb = 0
        for f in range(8):
            iw, wh, wl, wt = W.get(f"{prefix}.{f}")
            for c, (c0, c1) in enumerate(CHUNKS):
                b = nb % 8
                nb += 1
                t = group(b, c1 - c0, unit8(wh, wl, c0, c1), wt, yn[c])
                r = RES[:, f, c0:c1]
                d = P.dve(tt_(r, r, bank(b, c1 - c0), ALU.add), t, restok)
                bankfree[b] = [d]
            W.done(iw, t)
        return [d]

    def odd(h0, xfree):
        V = S["odd"]
        OT, Q_, K_, VT, VR = V["ot"], V["q"], V["k"], V["vt"], V["vr"]
        SPB, EB_, WB, AB = V["sp"], V["e"], V["w"], V["acc"]
        exp_ln_tables()
        xt = norm_split(h_src, 8, CHUNKS, "odd_norm_2", [h0] * 3, xfree)
        blk = [(128 * c, min(128, T2 - 128 * c)) for c in range(9)]
        vrfree = [("pe", P.n["pe"]), ("dve", P.n["dve"])]
        gdone = None
        for k in range(8):
            toks = []
            dst = (VR, Q_)[k % 2]

            def to_g(c, c0, c1, b, t):
                a = P.act(act_(dst[:, c0:c1], b, ACT.Silu), t, vrfree if k < 2 else gst[k % 2])
                toks.append(a)
                return a
            if k == 0:
                gst = [None, None]
            evac3(f"Q.{24 + k}", to_g, xt, 3 * (k % 2))
            gdone = P.dma("pool", f"gs{k % 2}", lambda e, k=k, dst=dst: e.dma_start(A["gs"][k], dst), toks)
            gst[k % 2] = [gdone]
        exp_ln_tables()
        state = {"z": gst[0] + gst[1], "v": gst[0]}
        free = {}
        pend = []
        last = {}

        def stage_a(it):
            n, t, i, ci, kb, top = it
            c0, c1 = CHUNKS[ci]
            s0, ks = blk[kb]
            a0 = max(c0, s0)
            x0, x1 = a0 - c0, c1 - c0
            b = n % 4
            out = PS[0:ks, b * 512 + x0:b * 512 + x1]
            fns = [mm_(out, K_[64 * i:64 * i + 64, s0:s0 + ks], Q_[64 * i:64 * i + 64, a0:c1],
                       True, False, True)]
            e1 = min(c1, s0 + 128)
            if s0 < c1 and e1 > a0:
                fns.append(mm_(PS[0:ks, b * 512 + x0:b * 512 + e1 - c0], idb[0:ks, 0:ks],
                               smb[0:ks, a0 - s0:e1 - s0], False, False, True))
            tp = P.pe(fns, bankfree[b], state["q"], state["k"], tb)
            state["z"] = [tp]
            s = n % 3
            ev, sp = EB_[n % 2][0:ks, 0:x1 - x0], SPB[s][0:ks, 0:x1 - x0]
            d = softplus(sp, ev, out, tp, free.get(("e", n % 2)), free.get(("sp", s)))
            free[("e", n % 2)] = [d]
            cur = state.get("acc")
            if kb:
                ns = (state.get("slot", 0) + 1) % 3
                state["slot"] = ns
                nxt = AB[ns]
                was = [free.get(("acc", ns)), free.get(("accr", ns)), free.get(("accw", ns))]
                if top:
                    dz = P.pool(lambda e: e.memset(nxt[:, 0:c1 - c0], 0.0), *was)
                    p = P.pool(cp_(nxt[0:ks, x0:x1], sp), dz, d)
                else:
                    cs_, ctok = cur
                    old = AB[cs_]
                    if ks < 128 or x0 > 0:
                        p = P.pool(cp_(nxt[:, 0:c1 - c0], old[:, 0:c1 - c0]), ctok, *was)
                        p = P.pool(tt_(nxt[0:ks, x0:x1], old[0:ks, x0:x1], sp, ALU.add), p, d)
                    else:
                        p = P.pool(tt_(nxt[:, x0:x1], old[:, x0:x1], sp, ALU.add), ctok, d, *was)
                    free[("accr", cs_)] = [p]
                free[("accw", ns)] = [p]
                state["acc"] = (ns, p)
                free[("spa", s)] = [p]
            else:
                free[("spa", s)] = []
            return d, cur

        def stage_b(it, d, cur):
            n, t, i, ci, kb, top = it
            c0, c1 = CHUNKS[ci]
            s0, ks = blk[kb]
            x0, x1 = max(c0, s0) - c0, c1 - c0
            b = n % 4
            s = n % 3
            out = PS[0:ks, b * 512 + x0:b * 512 + x1]
            fns = [mm_(out, m("ntri")[0:ks, 0:ks], SPB[s][0:ks, 0:x1 - x0], False, top, True)]
            tacc = None
            if not top:
                tacc = cur[1]
                fns.append(mm_(out, m("nones")[:, 0:ks], AB[cur[0]][:, x0:x1], False, True, True))
            tp = P.pe(fns, d, tacc)
            free[("sp", s)] = [tp] + free[("spa", s)]
            if not top:
                free[("acc", cur[0])] = [tp]
            w = WB[n % 2][0:ks, 0:x1 - x0]
            a = P.act(act_(w, out, ACT.Exp), tp, free.get(("w", n % 2)))
            bankfree[b] = [a]
            return a

        def stage_c(it, a):
            n, t, i, ci, kb, top = it
            c0, c1 = CHUNKS[ci]
            s0, ks = blk[kb]
            x0, x1 = max(c0, s0) - c0, c1 - c0
            ob = 4 + (2 * ci + i) % 4
            out = PS[64 * i:64 * i + 64, ob * 512 + x0:ob * 512 + x1]
            tp = P.pe([mm_(out, VT[0:ks, kb, 64 * i:64 * i + 64], WB[n % 2][0:ks, 0:x1 - x0],
                           top, kb == 0, True)], a, bankfree[ob], state["v"])
            free[("w", n % 2)] = [tp]
            last["v"] = tp
            if kb == 0:
                d = P.dve(cp_(OT[64 * i:64 * i + 64, t, c0:c1], PS[64 * i:64 * i + 64,
                                                                ob * 512:ob * 512 + c1 - c0]), tp)
                bankfree[ob] = [d]
                state["o"] = d
            else:
                bankfree[ob] = []

        def step(it):
            if it is not None:
                d, tacc = stage_a(it)
                pend.append([it, d, tacc, None])
            k = len(pend) - (1 if it is not None else 0)
            ready = pend[:k]
            late = [p for p in ready if p[3] is not None]
            for p in ready:
                if p[3] is None:
                    p[3] = stage_b(p[0], p[1], p[2])
                    break
            for p in late[:1]:
                stage_c(p[0], p[3])
                pend.remove(p)

        n = 0
        for t in range(8):
            qd = state["z"]

            def proj(unit, dst, scale, b0, fr_):
                toks = []

                def fn(c, c0, c1, b, tk):
                    a = P.act(act_(dst[:, c0:c1], b, ACT.Copy, scale=scale), tk, fr_)
                    toks.append(a)
                    return a
                evac3(unit, fn, xt, b0)
                return toks
            while pend:
                step(None)
            tq = proj(f"Q.{t}", Q_, 0.125, 0, qd)
            tk = proj(f"Q.{8 + t}", K_, 1.0, 3, qd)
            tv = proj(f"Q.{16 + t}", VR, 1.0, 0, state["v"])
            for part in range(3):
                bs = blk[4 * part:4 * part + 4]
                b = 3 + part
                tp = P.pe([tr_(PS[0:w, b * 512 + 128 * j:b * 512 + 128 * j + 128], VR[:, t0:t0 + w])
                           for j, (t0, w) in enumerate(bs)], tv, bankfree[b], tc)
                w = bs[0][1]
                i_ = PS[0:w, b * 512:b * 512 + 128 * len(bs)].rearrange("p (a b) -> p a b", a=len(bs))
                dv = P.dve(cp_(VT[0:w, 4 * part:4 * part + len(bs), :], i_), tp, last.get("v"))
                bankfree[b] = [dv]
            state["q"], state["k"], state["v"] = tq, tk, [dv, tp]
            for ci in range(3):
                top = (CHUNKS[ci][1] - 1) // 128
                for i in range(2):
                    for kb in range(top, -1, -1):
                        step((n, t, i, ci, kb, kb == top))
                        n += 1
        xdone = [("pe", P.n["pe"])]
        while pend:
            step(None)
        od = state["o"]
        yn = None
        gt = []
        for k in range(8):
            dst = (VR, Q_)[k % 2]
            tl = P.dma("pool", f"gin{k % 2}", lambda e, k=k, dst=dst: e.dma_start(dst, A["gs"][k]),
                       gst[0], gst[1], state["z"], state["v"], od, gt[k - 2:k - 1])
            d = P.dve(tt_(OT[:, k, :], OT[:, k, :], dst, ALU.mult), tl, od)
            gt.append(d)
            a = P.act(act_(XH[:, k, :], OT[:, k, :], ACT.Copy), d, xdone)
            p = P.pool(tt_(XL[:, k, :], OT[:, k, :], XH[:, k, :], ALU.subtract), a)
            yn = [a, p]
        d = add_gemm("QO", [yn] * 3, None)
        return d, None

    def final(h0):
        exp_ln_tables()
        for ci, (c0, c1) in enumerate(FFN_CHUNKS):
            R = TT[2][:, :]
            tr = msq(res_src, 8, c0, c1, h0, 0)
            for k in range(8):
                slot = 3 if k % 2 else 1
                tmp = TT[slot][:, :]
                d = P.dve(stt_(tmp, res_src(k, c0, c1), v("final_norm_2", k), R, ALU.mult, ALU.mult),
                          tr, tfree[slot])
                t = P.dma("sp", f"out{slot}", lambda e, k=k, tmp=tmp, c0=c0, c1=c1: e.dma_start(
                    A["out"][:, k, c0:c1], tmp), d)
                tfree[slot] = [t]
            tfree[2] = [d]
        P.wait("sp", [tfree[1], tfree[3]])

    def run():
        t = load("act", "x", RES[:, :, META:T2], A["x"])
        tm = load("act", "meta", RES[:, :, 0:META], A["meta"])
        rt, xf = ffn(1, [[t], [t]], [])
        rt, xf = mixer(rt, xf)
        rt, xf = ffn(2, rt, xf)
        rt, xf = even(rt[0] + rt[1] + [tm], xf)
        rt, xf = odd(rt, xf)
        final(rt)

    run()
    P.wait("sp", [(sem, v) for sem, v in sorted(P.dman.items())])
    return P, W


def layout(nc, ctx):
    F32, F32R, BF = mybir.dt.float32, mybir.dt.float32r, mybir.dt.bfloat16
    base = 16512
    S = {}

    def at(name, shape, dt, off):
        return nc.alloc_sbuf_tensor_at(name, [128] + shape, dt, offset=off)

    o = base
    S["vec"] = at("vec", [NVEC], F32, o)
    o += (NVEC * 4 + 31) // 32 * 32
    S["mat"] = at("mat", [len(MATS) * 128], F32, o)
    o += len(MATS) * 512
    S["mat2"] = at("mat2", [len(MATS2) * 128], F32, o)
    lam = at("mlam", [384], F32, o)
    otm = at("motm", [128], F32, o + 1536)
    o += len(MATS2) * 512
    for n in ("idb", "cmb", "smb"):
        S[n] = at(n, [128], BF, o)
        o += 256
    S["raw"] = [at(f"raw{i}", [1024], F32, o + 4096 * i) for i in range(2)]
    o += 8192
    S["whi"] = [at(f"whi{i}", [1024], F32R, o + 8192 * i) for i in range(3)]
    S["wlo"] = [at(f"wlo{i}", [1024], F32R, o + 8192 * i + 4096) for i in range(3)]
    o += 24576
    S["res"] = at("res", [8, T2], F32, o)
    o += 8 * T2 * 4
    S["xh"] = at("xh", [8, T2], F32R, o)
    S["xl"] = at("xl", [8, T2], F32R, o + 8 * T2 * 4)
    o += 2 * 8 * T2 * 4
    free0 = o
    arena = at("arena", [(229344 - free0) // 4], F32, free0)

    def cut(off, shape):
        n = 1
        for k in shape:
            n *= k
        ap = arena[:, off // 4:off // 4 + n]
        return ap if len(shape) == 1 else ap.rearrange("p (a b) -> p a b", a=shape[0])

    S["acc"] = cut(0, [8, T1])
    S["hh"] = at("hh", [4, T1], F32R, free0 + 32768)
    S["hl"] = at("hl", [4, T1], F32R, free0 + 49152)
    S["t"] = [cut(65536 + 2048 * i, [512]) for i in range(4)]
    S["ot"] = cut(0, [8, T1])
    M = S["mix"] = {}
    q0 = 32768
    M["q"], M["k"] = cut(q0, [T1]), cut(q0 + 4096, [T1])
    M["vt"] = cut(q0 + 8192, [8, 128])
    M["ncb"] = [cut(q0 + 12288 + 4096 * i, [T1]) for i in range(2)]
    M["nc8"] = cut(q0 + 20480, [T1])
    cs = M["cs"] = cut(q0 + 12288, [2, T1])
    M["cos"], M["sin"] = cs[:, 0, :], cs[:, 1, :]
    M["pt"] = [cut(q0 + 24576 + 4096 * i, [T1]) for i in range(2)]
    M["p"] = [cut(q0 + 32768 + 4096 * i, [T1]) for i in range(2)]
    M["otm"], M["lam"] = otm, lam
    M["sm"] = cut(q0 + 40960, [128])
    f = free0
    S["uh"], S["ul"] = at("uh", [2, T2], F32R, f), at("ul", [2, T2], F32R, f + 8320)
    S["yh"], S["yl"] = at("yh", [2, T2], F32R, f + 16640), at("yl", [2, T2], F32R, f + 24960)
    V = S["lru"] = {}
    V["xin"] = cut(33280, [T2 + 8])
    V["u"] = [cut(37472 + 4160 * i, [T2]) for i in range(2)]
    V["tb"] = [cut(45792 + 4160 * i, [T2]) for i in range(4)]
    V["sm"] = cut(62432, [64])
    V = S["ssd"] = {}
    V["x"] = cut(0, [9, 1024])
    V["bc"] = cut(36864, [4, T2])
    V["bt"] = cut(53504, [9, 256])
    V["dt"] = cut(62720, [9, 16])
    V["xin"] = cut(63296, [T2 + 8])
    V["cv"] = cut(67488, [T2])
    V["zin"] = [cut(4160 * i, [T2]) for i in range(2)]
    ar2 = at("arena2", [2 * 8 * T2], F32, free0 - 2 * 8 * T2 * 4)
    Q = S["scan"] = {}
    pos = 0
    for name, num, width in (("state", 2, 512), ("gt", 2, 1024), ("m", 2, 1024), ("cbm", 2, 128),
                             ("xd", 2, 512), ("xs", 2, 512), ("tx", 2, 512), ("y", 2, 1024),
                             ("ad", 2, 16), ("ex", 2, 48), ("ddt", 2, 16)):
        Q[name] = []
        for _ in range(num):
            Q[name].append(ar2[:, pos:pos + width])
            pos += width
    Q["aneg"] = ar2[:, pos:pos + 16]
    V = S["odd"] = {}
    V["ot"] = cut(0, [8, T2])
    V["q"], V["k"], V["vr"] = (cut(33280 + 4160 * i, [T2]) for i in range(3))
    V["vt"] = cut(45760, [9, 128])
    pos = 50368
    for name, num in (("sp", 3), ("e", 2), ("w", 2), ("acc", 3)):
        V[name] = [cut(pos + 1408 * i, [352]) for i in range(num)]
        pos += 1408 * num
    S["ps"] = ctx.enter_context(nc.psum_tensor("ps", [128, 4096], F32))
    return S


def build(nc, A):
    from contextlib import ExitStack
    with ExitStack() as ctx:
        S = layout(nc, ctx)
        _, W = emit(nc, A, S, None)
        P, _ = emit(nc, A, S, W.asked)
        names = list(Prog.ENG) + sorted(P.dman)
        sems = {n: ctx.enter_context(nc.semaphore("s_" + n)) for n in names}
        block = ctx.enter_context(nc.Block())

        def play(eng, key):
            for item in P.q[key]:
                if item[0] == "wait":
                    eng.wait_ge(sems[item[1]], item[2])
                else:
                    ins = item[1](eng)
                    if item[2] is not None:
                        ins.then_inc(sems[item[2]], item[3])

        @block.tensor
        def _(eng):
            play(eng, "pe")

        @block.scalar
        def _(eng):
            play(eng, "act")

        @block.vector
        def _(eng):
            play(eng, "dve")

        @block.gpsimd
        def _(eng):
            play(eng, "pool")

        @block.sync
        def _(eng):
            play(eng, "sp")


def _tiles(w):
    K, N = w.shape
    return w.reshape(K // 128, 128, N // 128, 128).transpose(2, 1, 0, 3).reshape(N // 128, 128, -1)


def _pairs(w):
    return w.reshape(2, 128, 2, 512).transpose(2, 1, 0, 3).reshape(2, 128, 1024)


def _pack(I):
    U = {}

    def put(prefix, arr):
        for i, a in enumerate(arr):
            U[f"{prefix}.{i}"] = a

    for f in (1, 2):
        put(f"G{f}", _tiles(I[f"ffn{f}_w_gate"][0]))
        put(f"U{f}", _tiles(I[f"ffn{f}_w_up"][0]))
        wd = I[f"ffn{f}_w_down"][0]
        for b in range(11):
            put(f"D{f}.{b}", _pairs(wd[256 * b:256 * b + 256]))
    w = I["w_in"][0]
    w = np.concatenate([w[:, 0:1536], w[:, 1544:3080], w[:, 1536:1544], np.zeros((D, 120), w.dtype)], axis=1)
    put("IN", _tiles(w))
    put("OUT", _tiles(I["w_out"][0]))
    w = I["even_w_in_2"][0]
    w = np.concatenate([w, np.zeros((D, 112), w.dtype)], axis=1)
    put("E", _tiles(w))
    for g in range(4):
        wa = I["lru_w_a_2"][0, g].reshape(2, 128, 256).transpose(1, 0, 2).reshape(128, 512)
        wx = I["lru_w_x_2"][0, g].reshape(2, 128, 256).transpose(1, 0, 2).reshape(128, 512)
        U[f"L.{g}"] = np.concatenate([wa, wx], axis=1)
        put(f"EO.{g}", _pairs(I["even_w_out_2"][0][256 * g:256 * g + 256]))
    put("EB", _tiles(I["even_w_out_2"][0][1024:]))
    put("Q", _tiles(I["odd_w_in_2"][0]))
    put("QO", _tiles(I["odd_w_out_2"][0]))
    return np.stack([U[n] for n in UNITS])


def _vectors(I):
    out = np.zeros((128, NVEC), np.float32)

    def fm(a):
        return a.reshape(-1, 128).T

    for n in ("ffn1_pre_g", "ffn1_post_g", "mix_pre_g", "mix_post_g", "ffn2_pre_g", "ffn2_post_g",
              "even_norm_2", "odd_norm_2", "final_norm_2", "lru_conv_b_2", "lru_b_a_2", "lru_b_x_2",
              "lru_lambda_2", "ssd_conv_b_2", "ssd_norm_2"):
        a = fm(I[n].reshape(-1))
        out[:, VEC[n]:VEC[n] + a.shape[1]] = a
    for n, w in (("lru_conv_w_2", 8), ("ssd_conv_w_2", 12)):
        for k in range(4):
            out[:, VEC[n] + k * w:VEC[n] + (k + 1) * w] = fm(I[n][0, k])
    out[0:8, VEC["fox_forget_b"]] = I["fox_forget_b"][0]
    out[0:16, VEC["ssd_dt_bias_2"]] = I["ssd_dt_bias_2"][0]
    for n, w in (("ssd_a_log_2", 16), ("ssd_d_2", 16)):
        out[:, VEC[n]:VEC[n] + w] = I[n].reshape(1, w)
    return out


def _mats():
    p = np.arange(128)
    i, j = p[:, None], p[None, :]
    M = {"ident": i == j, "ones": i >= 0 * j, "triu": i <= j, "low": i > j}
    M = {k: a.astype(np.float32) for k, a in M.items()}
    M["ntri"] = -(i >= j).astype(np.float32)
    M["nones"] = -np.ones((128, 128), np.float32)
    rot = np.zeros((128, 128), np.float32)
    for b in (0, 64):
        for a in range(8):
            rot[b + a + 8, b + a] = -1.0
            rot[b + a, b + a + 8] = 1.0
    M["rot"] = rot
    M["cmask"] = np.where(j > i, NEG, 0.0).astype(np.float32)
    M["smask"] = np.where(i >= j, NEG, 0.0).astype(np.float32)
    return [np.concatenate([M[n] for n in names], axis=1) for names in (MATS, MATS2, ("cmask", "smask"))]


def _rope():
    inv = (np.float32(500000.0) ** (-np.arange(0, 16, 2, dtype=np.float32) / np.float32(16))).astype(np.float32)
    ang = np.arange(T1, dtype=np.float32)[None, :] * inv[:, None]
    c, s = np.ones((128, T1), np.float32), np.zeros((128, T1), np.float32)
    for b in (0, 8, 64, 72):
        c[b:b + 8], s[b:b + 8] = np.cos(ang), np.sin(ang)
    return np.stack([c, s], axis=1)


def kernel(**inputs):
    import concourse.bacc as _bacc
    from concourse.bass_utils import run_bass_kernel_spmd as _run

    I = {k: np.asarray(a) for k, a in inputs.items()}
    fm = lambda a: np.ascontiguousarray(a.T.reshape(8, 128, -1).transpose(1, 0, 2))
    lam = np.concatenate([I[f"diff_lambda_{n}"].reshape(-1) for n in ("q1", "k1", "q2", "k2")]
                         + [I["diff_subln_g"].reshape(-1)])
    arrays = {
        "in_x_dram": fm(I["x"][0]),
        "in_meta_dram": fm(I["meta_2"]),
        "in_w_dram": _pack(I),
        "in_vec_dram": _vectors(I),
        "in_lam_dram": np.ascontiguousarray(np.broadcast_to(lam[None, :], (128, 384))),
        "in_mat_dram": _mats()[0],
        "in_mat2_dram": _mats()[1],
        "in_masks_dram": _mats()[2],
        "in_rope_dram": _rope(),
    }
    nc = _bacc.Bacc("TRN2", target_bir_lowering=False, num_devices=1)
    A = {}
    for name, a in arrays.items():
        A[name[3:-5]] = nc.dram_tensor(name, a.shape, mybir.dt.from_np(a.dtype), kind="ExternalInput").ap()
    A["out"] = nc.dram_tensor("out_0_dram", (128, 8, T1), mybir.dt.float32, kind="ExternalOutput").ap()
    A["zs"] = nc.dram_tensor("zs_scratch", (8, 128, T2), mybir.dt.float32).ap()
    A["gs"] = nc.dram_tensor("gs_scratch", (8, 128, T2), mybir.dt.float32).ap()
    A["rs"] = nc.dram_tensor("rs_scratch", (128, 8, T2), mybir.dt.float32).ap()
    build(nc, A)
    r = _run(nc, [arrays], core_ids=[0])
    got = r.results[0]["out_0_dram"]
    return np.ascontiguousarray(got.transpose(1, 0, 2).reshape(D, T1).T[None])
```

```python
import math

import concourse.bass as bass
from concourse import mybir
import numpy as np

D = 1024
T1 = 1024
META = 16
T2 = T1 + META
FF = 2816
EPS = 1e-6
NEG = -1e30
FFN_CHUNKS = [(0, 512), (512, 1024)]
CHUNKS = [(0, 352), (352, 704), (704, 1040)]

UNITS = []
for _f in (1, 2):
    UNITS += [f"G{_f}.{j}" for j in range(22)]
    UNITS += [f"U{_f}.{j}" for j in range(22)]
    UNITS += [f"D{_f}.{b}.{c}" for b in range(11) for c in range(2)]
UNITS += [f"IN.{i}" for i in range(25)]
UNITS += [f"OUT.{i}" for i in range(8)]
UNITS += [f"E.{i}" for i in range(37)]
UNITS += [f"L.{g}" for g in range(4)]
UNITS += [f"EO.{g}.{c}" for g in range(4) for c in range(2)]
UNITS += [f"EB.{i}" for i in range(8)]
UNITS += [f"Q.{i}" for i in range(32)]
UNITS += [f"QO.{i}" for i in range(8)]
UNIT_AT = {name: n for n, name in enumerate(UNITS)}

VEC = {}
_n = 0
for _name, _w in [("ffn1_pre_g", 8), ("ffn1_post_g", 8), ("mix_pre_g", 8), ("mix_post_g", 8),
                  ("ffn2_pre_g", 8), ("ffn2_post_g", 8), ("even_norm_2", 8), ("odd_norm_2", 8),
                  ("final_norm_2", 8), ("lru_conv_w_2", 32), ("lru_conv_b_2", 8), ("lru_b_a_2", 8),
                  ("lru_b_x_2", 8), ("lru_lambda_2", 8), ("ssd_conv_w_2", 48), ("ssd_conv_b_2", 12),
                  ("ssd_norm_2", 8), ("fox_forget_b", 1), ("ssd_dt_bias_2", 1),
                  ("ssd_a_log_2", 16), ("ssd_d_2", 16)]:
    VEC[_name] = _n
    _n += _w
NVEC = _n
MATS = ["ident", "ones", "rot"]
MATS2 = ["triu", "low", "ntri", "nones"]


class Prog:

    ENG = ("pe", "act", "dve", "pool", "sp")

    def __init__(self):
        self.q = {e: [] for e in self.ENG}
        self.n = {e: 0 for e in self.ENG}
        self.waited = {}
        self.dman = {}

    def wait(self, eng, toks):
        for t in toks:
            if t is None:
                continue
            if isinstance(t, list):
                self.wait(eng, t)
                continue
            sem, v = t
            if self.waited.get((eng, sem), 0) < v:
                self.waited[(eng, sem)] = v
                self.q[eng].append(("wait", sem, v))

    def do(self, eng, fn, *toks):
        self.wait(eng, toks)
        self.n[eng] += 1
        self.q[eng].append(("ins", fn, eng, 1))
        return (eng, self.n[eng])

    def act(self, fn, *toks):
        return self.do("act", fn, *toks)

    def dve(self, fn, *toks):
        return self.do("dve", fn, *toks)

    def pool(self, fn, *toks):
        return self.do("pool", fn, *toks)

    def act_raw(self, fn):
        self.q["act"].append(("ins", fn, None, 0))

    def pe(self, fns, *toks):
        self.wait("pe", toks)
        for fn in fns[:-1]:
            self.q["pe"].append(("ins", fn, None, 0))
        self.n["pe"] += 1
        self.q["pe"].append(("ins", fns[-1], "pe", 1))
        return ("pe", self.n["pe"])

    def dma(self, eng, sem, fn, *toks):
        self.wait(eng, toks)
        self.dman[sem] = self.dman.get(sem, 0) + 16
        self.q[eng].append(("ins", fn, sem, 16))
        return (sem, self.dman[sem])


class Weights:

    NRAW, NSPL = 2, 3

    def __init__(self, P, order, dram, raw, hi, lo, COPY, SUB):
        self.P, self.order, self.dram = P, order, dram
        self.raw, self.hi, self.lo = raw, hi, lo
        self.COPY, self.SUB = COPY, SUB
        self.asked = []
        self.nload = self.nsplit = 0
        self.loaded, self.parted, self.free = {}, {}, {}

    def _load(self, i):
        s = i % self.NRAW
        src = self.dram[UNIT_AT[self.order[i]]]
        dst = self.raw[s][:, :]
        self.loaded[i] = self.P.dma("sp", f"w{s}", lambda e: e.dma_start(dst, src),
                                    self.parted.get(i - self.NRAW))

    def _split(self, i):
        s, r = i % self.NSPL, i % self.NRAW
        raw, hi, lo, COPY, SUB = self.raw[r], self.hi[s], self.lo[s], self.COPY, self.SUB
        n = {"D": 1024, "L": 1024}.get(self.order[i][0], 1024)
        a = self.P.act(lambda e: e.activation(hi[:, 0:n], raw[:, 0:n], COPY),
                       self.loaded[i], self.free.get(i - self.NSPL))
        b = self.P.pool(lambda e: e.tensor_tensor(lo[:, 0:n], raw[:, 0:n], hi[:, 0:n], SUB),
                        self.loaded[i], self.free.get(i - self.NSPL), a)
        self.parted[i] = [a, b]

    def get(self, name):
        i = len(self.asked)
        self.asked.append(name)
        if self.order is None:
            return i, self.hi[0], self.lo[0], []
        assert self.order[i] == name
        while self.nsplit <= min(i + 1, len(self.order) - 1):
            while self.nload <= min(self.nsplit + 1, len(self.order) - 1):
                if self.nload >= self.NRAW and (self.nload - self.NRAW) not in self.parted:
                    break
                self._load(self.nload)
                self.nload += 1
            self._split(self.nsplit)
            self.nsplit += 1
        while self.nload < len(self.order) and (self.nload - self.NRAW) in self.parted:
            self._load(self.nload)
            self.nload += 1
        return i, self.hi[i % self.NSPL], self.lo[i % self.NSPL], self.parted[i]

    def done(self, i, tok):
        self.free[i] = tok


def emit(nc, A, S, order):
    ALU = mybir.AluOpType
    ACT = mybir.ActivationFunctionType
    AX = mybir.AxisListType
    P = Prog()
    W = Weights(P, order, A["w"], S["raw"], S["whi"], S["wlo"], ACT.Copy, ALU.subtract)
    PS = S["ps"]
    bankfree = {b: [] for b in range(8)}
    RES, XH, XL = S["res"], S["xh"], S["xl"]
    TT = S["t"]
    vec, mat = S["vec"], S["mat"]


    def v(name, i=0):
        c = VEC[name] + i
        return vec[:, c:c + 1]

    def m(name):
        if name in MATS2:
            i = MATS2.index(name)
            return S["mat2"][:, i * 128:(i + 1) * 128]
        i = MATS.index(name)
        return mat[:, i * 128:(i + 1) * 128]

    def bank(b, n=512, p0=0, p1=128):
        return PS[p0:p1, b * 512:b * 512 + n]

    def load(eng, sem, dst, src, *toks):
        return P.dma(eng, sem, lambda e: e.dma_start(dst, src), *toks)

    tc = [load("act", "cst", vec[:, :], A["vec"]), load("act", "cst", mat[:, :], A["mat"]),
          load("act", "cst", TT[0][:, 0:256], A["masks"])]
    tc = tc[-1]
    idb, cmb, smb = S["idb"], S["cmb"], S["smb"]
    tb = [P.dve(lambda e: e.tensor_copy(idb[:, :], m("ident")), tc),
          P.dve(lambda e: e.tensor_copy(cmb[:, :], TT[0][:, 0:128]), tc),
          P.dve(lambda e: e.tensor_copy(smb[:, :], TT[0][:, 128:256]), tc)][-1]

    def mm3(out, whi, wlo, xhi, xlo, first, last):
        return [lambda e: e.matmul(out, whi, xhi, start=first, stop=False),
                lambda e: e.matmul(out, wlo, xhi, start=False, stop=False),
                lambda e: e.matmul(out, whi, xlo, start=False, stop=last)]

    def group(b, n, parts, *toks):
        assert b not in statbusy
        P.wait("pe", [bankfree[b]])
        by = [t for t in toks if isinstance(t, KToks)]
        P.wait("pe", [t for t in toks if not isinstance(t, KToks)])
        for k, (wh, wl, xh, xl) in enumerate(parts):
            t = P.pe(mm3(bank(b, n), wh, wl, xh, xl, k == 0, k == len(parts) - 1),
                     *[q[k] for q in by])
        bankfree[b] = [t]
        tick(len(parts) // 2 + 1)
        return t

    def unit8(wh, wl, c0, c1, XHt=None, XLt=None, K=8):
        XHt, XLt = XHt or XH, XLt or XL
        return [(wh[:, k * 128:(k + 1) * 128], wl[:, k * 128:(k + 1) * 128],
                 XHt[:, k, c0:c1], XLt[:, k, c0:c1]) for k in range(K)]

    def act_(out, in_, func, **kw):
        return lambda e: e.activation(out, in_, func, **kw)

    def tt_(out, a, b, op):
        return lambda e: e.tensor_tensor(out, a, b, op)

    def ts_(out, a, s1, s2, op0, op1=ALU.bypass):
        return lambda e: e.tensor_scalar(out, a, s1, s2, op0, op1)

    def stt_(out, a, s1, b, op0, op1):
        return lambda e: e.scalar_tensor_tensor(out, a, s1, b, op0, op1)

    def cp_(out, a):
        return lambda e: e.tensor_copy(out, a)

    def mm_(out, lhsT, rhs, start=True, stop=True, skip=False):
        return lambda e: e.matmul(out, lhsT, rhs, start=start, stop=stop, skip_group_check=skip)

    def tr_(out, in_, n=128):
        return lambda e: e.transpose(out, in_, m("ident")[0:n, 0:n])

    def exp_ln_tables():
        P.act_raw(lambda e: e.preload_act_table_set("natural_log_exp_and_others"))

    tfree = {i: [] for i in range(8)}
    tfree[0] = [tb]

    def stats(src, KT, c0, c1, srctoks, p, dim, factor, busy):
        n = c1 - c0
        bk, rs = 2 + p, 2 + 2 * p
        R, V = TT[rs][:, 0:n], TT[5][:, 0:n]
        busy.add(bk)
        for k in range(KT):
            s = (0, 1, 6)[sq_[0] % 3]
            sq_[0] += 1
            SQ = TT[s][:, 0:n]
            a = P.act(act_(SQ, src(k, c0, c1), ACT.Square), tfree[s], srctoks[k])
            g = P.pe([mm_(bank(bk, n), m("ones"), SQ, k == 0, k == KT - 1, True)],
                     a, bankfree[bk] if k == 0 else None, tc)
            tfree[s] = [g]
            yield
        d = P.dve(ts_(V, bank(bk, n), 1.0 / dim, EPS, ALU.mult, ALU.add), g, tfree[5])
        bankfree[bk] = [d]
        busy.discard(bk)
        a = P.act(act_(R, V, ACT.Ln), d, tfree[rs])
        a = P.act(act_(R, R, ACT.Exp, scale=-0.5), a)
        d = P.dve(tt_(V, R, V, ALU.mult), a)
        d = P.dve(stt_(V, V, -0.5 * factor, R, ALU.mult, ALU.mult), d)
        d = P.dve(stt_(R, V, 1.5 * factor, R, ALU.add, ALU.mult), d)
        tfree[5] = [d]
        tfree[rs] = [d]
        yield d

    sq_ = [0]
    tm_ = [0]
    statbusy = set()

    def tmp_slot(n):
        s = (3, 7)[tm_[0] % 2]
        tm_[0] += 1
        return s, TT[s][:, 0:n]

    def chain(p, dst, srctoks, post, pre, KT=8, dim=D, k0=0):
        rs = 2 + 2 * p
        if post is not None:
            acc, gname, factor, c0, c1 = post
            n = c1 - c0
            R = TT[rs][:, 0:n]
            for tr in stats(acc, KT, c0, c1, srctoks, p, D, factor, statbusy):
                yield
            ready = []
            for k in range(KT):
                s, tmp = tmp_slot(n)
                d = P.dve(stt_(tmp, acc(k, c0, c1), v(gname, k), R, ALU.mult, ALU.mult), tr, tfree[s])
                tfree[rs] = [d]
                yk = RES[:, k, META + c0:META + c1]
                d = (P.pool if k % 2 else P.dve)(tt_(yk, yk, tmp, ALU.add), d, resback[0])
                tfree[s] = [d]
                ready.append([d])
                yield
            srctoks = ready
        src, gname, c0, c1 = pre
        n = c1 - c0
        R = TT[rs][:, 0:n]
        for tr in stats(src, KT, c0, c1, srctoks, p, dim, 1.0, statbusy):
            yield
        for k in range(KT):
            s, tmp = tmp_slot(n)
            d = P.dve(stt_(tmp, src(k, c0, c1), v(gname, k0 + k), R, ALU.mult, ALU.mult), tr, tfree[s], tc)
            tfree[rs] = [d]
            xh, xl = XH[:, k0 + k, c0:c1], XL[:, k0 + k, c0:c1]
            a = P.act(act_(xh, tmp, ACT.Copy), d, xfree_[0])
            q = (P.dve if k % 2 else P.pool)(tt_(xl, tmp, xh, ALU.subtract), a, xfree_[0])
            tfree[s] = [q]
            dst.append([a, q, d])
            yield

    xfree_ = [[]]
    resback = [None]

    def spill(xt):
        xt.all()
        return P.dma("pool", "spill", lambda e: e.dma_start(A["rs"], RES[:, :, :]),
                     [(q, P.n[q]) for q in ("dve", "pool", "act")], ("meta", 16))

    def restore_tile(f, *toks):
        return P.dma("pool", f"back{f}", lambda e: e.dma_start(RES[:, f, :], A["rs"][:, f, :]), *toks)
    LAG = 10

    class KToks(list):
        pass

    class Chains:

        def __init__(self, gens, outs, per=1):
            self.gens, self.outs, self.per = gens, outs, per
            self.steps = [0] * len(gens)
            self.over = [False] * len(gens)
            self.open = len(gens)

        def step(self, i):
            if i >= self.open or (i >= 2 and not self.over[i - 2]) or self.over[i]:
                return False
            try:
                next(self.gens[i])
                self.steps[i] += 1
            except StopIteration:
                self.over[i] = True
            return True

        def advance(self):
            for i in range(len(self.gens)):
                if not self.over[i]:
                    done = self.step(i)
                    if i + 1 < len(self.gens) and self.steps[i] > LAG:
                        self.step(i + 1)
                    return done
            return False

        def __getitem__(self, c):
            last = self.per * (c + 1) - 1
            while not self.over[last]:
                assert self.advance()
            out = KToks()
            for i in range(self.per * c, last + 1):
                out += self.outs[i]
            return out

        def all(self):
            return [self[c] for c in range(len(self.gens) // self.per)]

    background = []

    def tick(n=1):
        for _ in range(n):
            while background and all(background[0].over):
                background.pop(0)
            if background:
                background[0].advance()

    def chains(specs, xfree, per=1, **kw):
        xfree_[0] = xfree
        outs = [[] for _ in specs]
        gens = [chain(i % 2, outs[i], s[0], s[1], s[2], **dict(kw, **(s[3] if len(s) > 3 else {})))
                for i, s in enumerate(specs)]
        c = Chains(gens, outs, per)
        background.append(c)
        return c

    res_src = lambda k, a, b: RES[:, k, META + a:META + b]
    h_src = lambda k, a, b: RES[:, k, a:b]

    def ffn(f, xt, nxt):
        ACC, H_H, H_L = S["acc"], S["hh"], S["hl"]
        T = FFN_CHUNKS
        hfree = {s: [] for s in range(4)}
        hready = {}
        acctok = [[None] * 8, [None] * 8]
        nb = [0]

        def gate_up(j):
            ig, gh, gl, gt = W.get(f"G{f}.{j}")
            iu, uh, ul, ut = W.get(f"U{f}.{j}")
            s = j % 4
            for c, (c0, c1) in enumerate(T):
                b = 2 * ((2 * j + c) % 2)
                tg = group(b, 512, unit8(gh, gl, c0, c1), gt, xt[c])
                tu = group(b + 1, 512, unit8(uh, ul, c0, c1), ut)
                ta, tb_, = (0, 1) if c == 0 else (2, 3)
                ea, eb = TT[ta][:, :], TT[tb_][:, :]
                g_, u_ = bank(b), bank(b + 1)
                hh, hl = H_H[:, s, c0:c1], H_L[:, s, c0:c1]
                d1 = P.act(lambda e, ea=ea, g_=g_: e.activation(ea, g_, ACT.Silu), tg, tfree[ta])
                d2 = P.dve(lambda e, ea=ea, eb=eb, u_=u_: e.tensor_tensor(eb, u_, ea, ALU.mult),
                           d1, tu, tfree[tb_])
                bankfree[b], bankfree[b + 1] = [d1], [d2]
                a = P.act(lambda e, hh=hh, eb=eb: e.activation(hh, eb, ACT.Copy), d2, hfree[s])
                p = P.pool(lambda e, hh=hh, hl=hl, eb=eb: e.tensor_tensor(hl, eb, hh, ALU.subtract), a)
                tfree[ta], tfree[tb_] = [d2], [p]
                hready[j, c] = [a, p]
            W.done(ig, tg)
            W.done(iu, tu)

        def down_group(b, c, ft, un):
            iw, wh, wl, wt = un
            c0, c1 = T[c]
            pb = 4 + nb[0] % 4
            nb[0] += 1
            parts = []
            for k in range(2):
                o = k * 512 + ft % 4 * 128
                s = (2 * b + k) % 4
                parts.append((wh[:, o:o + 128], wl[:, o:o + 128], H_H[:, s, c0:c1], H_L[:, s, c0:c1]))
            t = group(pb, 512, parts, wt, hready[2 * b, c], hready[2 * b + 1, c])
            acc, pp = ACC[:, ft, c0:c1], bank(pb)
            d = P.dve(cp_(acc, pp) if b == 0 else tt_(acc, acc, pp, ALU.add), t)
            bankfree[pb] = [d]
            acctok[c][ft] = [d]
            return t

        def down(b):
            for h in range(2):
                un = W.get(f"D{f}.{b}.{h}")
                for fi in range(4):
                    for c in range(2):
                        t = down_group(b, c, 4 * h + fi, un)
                W.done(un[0], t)
            for k in range(2):
                hfree[(2 * b + k) % 4] = [t]

        for b in range(11):
            gate_up(2 * b)
            if b:
                down(b - 1)
            gate_up(2 * b + 1)
        xdone = ("pe", P.n["pe"])
        un = [W.get(f"D{f}.10.{h}") for h in range(2)]
        for ft in range(8):
            down_group(10, 0, ft, un[ft // 4])
        exp_ln_tables()
        out = nxt(lambda k, a, b: ACC[:, k, a:b], f"ffn{f}_post_g", 0.5, acctok, [xdone])
        out.open = 1
        for ft in range(8):
            t = down_group(10, 1, ft, un[ft // 4])
            if ft == 3:
                W.done(un[0][0], t)
        W.done(un[1][0], t)
        out.open = len(out.gens)
        return out

    def to_first(gpre):
        def make(acc, gpost, factor, acctok, xfree):
            return chains([(acctok[c], (acc, gpost, factor, c0, c1), (res_src, gpre, c0, c1))
                           for c, (c0, c1) in enumerate(FFN_CHUNKS)], xfree)
        return make

    def to_second(acc, gpost, factor, acctok, xfree):
        return chains([(acctok[min(c, 1)], (acc, gpost, factor, max(c0 - META, 0), c1 - META),
                        (h_src, "even_norm_2", c0, c1)) for c, (c0, c1) in enumerate(CHUNKS)], xfree)

    def softplus(out, tmp, src, srctok, tmpfree, outfree):
        d = P.dve(ts_(tmp, src, 40.0, None, ALU.min), srctok, tmpfree)
        a = P.act(act_(tmp, tmp, ACT.Exp), d)
        a = P.act(act_(tmp, tmp, ACT.Ln, bias=1.0), a)
        return P.dve(tt_(out, src, tmp, ALU.max), a, outfree)

    def mixer(xt, nxt):
        M = S["mix"]
        OT, OTM = S["ot"], M["otm"]
        NC8, COS, SIN = M["nc8"], M["cos"], M["sin"]
        PT, PP, SM, LAM = M["pt"], M["p"], M["sm"], M["lam"]
        T = FFN_CHUNKS
        exp_ln_tables()
        tlam = load("sp", "lam", LAM[:, :], A["lam"])
        SUBG = LAM[:, 256:384]
        sm = lambda i, n=1: SM[:, i:i + n]
        d = []
        for i in range(2):
            q, k = LAM[:, 128 * i:128 * i + 64], LAM[:, 128 * i + 64:128 * i + 128]
            d1 = P.dve(lambda e, q=q, k=k, i=i: e.scalar_tensor_tensor(
                q, q, 1.0, k, ALU.mult, ALU.mult, accum_out=sm(i)), tlam)
            d.append(P.act(act_(sm(i), sm(i), ACT.Exp), d1))
        d1 = P.dve(tt_(sm(0), sm(0), sm(1), ALU.subtract), d)
        tnl = P.dve(ts_(sm(0), sm(0), 0.2, -1.0, ALU.add, ALU.mult), d1)
        tsg = P.dve(ts_(SUBG, SUBG, 0.8, None, ALU.mult), tlam)
        NLAM = sm(0)
        i24, wh, wl, wt = W.get("IN.24")
        tg = []
        for c, (c0, c1) in enumerate(T):
            tg.append(group(c, 512, unit8(wh, wl, c0, c1), wt, xt[c]))
        W.done(i24, tg[1])
        z8 = PT[0][0:8, 0:1024]
        e8 = PT[1][0:8, 0:1024]
        fb = v("fox_forget_b")[0:8, :]
        for c, (c0, c1) in enumerate(T):
            d = P.dve(ts_(z8[:, c0:c1], bank(c, 512, 0, 8), fb, -1.0, ALU.add, ALU.mult), tg[c], tc,
                      tfree[6], tfree[7])
            bankfree[c] = [d]
        d = softplus(z8, e8, z8, d, tfree[4] + tfree[5], None)
        dz = P.dve(lambda e: e.memset(e8, 0.0), d)
        dn = P.dve(lambda e: e.tensor_tensor_scan(NC8[0:8, :], z8, e8, 0.0, ALU.add, ALU.add), dz, d)
        CT = sm(64, 64)
        ptfree = [[dn], [dn]]
        pfree = [tfree[0] + tfree[1], tfree[2] + tfree[3]]
        otmfree = [None, None]
        smfree = {}
        pend = []
        late_tr = []
        tiles = {}
        last = {}
        tsp = spill(xt)

        def project(t):
            s = t % 2
            QT, KT_, VT, NCB = M["q"][s], M["k"][s], M["vt"][s], M["ncb"][s]
            VR, RT = M["vr"], M["rt"]
            o, u = (0 if t < 4 else 12), t % 4
            free = [last.get(("s", t - 2)), last.get(("v", t - 2)), tsp]
            tl = {}
            if t == 4:
                last["rope"] = load("pool", "rope", M["cs"][:, :, :], A["rope"], ("dve", P.n["dve"]),
                                    last.get(("s", 2)))
            trope = last.get("rope")
            for which, dst, scale in (("q", QT, 0.125), ("k", KT_, 1.0), ("v", VR, 1.0)):
                iw, wh, wl, wt = W.get(f"IN.{o + 4 * 'qkv'.index(which) + u}")
                fr = last.get("vr") if which == "v" else free
                toks = []
                for c, (c0, c1) in enumerate(T):
                    P.wait("pe", [bankfree[7], wt, xt[c]])
                    parts = unit8(wh, wl, c0, c1)
                    for k, (a, b, x, y) in enumerate(parts):
                        tk = P.pe(mm3(bank(7), a, b, x, y, k == 0, k == 7))
                        if k < 7:
                            yield
                    a = P.act(act_(dst[:, c0:c1], bank(7), ACT.Copy, scale=scale), tk, fr, tsp)
                    bankfree[7] = [a]
                    toks.append(a)
                    yield
                W.done(iw, tk)
                if t >= 4 and which != "v":
                    for c, (c0, c1) in enumerate(T):
                        X, tmp = dst[:, c0:c1], RT[:, c0:c1]
                        tr = P.pe([mm_(bank(7), m("rot"), X)], toks[c], bankfree[7])
                        d1 = P.dve(tt_(tmp, bank(7), SIN[:, c0:c1], ALU.mult), tr, trope, tsp)
                        bankfree[7] = [d1]
                        d2 = P.pool(tt_(X, X, COS[:, c0:c1], ALU.mult), toks[c], tr, trope)
                        toks[c] = P.dve(tt_(X, X, tmp, ALU.add), d1, d2)
                        yield
                tl[which] = toks
            for h in range(2):
                tp = P.pe([tr_(PS[:, 3584 + 128 * k:3712 + 128 * k], VR[:, 512 * h + 128 * k:512 * h + 128 * k + 128])
                           for k in range(4)], tl["v"], bankfree[7], tc)
                a = P.act(act_(VT[:, 4 * h:4 * h + 4, :], bank(7).rearrange("p (a b) -> p a b", a=4),
                               ACT.Copy), tp, free)
                bankfree[7] = [a]
                yield
            last["vr"] = tp
            tl["v"] = a
            if t < 4:
                tl["nc"] = []
                for i in range(2):
                    h = 2 * t + i
                    sel = m("ident")[0:8, h:h + 1].to_broadcast([8, 128])
                    for c, (c0, c1) in enumerate(T):
                        tp = P.pe([mm_(bank(7), sel, NC8[0:8, c0:c1])], bankfree[7], dn)
                        dd = P.dve(cp_(NCB[i][:, c0:c1], bank(7)), tp, tsp)
                        bankfree[7] = [dd]
                        tl["nc"].append(dd)
                        yield
            tiles[t] = tl

        def stage_a(n, t, qb, i):
            nk = 128 * (qb + 1)
            pb = n % 2
            b0 = 2 * pb
            QT, KT_, NCB, state = M["q"][t % 2], M["k"][t % 2], M["ncb"][t % 2], tiles[t]
            fns = []
            for c0 in range(0, nk, 512):
                c1 = min(nk, c0 + 512)
                o = PS[:, b0 * 512 + c0:b0 * 512 + c1]
                fns.append(mm_(o, QT[64 * i:64 * i + 64, 128 * qb:128 * qb + 128],
                               KT_[64 * i:64 * i + 64, c0:c1], True, c1 != nk))
            fns.append(mm_(PS[:, b0 * 512 + nk - 128:b0 * 512 + nk], idb[:, :], cmb[:, :], False, True))
            ts = P.pe(fns, state["q"], state["k"], bankfree[b0], bankfree[b0 + 1], tb)
            last["s", t] = ts
            pp = PP[pb][:, 0:nk]
            src = PS[:, b0 * 512:b0 * 512 + nk]
            j = 4 * (n % 4)
            mx, bias, rs, ri = sm(8 + j), sm(9 + j), sm(10 + j), sm(11 + j)
            if t < 4:
                nc_ = NCB[i][:, 0:nk]
                d = P.dve(lambda e, sc=src: e.tensor_tensor_reduce(
                    out=pp, in0=sc, in1=nc_, scale=1.0, scalar=-3e38, op0=ALU.add, op1=ALU.max,
                    accum_out=mx), ts, pfree[pb], state["nc"], smfree.get(n % 4))
                bankfree[b0] = bankfree[b0 + 1] = [d]
                src = pp
                c = CT[:, 8 * qb + 2 * t + i:8 * qb + 2 * t + i + 1]
                d = P.dve(tt_(mx, mx, c, ALU.subtract), d, dct)
                db = P.dve(stt_(bias, mx, -1.0, c, ALU.mult, ALU.subtract), d)
            else:
                d = P.dve(lambda e: e.tensor_reduce(mx, src, AX.X, ALU.max), ts, smfree.get(n % 4))
                db = P.dve(ts_(bias, mx, -1.0, None, ALU.mult), d)
            a = P.act(act_(pp, src, ACT.Exp, bias=bias, accum_out=rs), db, pfree[pb])
            if t >= 4:
                bankfree[b0] = bankfree[b0 + 1] = [a]
            dr = P.dve(lambda e: e.reciprocal(ri, rs), a)
            return a, dr

        def stage_b(n, t, qb, i, ta):
            nk = 128 * (qb + 1)
            pb = n % 2
            fns = [tr_(PS[:, 2048 + 128 * k:2176 + 128 * k], PP[pb][:, 128 * k:128 * k + 128])
                   for k in range(qb + 1)]
            tp = P.pe(fns, ta, bankfree[4], bankfree[5], tc)
            pfree[pb] = [tp]
            s = n % 2
            dst, src = PT[s][:, 0:nk], PS[:, 2048:2048 + nk]
            te = P.act(act_(dst, src, ACT.Copy), tp, ptfree[s]) if n % 2 else \
                P.dve(cp_(dst, src), tp, ptfree[s])
            bankfree[4] = bankfree[5] = [te]
            return te

        def stage_c(n, t, qb, i, te, dr):
            s = n % 2
            w = 64 if t < 4 else 128
            o = i * 64 if t < 4 else 0
            out = PS[:, 3072:3072 + w]
            VT, OT2 = M["vt"][t % 2], OTM[n // 2 % 2]
            fns = [mm_(out, PT[s][:, 128 * k:128 * k + 128], VT[:, k, o:o + w], k == 0, k == qb)
                   for k in range(qb + 1)]
            tp = P.pe(fns, te, bankfree[6], tiles[t]["v"])
            ptfree[s] = [tp]
            last["v", t] = tp
            j = 4 * (n % 4)
            rs, ri = sm(10 + j), sm(11 + j)
            of = otmfree[n // 2 % 2]
            if t < 4:
                d = P.dve(ts_(OT2[:, o:o + w], out, ri, None, ALU.mult), tp, dr, of)
            elif i == 0:
                d = P.dve(ts_(OT2[:, :], out, ri, None, ALU.mult), tp, dr, of)
                last["o1"] = d
            else:
                d = P.dve(tt_(ri, ri, NLAM, ALU.mult), dr, tnl)
                d = P.dve(stt_(OT2[:, :], out, ri, OT2[:, :], ALU.mult, ALU.add), tp, d, last["o1"])
            bankfree[6] = [d]
            smfree[n % 4] = [d]
            if i == 0:
                return
            if t >= 4:
                x, y, z, sq = sm(28), sm(29), sm(30), M["sq"]
                d = P.dve(lambda e: e.scalar_tensor_tensor(sq, OT2[:, :], 1.0, OT2[:, :], ALU.mult,
                                                           ALU.mult, accum_out=x), d)
                d = P.dve(ts_(x, x, 1.0 / 128, EPS, ALU.mult, ALU.add), d)
                a = P.act(act_(y, x, ACT.Ln), d)
                a = P.act(act_(y, y, ACT.Exp, scale=-0.5), a)
                d = P.dve(tt_(z, y, y, ALU.mult), a)
                d = P.dve(tt_(z, z, x, ALU.mult), d)
                d = P.dve(ts_(z, z, -0.5, 1.5, ALU.mult, ALU.add), d)
                d = P.dve(tt_(y, y, z, ALU.mult), d)
                d = P.dve(stt_(OT2[:, :], OT2[:, :], y, SUBG, ALU.mult, ALU.mult), d, tsg)
            late_tr.append((n, t, qb, d))

        def stage_d(n, t, qb, d):
            OT2 = OTM[n // 2 % 2]
            tp = P.pe([tr_(PS[:, 3328:3456], OT2[:, :])], d, bankfree[6], tc)
            otmfree[n // 2 % 2] = tp
            a = P.act(act_(OT[:, t, 128 * qb:128 * qb + 128], PS[:, 3328:3456], ACT.Copy), tp)
            bankfree[6] = bankfree[6] + [a]
            last["ot"] = a

        fill = [None]

        def work(n):
            for _ in range(n):
                if fill[0] is not None and next(fill[0], "end") == "end":
                    fill[0] = None

        def step(item, w=0):
            late = late_tr[:]
            del late_tr[:]
            if item is not None:
                ta, dr = stage_a(*item)
                pend.append([item, ta, dr, None])
            for x in late:
                stage_d(*x)
            work(w // 2)
            k = len(pend) - (1 if item is not None else 0)
            ready = pend[:k]
            late = [p for p in ready if p[3] is not None]
            for p in ready:
                if p[3] is None:
                    p[3] = stage_b(*p[0], p[1])
                    break
            work(w - w // 2)
            for p in late[:1]:
                stage_c(*p[0], p[3], p[2])
                pend.remove(p)

        first = project(0)
        for _ in range(48):
            next(first)
        tct = P.pe([mm_(PS[:, 8 * b:8 * b + 8], NC8[0:8, 128 * b:128 * b + 128], m("ident")[0:8, 0:8])
                    for b in range(8)], dn, bankfree[0])
        dct = P.dve(cp_(CT, PS[:, 0:64]), tct)
        bankfree[0] = [dct]
        for _ in first:
            pass
        n = 0
        for t in range(8):
            fill[0] = project(t + 1) if t < 7 else None
            for qb in range(8):
                for i in range(2):
                    step((n, t, qb, i), 4)
                    n += 1
            work(1000)
        xdone = [("pe", P.n["pe"])]
        while pend or late_tr:
            step(None)
        aend = [(q, P.n[q]) for q in ("pe", "dve", "act", "pool")]
        resback[0] = [restore_tile(f, aend) for f in range(8)]
        state = {"ot": last["ot"]}
        tfree[0] = tfree[1] = list(pfree[0])
        tfree[2] = tfree[3] = list(pfree[1])
        tfree[6] = tfree[7] = list(ptfree[0])
        tfree[4] = tfree[5] = list(ptfree[1])
        toks = []
        for k in range(8):
            for c, (c0, c1) in enumerate(T):
                x, xh, xl = OT[:, k, c0:c1], XH[:, k, c0:c1], XL[:, k, c0:c1]
                a = P.act(act_(xh, x, ACT.Copy), state["ot"], xdone)
                p = P.dve(tt_(xl, x, xh, ALU.subtract), a)
                toks.append([a, p])
        osplit = toks[-1]
        acctok = [[None] * 8, [None] * 8]
        S_acc = S["acc"]
        out = nxt(lambda k, a, b: S_acc[:, k, a:b], "mix_post_g", 1.0, acctok, None)
        out.open = 0
        for f in range(8):
            iw, wh, wl, wt = W.get(f"OUT.{f}")
            for c, (c0, c1) in enumerate(T):
                b = (2 * f + c) % 8
                t = group(b, 512, unit8(wh, wl, c0, c1), wt, osplit)
                d = P.dve(cp_(S_acc[:, f, c0:c1], bank(b)), t, osplit)
                bankfree[b] = [d]
                acctok[c][f] = [d]
                if f == 7:
                    xfree_[0] = [t]
                    out.open = c + 1
            W.done(iw, t)
        return out

    def evac3(unit, fn, xt, b0, *toks):
        iw, wh, wl, wt = W.get(unit)
        for c, (c0, c1) in enumerate(CHUNKS):
            b = b0 + c
            t = group(b, c1 - c0, unit8(wh, wl, c0, c1), wt, xt[c], *toks)
            bankfree[b] = [fn(c, c0, c1, bank(b, c1 - c0), t)]
        W.done(iw, t)

    def conv4(out, x, wname, nw, bname, tile, srctoks, free):
        d = P.dve(ts_(out, x[:, 0:T2], v(wname, tile), v(bname, tile), ALU.mult, ALU.add), srctoks, free)
        for k in range(1, 4):
            d = P.dve(stt_(out, x[:, k:k + T2], v(wname, nw * k + tile), out, ALU.mult, ALU.add), d)
        return d

    def even(xt):
        V = S["lru"]
        XIN, U, TB = V["xin"], V["u"], V["tb"]
        UH, UL, YH, YL = S["uh"], S["ul"], S["yh"], S["yl"]
        pe0 = [("pe", P.n["pe"])]
        sm = V["sm"]
        AC, N8 = sm[:, 32:40], sm[:, 40:48]

        def decay():
            L, E1, Z, Z2, AC, N8 = [sm[:, 8 * i:8 * i + 8] for i in range(6)]
            lam = vec[:, VEC["lru_lambda_2"]:VEC["lru_lambda_2"] + 8]
            d = P.dve(ts_(L, lam, -1.0, None, ALU.mult), tc, lru_t)
            d = P.dve(tt_(E1, L, lam, ALU.min), d)
            a = P.act(act_(E1, E1, ACT.Exp), d)
            d = P.dve(ts_(Z, E1, 2.0, None, ALU.add), a)
            d = P.dve(lambda e: e.reciprocal(Z, Z), d)
            d = P.dve(tt_(Z, Z, E1, ALU.mult), d)
            d = P.dve(tt_(Z2, Z, Z, ALU.mult), d)
            d = P.dve(ts_(AC, Z2, 1.0 / 17, 1.0 / 15, ALU.mult, ALU.add), d)
            for q in (13, 11, 9, 7, 5, 3, 1):
                d = P.dve(tt_(AC, AC, Z2, ALU.mult), d)
                d = P.dve(ts_(AC, AC, 1.0 / q, None, ALU.add), d)
            d = P.dve(tt_(AC, AC, Z, ALU.mult), d)
            d = P.dve(ts_(L, L, 0.0, 8.0, ALU.max, ALU.mult), d)
            d = P.dve(stt_(AC, AC, 16.0, L, ALU.mult, ALU.add), d)
            ts8 = P.dve(ts_(N8, AC, -1.0, None, ALU.mult), d)
            return ts8
        S8 = AC
        ts8 = None
        tz = P.pool(lambda e, x=XIN: e.memset(x[:, 0:3], 0.0), pe0)
        R_, I_, A_, L_ = TB
        xinfree, ufree = [], [[], []]
        uhfree, yfree = [], []
        tbfree = {0: [], 1: [], 2: [], 3: []}
        ynb = [0]
        restok = None
        for g in range(4):
            ut = []
            for ti in range(2):
                tile = 2 * g + ti
                toks = []

                def to_xin(c, c0, c1, b, t):
                    a = P.act(act_(XIN[:, 3 + c0:3 + c1], b, ACT.Copy), t, xinfree, tz)
                    toks.append(a)
                    return a
                evac3(f"E.{tile}", to_xin, xt, 0 if ti == 0 else 3)
                if ts8 is None:
                    hx = xt.all()
                    lru_t = [tfree[i] for i in range(8)]
                    restok = [("dve", P.n["dve"]), ("pool", P.n["pool"])]
                    tm2 = load("act", "mat2", S["mat2"][:, :], A["mat2"], restok)
                    tbfree = {i: [lru_t] for i in range(4)}
                    ts8 = decay()
                d = conv4(U[ti], XIN, "lru_conv_w_2", 8, "lru_conv_b_2", tile, toks, ufree[ti])
                xinfree = [d]
                a = P.act(act_(UH[:, ti, :], U[ti], ACT.Copy), d, uhfree)
                p = P.pool(tt_(UL[:, ti, :], U[ti], UH[:, ti, :], ALU.subtract), a)
                ut += [a, p]
            il, lh, ll, lt = W.get(f"L.{g}")
            for tj in range(2):
                tile = 2 * g + tj
                st = {0: [], 1: [], 2: []}
                for which, dst, bname in ((0, R_, "lru_b_a_2"), (1, I_, "lru_b_x_2")):
                    for c, (c0, c1) in enumerate(CHUNKS):
                        b = 3 * which + c
                        parts = []
                        for ki in range(2):
                            o = which * 512 + ki * 256 + tj * 128
                            parts.append((lh[:, o:o + 128], ll[:, o:o + 128],
                                          UH[:, ki, c0:c1], UL[:, ki, c0:c1]))
                        t = group(b, c1 - c0, parts, lt, ut)
                        a = P.act(act_(dst[:, c0:c1], bank(b, c1 - c0), ACT.Sigmoid,
                                       bias=v(bname, tile)), t, tbfree[which])
                        bankfree[b] = [a]
                        st[which].append(a)
                uhfree = [t]
                G_ = XIN[:, 3:3 + T2]

                def to_g(c, c0, c1, b, t):
                    a = P.act(act_(G_[:, c0:c1], b, ACT.Sigmoid), t, xinfree)
                    d = P.dve(tt_(G_[:, c0:c1], b, G_[:, c0:c1], ALU.mult), a)
                    st[2].append(d)
                    return d
                if tj == 1:
                    W.done(il, t)
                evac3(f"E.{8 + tile}", to_g, xt, 0)
                s8, n8 = S8[:, tile:tile + 1], N8[:, tile:tile + 1]
                at = P.act(act_(L_, R_, ACT.Tanh, scale=s8), st[0], ts8, tbfree[3])
                exp_ln_tables()
                aa = P.act(act_(A_, R_, ACT.Exp, scale=n8), ts8, tbfree[2])
                d = P.dve(ts_(L_, L_, 1e-18, None, ALU.max), at)
                a1 = P.act(act_(R_, L_, ACT.Ln, scale=2.0), d, aa)
                a2 = P.act(act_(L_, L_, ACT.Ln, bias=1.0), a1)
                d = P.dve(tt_(R_, R_, L_, ALU.subtract), a1, a2)
                a3 = P.act(act_(R_, R_, ACT.Exp, scale=0.5), d)
                d = P.pool(tt_(I_, I_, U[tj], ALU.mult), st[1], ut)
                ufree[tj] = [d]
                d = P.dve(tt_(I_, I_, R_, ALU.mult), d, a3)
                tbfree[0] = [d]
                d = P.dve(lambda e: e.tensor_tensor_scan(L_, A_, I_, 0.0, ALU.mult, ALU.add), d, aa)
                tbfree[1] = tbfree[2] = [d]
                d = P.dve(tt_(L_, L_, G_, ALU.mult), d, st[2])
                xinfree = [d]
                a = P.act(act_(YH[:, tj, :], L_, ACT.Copy), d, yfree)
                p = P.pool(tt_(YL[:, tj, :], L_, YH[:, tj, :], ALU.subtract), a)
                tbfree[3] = [p]
            yt = [a, p]
            for hh in range(2):
                iw, wh, wl, wt = W.get(f"EO.{g}.{hh}")
                for fi in range(4):
                    f = 4 * hh + fi
                    for c, (c0, c1) in enumerate(CHUNKS):
                        b = 6 + ynb[0] % 2
                        ynb[0] += 1
                        parts = [(wh[:, k * 512 + fi * 128:k * 512 + fi * 128 + 128],
                                  wl[:, k * 512 + fi * 128:k * 512 + fi * 128 + 128],
                                  YH[:, k, c0:c1], YL[:, k, c0:c1]) for k in range(2)]
                        t = group(b, c1 - c0, parts, wt, yt)
                        r = RES[:, f, c0:c1]
                        d = P.dve(tt_(r, r, bank(b, c1 - c0), ALU.add), t, restok)
                        bankfree[b] = [d]
                W.done(iw, t)
            yfree = [t]
            restok = [d]
        lru_end = [d, t, a, p, ("pool", P.n["pool"]), ("act", P.n["act"])]
        tsp = P.dma("pool", "spill", lambda e: e.dma_start(A["rs"], RES[:, :, :]), d)
        V = S["ssd"]
        X, BC, BT, DT = V["x"], V["bc"], V["bt"], V["dt"]
        XIN, CV = V["xin"], V["cv"]
        tz = P.pool(lambda e, x=XIN: e.memset(x[:, 0:3], 0.0), lru_end)
        cvfree, xinfree = list(lru_end), list(lru_end)
        zdone = None
        for k in range(8):
            toks = []

            def to_z(c, c0, c1, b, t):
                a = P.act(act_(CV[:, c0:c1], b, ACT.Silu), t, cvfree)
                toks.append(a)
                return a
            evac3(f"E.{16 + k}", to_z, xt, 3 * (k % 2))
            zdone = P.dma("pool", "zs", lambda e, k=k: e.dma_start(A["zs"][k], CV), toks)
            cvfree = [zdone]
        nblk = 9
        blk = [(128 * c, min(128, T2 - 128 * c)) for c in range(nblk)]
        xtok = None
        for k in range(12):
            toks = []

            def to_x(c, c0, c1, b, t):
                a = P.act(act_(XIN[:, 3 + c0:3 + c1], b, ACT.Copy), t, xinfree, tz)
                toks.append(a)
                return a
            evac3(f"E.{24 + k}", to_x, xt, 0)
            d = conv4(CV, XIN, "ssd_conv_w_2", 12, "ssd_conv_b_2", k, toks, cvfree)
            xinfree = [d]
            dst = CV if k < 8 else BC[:, k - 8, :]
            a = P.act(act_(dst, CV, ACT.Silu), d, lru_end)
            cvfree = [a]
            if k < 10:
                src = dst
                for part in range(3):
                    bs = blk[4 * part:4 * part + 4]
                    b = 3 + part
                    t = P.pe([tr_(PS[0:n, b * 512 + 128 * j:b * 512 + 128 * j + 128], src[:, t0:t0 + n])
                              for j, (t0, n) in enumerate(bs)], a, bankfree[b], tc)
                    n = bs[0][1]
                    o = BT[0:n, 4 * part:4 * part + len(bs), (k - 8) * 128:(k - 7) * 128] if k >= 8 else \
                        X[0:n, 4 * part:4 * part + len(bs), k * 128:(k + 1) * 128]
                    i_ = PS[0:n, b * 512:b * 512 + 128 * len(bs)].rearrange("p (a b) -> p a b", a=len(bs))
                    xtok = P.dve(cp_(o, i_), t, lru_end)
                    bankfree[b] = [xtok]
                cvfree = [a, t]
        bctok = a
        exp_ln_tables()
        dtf, dte = XIN[0:16, 0:T2], CV[0:16, 0:T2]
        db = v("ssd_dt_bias_2")[0:16, :]
        toks = []

        def to_dt(c, c0, c1, b, t):
            d = P.dve(ts_(dtf[:, c0:c1], b[0:16, :], db, None, ALU.add), t, xinfree)
            toks.append(d)
            return d
        evac3("E.36", to_dt, xt, 0)
        xdone = [("pe", P.n["pe"])]
        d = softplus(dtf, dte, dtf, toks, cvfree, None)
        t = P.pe([mm_(PS[0:n, 1536 + 16 * c:1552 + 16 * c], dtf[:, t0:t0 + n], m("ident")[0:16, 0:16])
                  for c, (t0, n) in enumerate(blk)], d, bankfree[3])
        dd = [P.dve(cp_(DT[:, 0:8, :], PS[:, 1536:1664].rearrange("p (a b) -> p a b", a=8)), t, lru_end),
              P.dve(cp_(DT[0:16, 8, :], PS[0:16, 1664:1680]), t)]
        bankfree[3] = [dd[1]]
        dtt = dd[1]
        Q = S["scan"]
        ANEG = Q["aneg"]
        a = P.act(act_(ANEG, vec[:, VEC["ssd_a_log_2"]:VEC["ssd_a_log_2"] + 16], ACT.Exp), xdone)
        ta = P.dve(ts_(ANEG, ANEG, -1.0, None, ALU.mult), a)
        DD = vec[:, VEC["ssd_d_2"]:VEC["ssd_d_2"] + 16]
        ST = Q["state"]
        YT = RES
        sttok = [None, None]
        stread = [None, None]
        fr = {}

        def bc3(ap, w):
            p, h = ap.shape
            return ap.unsqueeze(2).to_broadcast([p, h, w])

        def bh(ap, h):
            p, w = ap.shape
            return ap.unsqueeze(1).to_broadcast([p, h, w])

        def r3(ap, h):
            return ap.rearrange("p (a b) -> p a b", a=h)

        ytok = None
        for c, (t0, n) in enumerate(blk):
            s2 = c % 2
            AD, EX, DDT, Y = Q["ad"][s2], Q["ex"][s2], Q["ddt"][s2], Q["y"][s2]
            d = P.dve(tt_(AD[0:n, :], DT[0:n, c, :], ANEG[0:n, :], ALU.mult), ta, dtt, fr.get(("ad", s2)))
            tad = d
            t = P.pe([mm_(PS[0:n, 0:16], m("triu")[0:n, 0:n], AD[0:n, :]),
                      mm_(PS[0:n, 16:32], m("low")[0:n, 0:n], AD[0:n, :]),
                      mm_(PS[:, 32:48], m("ones")[0:n, :], AD[0:n, :])], d, bankfree[0], tm2)
            a0 = P.act(act_(EX[0:n, 0:32], PS[0:n, 0:32], ACT.Exp), t, fr.get(("ex", s2)))
            a1 = P.act(act_(EX[:, 32:48], PS[:, 32:48], ACT.Exp), t)
            bankfree[0] = [a1]
            dq = P.dve(tt_(DDT[0:n, :], DT[0:n, c, :], EX[0:n, 16:32], ALU.mult), a0, fr.get(("ddt", s2)))
            ydone = []
            for g in range(2):
                k2 = g
                GT, M_, CBM, XD, XS, TX = (Q[q][k2] for q in ("gt", "m", "cbm", "xd", "xs", "tx"))
                hs = slice(8 * g, 8 * g + 8)
                xg = r3(X[0:n, c, 512 * g:512 * g + 512], 8)
                gt3 = r3(GT[0:n, 0:8 * n], 8)
                p = P.pool(tt_(gt3, bh(m("triu")[0:n, 0:n], 8), bc3(AD[0:n, hs], n), ALU.mult),
                           tad, fr.get(("gt", k2)), tm2)
                w = 4 * n
                t = P.pe([mm_(PS[0:n, 512:512 + w], m("low")[0:n, 0:n], GT[0:n, 0:w]),
                          mm_(PS[0:n, 1024:1024 + w], m("low")[0:n, 0:n], GT[0:n, w:2 * w])],
                         p, bankfree[1], bankfree[2])
                fr[("gt", k2)] = [t]
                a = None
                for q in range(2):
                    a = P.act(act_(M_[0:n, q * w:q * w + w], PS[0:n, 512 + 512 * q:512 + 512 * q + w], ACT.Exp),
                              t, fr.get(("m", k2)))
                bankfree[1] = bankfree[2] = [a]
                tcb = P.pe([mm_(PS[0:n, 2560:2560 + n], BC[:, g, t0:t0 + n], BC[:, 2 + g, t0:t0 + n])],
                           bctok, bankfree[5])
                d = P.dve(tt_(CBM[0:n, 0:n], PS[0:n, 2560:2560 + n], m("triu")[0:n, 0:n], ALU.mult),
                          tcb, fr.get(("cbm", k2)), tm2)
                bankfree[5] = [d]
                m3 = r3(M_[0:n, 0:8 * n], 8)
                dm = P.dve(tt_(m3, m3, bh(CBM[0:n, 0:n], 8), ALU.mult), a, d)
                fr[("cbm", k2)] = [dm]
                ps_ = P.pool(tt_(r3(XS[0:n, :], 8), xg, bc3(DT[0:n, c, hs], 64), ALU.mult),
                             xtok, dtt, fr.get(("xs", k2)))
                pd_ = P.pool(tt_(r3(XD[0:n, :], 8), xg, bc3(DDT[0:n, hs], 64), ALU.mult),
                             dq, fr.get(("xd", k2)))
                px_ = P.pool(tt_(r3(TX[0:n, :], 8), xg, bc3(DD[0:n, hs], 64), ALU.mult),
                             fr.get(("tx", k2)))
                ty = P.pe([mm_(PS[0:n, 1536 + 64 * h:1600 + 64 * h], M_[0:n, h * n:h * n + n],
                               XS[0:n, 64 * h:64 * h + 64]) for h in range(8)], dm, ps_, bankfree[3])
                fr[("m", k2)] = [ty]
                fr[("xs", k2)] = [ty]
                yv = Y[0:n, 512 * g:512 * g + 512]
                if c:
                    to = P.pe([mm_(PS[0:n, 2048:2560], BC[:, 2 + g, t0:t0 + n], ST[g])],
                              sttok[g], bankfree[4])
                    stread[g] = to
                    d = P.dve(tt_(r3(yv, 8), r3(PS[0:n, 2048:2560], 8), bc3(EX[0:n, hs], 64), ALU.mult),
                              to, a0, fr.get(("y", s2)))
                    bankfree[4] = [d]
                    d = P.dve(tt_(yv, yv, PS[0:n, 1536:2048], ALU.add), ty, d)
                    bankfree[3] = [d]
                    d = P.dve(tt_(yv, yv, TX[0:n, :], ALU.add), px_, d)
                else:
                    d = P.dve(tt_(yv, TX[0:n, :], PS[0:n, 1536:2048], ALU.add), ty, px_)
                    bankfree[3] = [d]
                fr[("tx", k2)] = [d]
                ydone.append(d)
                if c < nblk - 1:
                    tb_ = P.pe([mm_(PS[:, 2560:3072], BT[0:n, c, 128 * g:128 * g + 128], XD[0:n, :])],
                               pd_, xtok, bankfree[5])
                    fr[("xd", k2)] = [tb_]
                    if c:
                        d = P.dve(tt_(r3(ST[g], 8), r3(ST[g], 8), bc3(EX[:, 32 + 8 * g:40 + 8 * g], 64),
                                      ALU.mult), stread[g], a1, sttok[g])
                        d = P.dve(tt_(ST[g], ST[g], PS[:, 2560:3072], ALU.add), d, tb_)
                    else:
                        d = P.dve(cp_(ST[g], PS[:, 2560:3072]), tb_, xdone)
                    bankfree[5] = [d]
                    sttok[g] = d
            fr[("ad", s2)] = [t, p]
            fr[("ex", s2)] = [d, ydone]
            fr[("ddt", s2)] = [pd_]
            for half in range(2):
                b = 6 + half
                t = P.pe([tr_(PS[:, b * 512 + 128 * j:b * 512 + 128 * j + n],
                              Y[0:n, 512 * half + 128 * j:512 * half + 128 * j + 128], n) for j in range(4)],
                         ydone, bankfree[b], tc)
                src = PS[:, b * 512:b * 512 + 512].rearrange("p (a b) -> p a b", a=4)[:, :, 0:n]
                ytok = P.act(act_(YT[:, 4 * half:4 * half + 4, t0:t0 + n], src, ACT.Copy), t, tsp)
                bankfree[b] = [ytok]
            fr[("y", s2)] = [t]
        scan_end = [("pe", P.n["pe"]), ("dve", P.n["dve"]), ("pool", P.n["pool"]), ("act", P.n["act"])]
        for i in range(8):
            tfree[i] = list(scan_end)
        exp_ln_tables()
        gt = []
        for k in range(8):
            dst = V["zin"][k % 2]
            tl = P.dma("pool", f"zin{k % 2}", lambda e, k=k, dst=dst: e.dma_start(dst, A["zs"][k]),
                       zdone, scan_end, gt[k - 2:k - 1])
            gt.append(P.dve(tt_(YT[:, k, :], YT[:, k, :], dst, ALU.mult), tl, ytok))
        specs = []
        for c0, c1 in CHUNKS:
            for grp in range(2):
                specs.append((gt[4 * grp:4 * grp + 4], None,
                              (lambda k, a, b, grp=grp: YT[:, 4 * grp + k, a:b], "ssd_norm_2", c0, c1),
                              dict(k0=4 * grp)))
        yn = chains(specs, scan_end, per=2, KT=4, dim=512)
        back = {}

        def restore(f):
            if not back:
                y2 = yn[2]
                for k in range(8):
                    back[k] = P.dma("pool", f"back{k}", lambda e, k=k: e.dma_start(RES[:, k, :], A["rs"][:, k, :]),
                                    y2[k], tsp)
            return back[f]
        return add_gemm("EB", yn, restore, "odd_norm_2")

    def add_gemm(prefix, yn, restok, gname):
        nb = 0
        toks = [[None] * 8 for _ in CHUNKS]
        late = {}
        if gname:
            out = chains([(toks[c], None, (h_src, gname, c0, c1)) for c, (c0, c1) in enumerate(CHUNKS)], None)
            out.open = 0
        for f in range(8):
            iw, wh, wl, wt = W.get(f"{prefix}.{f}")
            for c, (c0, c1) in enumerate(CHUNKS):
                b = nb % 8
                nb += 1
                t = group(b, c1 - c0, unit8(wh, wl, c0, c1), wt, yn[c])
                late[c] = (b, t)
                if c < 2 and restok is not None and f == 0:
                    continue
                for cc, (bb, tt) in sorted(late.items()):
                    r = RES[:, f, CHUNKS[cc][0]:CHUNKS[cc][1]]
                    d = P.dve(tt_(r, r, bank(bb, CHUNKS[cc][1] - CHUNKS[cc][0]), ALU.add), tt,
                              restok(f) if restok else None)
                    bankfree[bb] = [d]
                    toks[cc][f] = [d]
                late = {}
                if f == 7 and gname:
                    xfree_[0] = [t]
                    out.open = c + 1
            W.done(iw, t)
        return out if gname else toks

    def odd(xt):
        V = S["odd"]
        OT, VR, GB = V["ot"], V["vr"], V["gb"]
        SPB, EB_, WB, AB = V["sp"], V["e"], V["w"], V["acc"]
        blk = [(128 * c, min(128, T2 - 128 * c)) for c in range(9)]
        pe0 = [("pe", P.n["pe"])]
        gdone = None
        for k in range(8):
            toks = []
            dst = (VR, V["q"][0])[k % 2]

            def to_g(c, c0, c1, b, t):
                a = P.act(act_(dst[:, c0:c1], b, ACT.Silu), t, pe0 if k < 2 else gst[k % 2])
                toks.append(a)
                return a
            if k == 0:
                gst = [None, None]
            evac3(f"Q.{24 + k}", to_g, xt, 3 * (k % 2))
            gdone = P.dma("pool", f"gs{k % 2}", lambda e, k=k, dst=dst: e.dma_start(A["gs"][k], dst), toks)
            gst[k % 2] = [gdone]
        exp_ln_tables()
        tsp = spill(xt)
        state = {}
        free = {}
        pend = []
        last = {"vr": gst[0], ("z", -2): gst[1]}
        tiles = {}

        def stage_a(it):
            n, t, i, ci, kb, top = it
            c0, c1 = CHUNKS[ci]
            s0, ks = blk[kb]
            a0 = max(c0, s0)
            x0, x1 = a0 - c0, c1 - c0
            b = n % 4
            Q_, K_ = V["q"][t % 2], V["k"][t % 2]
            out = PS[0:ks, b * 512 + x0:b * 512 + x1]
            fns = [mm_(out, K_[64 * i:64 * i + 64, s0:s0 + ks], Q_[64 * i:64 * i + 64, a0:c1],
                       True, False, True)]
            e1 = min(c1, s0 + 128)
            if s0 < c1 and e1 > a0:
                fns.append(mm_(PS[0:ks, b * 512 + x0:b * 512 + e1 - c0], idb[0:ks, 0:ks],
                               smb[0:ks, a0 - s0:e1 - s0], False, False, True))
            tp = P.pe(fns, bankfree[b], tiles[t]["q"], tiles[t]["k"], tb)
            last["z", t] = tp
            s = n % 3
            ev, sp = EB_[n % 2][0:ks, 0:x1 - x0], SPB[s][0:ks, 0:x1 - x0]
            d = softplus(sp, ev, out, tp, free.get(("e", n % 2)), free.get(("sp", s)))
            free[("e", n % 2)] = [d]
            cur = state.get("acc")
            if kb:
                ns = (state.get("slot", 0) + 1) % 3
                state["slot"] = ns
                nxt = AB[ns]
                was = [free.get(("acc", ns)), free.get(("accr", ns)), free.get(("accw", ns))]
                if top:
                    dz = P.pool(lambda e: e.memset(nxt[:, 0:c1 - c0], 0.0), *was)
                    p = P.pool(cp_(nxt[0:ks, x0:x1], sp), dz, d)
                else:
                    cs_, ctok = cur
                    old = AB[cs_]
                    if ks < 128 or x0 > 0:
                        p = P.pool(cp_(nxt[:, 0:c1 - c0], old[:, 0:c1 - c0]), ctok, *was)
                        p = P.pool(tt_(nxt[0:ks, x0:x1], old[0:ks, x0:x1], sp, ALU.add), p, d)
                    else:
                        p = P.pool(tt_(nxt[:, x0:x1], old[:, x0:x1], sp, ALU.add), ctok, d, *was)
                    free[("accr", cs_)] = [p]
                free[("accw", ns)] = [p]
                state["acc"] = (ns, p)
                free[("spa", s)] = [p]
            else:
                free[("spa", s)] = []
            return d, cur

        def stage_b(it, d, cur):
            n, t, i, ci, kb, top = it
            c0, c1 = CHUNKS[ci]
            s0, ks = blk[kb]
            x0, x1 = max(c0, s0) - c0, c1 - c0
            b = n % 4
            s = n % 3
            out = PS[0:ks, b * 512 + x0:b * 512 + x1]
            fns = [mm_(out, m("ntri")[0:ks, 0:ks], SPB[s][0:ks, 0:x1 - x0], False, top, True)]
            tacc = None
            if not top:
                tacc = cur[1]
                fns.append(mm_(out, m("nones")[:, 0:ks], AB[cur[0]][:, x0:x1], False, True, True))
            tp = P.pe(fns, d, tacc)
            free[("sp", s)] = [tp] + free[("spa", s)]
            if not top:
                free[("acc", cur[0])] = [tp]
            w = WB[n % 2][0:ks, 0:x1 - x0]
            a = P.act(act_(w, out, ACT.Exp), tp, free.get(("w", n % 2)))
            bankfree[b] = [a]
            return a

        def stage_c(it, a):
            n, t, i, ci, kb, top = it
            c0, c1 = CHUNKS[ci]
            s0, ks = blk[kb]
            x0, x1 = max(c0, s0) - c0, c1 - c0
            ob = 4 + i
            VT = V["vt"][t % 2]
            out = PS[64 * i:64 * i + 64, ob * 512 + x0:ob * 512 + x1]
            tp = P.pe([mm_(out, VT[0:ks, kb, 64 * i:64 * i + 64], WB[n % 2][0:ks, 0:x1 - x0],
                           top, kb == 0, True)], a, bankfree[ob], tiles[t]["v"])
            free[("w", n % 2)] = [tp]
            last["v", t] = tp
            if kb == 0:
                d = P.dve(cp_(OT[64 * i:64 * i + 64, t, c0:c1], PS[64 * i:64 * i + 64,
                                                                ob * 512:ob * 512 + c1 - c0]), tp)
                bankfree[ob] = [d]
                state["o"] = d
            else:
                bankfree[ob] = []

        fill = [None]

        def work(n):
            for _ in range(n):
                if fill[0] is not None and next(fill[0], "end") == "end":
                    fill[0] = None

        def step(it, w=0):
            if it is not None:
                d, tacc = stage_a(it)
                pend.append([it, d, tacc, None])
            work(w)
            k = len(pend) - (1 if it is not None else 0)
            ready = pend[:k]
            late = [p for p in ready if p[3] is not None]
            for p in ready:
                if p[3] is None:
                    p[3] = stage_b(p[0], p[1], p[2])
                    break
            work(w)
            for p in late[:1]:
                stage_c(p[0], p[3])
                pend.remove(p)

        osplit = KToks([None] * 8)
        gtok = {}

        def gate(k):
            tl = P.dma("pool", "gin", lambda e: e.dma_start(GB, A["gs"][k]), gst[0], gst[1], tsp,
                       gtok.get(k - 1))
            gtok[k] = P.dve(tt_(OT[:, k, :], OT[:, k, :], GB, ALU.mult), tl, state["o"])

        def split(k):
            a = P.act(act_(XH[:, k, :], OT[:, k, :], ACT.Copy), gtok[k], xdone)
            q = P.pool(tt_(XL[:, k, :], OT[:, k, :], XH[:, k, :], ALU.subtract), a)
            osplit[k] = [a, q]

        def project(t):
            s = t % 2
            QT, KT_, VT = V["q"][s], V["k"][s], V["vt"][s]
            fr = [last.get(("z", t - 2)), last.get(("v", t - 2)), tsp]
            tl = {}
            nb = 0
            for which, dst, scale in (("q", QT, 0.125), ("k", KT_, 1.0), ("v", VR, 1.0)):
                iw, wh, wl, wt = W.get(f"Q.{8 * 'qkv'.index(which) + t}")
                toks = []
                for c, (c0, c1) in enumerate(CHUNKS):
                    b = 6 + nb % 2
                    nb += 1
                    P.wait("pe", [bankfree[b], wt, xt[c]])
                    for k, (a, b_, x, y) in enumerate(unit8(wh, wl, c0, c1)):
                        tk = P.pe(mm3(bank(b, c1 - c0), a, b_, x, y, k == 0, k == 7))
                        if k < 7:
                            yield
                    a = P.act(act_(dst[:, c0:c1], bank(b, c1 - c0), ACT.Copy, scale=scale), tk,
                              last["vr"] if which == "v" else fr)
                    bankfree[b] = [a]
                    toks.append(a)
                    yield
                W.done(iw, tk)
                tl[which] = toks
            if t == 7:
                xdone.append(tk)
            for part in range(3):
                bs = blk[4 * part:4 * part + 4]
                b = 6 + nb % 2
                nb += 1
                tp = P.pe([tr_(PS[0:w, b * 512 + 128 * j:b * 512 + 128 * j + 128], VR[:, t0:t0 + w])
                           for j, (t0, w) in enumerate(bs)], tl["v"], bankfree[b], tc)
                w = bs[0][1]
                i_ = PS[0:w, b * 512:b * 512 + 128 * len(bs)].rearrange("p (a b) -> p a b", a=len(bs))
                dv = P.dve(cp_(VT[0:w, 4 * part:4 * part + len(bs), :], i_), tp, fr)
                bankfree[b] = [dv]
                yield
            last["vr"] = tp
            tl["v"] = dv
            tiles[t] = tl

        xdone = []
        for _ in project(0):
            pass
        n = 0
        for t in range(8):
            m_ = 0
            fill[0] = project(t + 1) if t < 7 else None
            for ci in range(3):
                top = (CHUNKS[ci][1] - 1) // 128
                for i in range(2):
                    for kb in range(top, -1, -1):
                        step((n, t, i, ci, kb, kb == top), 1)
                        n += 1
                        m_ += 1
                        if t and m_ == 6:
                            gate(t - 1)
                        if t == 7 and m_ > 6 and m_ % 4 == 0 and osplit[6] is None:
                            split(sum(s is not None for s in osplit))
            work(1000)
        while pend:
            step(None)
        gate(7)
        split(7)
        end = [("dve", P.n["dve"]), ("pe", P.n["pe"])]
        back = [restore_tile(f, end) for f in range(8)]
        return add_gemm("QO", [osplit] * 3, lambda f: back[f], None)

    def final(toks):
        exp_ln_tables()
        for ci, (c0, c1) in enumerate(CHUNKS):
            c0 = max(c0, META)
            n = c1 - c0
            rs = 2 + 2 * (ci % 2)
            for tr in stats(h_src, 8, c0, c1, toks[ci], ci % 2, D, 1.0, statbusy):
                pass
            for k in range(8):
                s, tmp = (3, 7, 0, 1)[k % 4], TT[(3, 7, 0, 1)[k % 4]][:, 0:n]
                d = P.dve(stt_(tmp, h_src(k, c0, c1), v("final_norm_2", k), TT[rs][:, 0:n], ALU.mult,
                               ALU.mult), tr, tfree[s])
                tfree[rs] = [d]
                t = load("sp" if k % 2 else "act", f"out{s}", A["out"][:, k, c0 - META:c1 - META], tmp, d)
                tfree[s] = [t]

    def run():
        tx = [[], []]
        for c, (c0, c1) in enumerate(FFN_CHUNKS):
            for k in range(0, 8, 2):
                t = load(("act", "pool")[k // 2 % 2], f"x{c}{k}", RES[:, k:k + 2, META + c0:META + c1],
                         A["x"][:, k:k + 2, c0:c1])
                tx[c] += [[t], [t]]
        tm = load("act", "meta", RES[:, :, 0:META], A["meta"])
        exp_ln_tables()
        xt = chains([(tx[c], None, (res_src, "ffn1_pre_g", c0, c1)) for c, (c0, c1) in enumerate(FFN_CHUNKS)], [])
        xt = ffn(1, xt, to_first("mix_pre_g"))
        xt = mixer(xt, to_first("ffn2_pre_g"))
        if xt is None:
            return
        P.wait("act", [tm])
        P.wait("dve", [tm])
        xt = ffn(2, xt, to_second)
        xt = even(xt)
        toks = odd(xt)
        final(toks)

    run()
    P.wait("sp", [(sem, v) for sem, v in sorted(P.dman.items())])
    return P, W


def layout(nc, ctx):
    F32, F32R, BF = mybir.dt.float32, mybir.dt.float32r, mybir.dt.bfloat16
    base = 16512
    S = {}

    def at(name, shape, dt, off):
        return nc.alloc_sbuf_tensor_at(name, [128] + shape, dt, offset=off)

    o = base
    S["vec"] = at("vec", [NVEC], F32, o)
    o += (NVEC * 4 + 31) // 32 * 32
    S["mat"] = at("mat", [len(MATS) * 128], F32, o)
    o += len(MATS) * 512
    S["mat2"] = at("mat2", [len(MATS2) * 128], F32, o)
    lam = at("mlam", [384], F32, o)
    otm = at("motm", [128], F32, o + 1536)
    o += len(MATS2) * 512
    for n in ("idb", "cmb", "smb"):
        S[n] = at(n, [128], BF, o)
        o += 256
    S["raw"] = [at(f"raw{i}", [1024], F32, o + 4096 * i) for i in range(2)]
    o += 8192
    S["whi"] = [at(f"whi{i}", [1024], F32R, o + 8192 * i) for i in range(3)]
    S["wlo"] = [at(f"wlo{i}", [1024], F32R, o + 8192 * i + 4096) for i in range(3)]
    o += 24576
    S["res"] = at("res", [8, T2], F32, o)
    o += 8 * T2 * 4
    S["xh"] = at("xh", [8, T2], F32R, o)
    S["xl"] = at("xl", [8, T2], F32R, o + 8 * T2 * 4)
    o += 2 * 8 * T2 * 4
    free0 = o
    arena = at("arena", [(229344 - free0) // 4], F32, free0)

    def cut(off, shape):
        n = 1
        for k in shape:
            n *= k
        ap = arena[:, off // 4:off // 4 + n]
        return ap if len(shape) == 1 else ap.rearrange("p (a b) -> p a b", a=shape[0])

    S["acc"] = cut(0, [8, T1])
    S["hh"] = at("hh", [4, T1], F32R, free0 + 32768)
    S["hl"] = at("hl", [4, T1], F32R, free0 + 49152)
    S["t"] = [cut(off + 2048 * i, [512]) for off in (65536, 57344) for i in range(4)]
    S["ot"] = cut(0, [8, T1])
    M = S["mix"] = {}
    q0 = 32768
    ar3 = at("arena3", [8 * T2], F32, free0 - 3 * 8 * T2 * 4)

    def cut3(off, shape):
        n = 1
        for k in shape:
            n *= k
        ap = ar3[:, off // 4:off // 4 + n]
        return ap if len(shape) == 1 else ap.rearrange("p (a b) -> p a b", a=shape[0])

    M["q"], M["k"] = [cut(q0, [T1]), cut3(0, [T1])], [cut(q0 + 4096, [T1]), cut3(4096, [T1])]
    M["vt"] = [cut(q0 + 8192, [8, 128]), cut3(8192, [8, 128])]
    M["ncb"] = [[cut(q0 + 12288 + 4096 * i, [T1]) for i in range(2)],
                [cut3(16384 + 4096 * i, [T1]) for i in range(2)]]
    M["vr"], M["rt"] = cut3(12288, [T1]), cut3(24576, [T1])
    M["sq"] = cut3(29184, [128])
    M["nc8"] = cut(q0 + 20480, [T1])
    cs = M["cs"] = cut(q0 + 12288, [2, T1])
    M["cos"], M["sin"] = cs[:, 0, :], cs[:, 1, :]
    M["pt"] = [cut(q0 + 24576 + 4096 * i, [T1]) for i in range(2)]
    M["p"] = [cut(q0 + 32768 + 4096 * i, [T1]) for i in range(2)]
    M["otm"], M["lam"] = [otm, cut3(28672, [128])], lam
    M["sm"] = cut(q0 + 40960, [128])
    f = free0
    S["uh"], S["ul"] = at("uh", [2, T2], F32R, f), at("ul", [2, T2], F32R, f + 8320)
    S["yh"], S["yl"] = at("yh", [2, T2], F32R, f + 16640), at("yl", [2, T2], F32R, f + 24960)
    V = S["lru"] = {}
    V["xin"] = cut(33280, [T2 + 8])
    V["u"] = [cut(37472 + 4160 * i, [T2]) for i in range(2)]
    V["tb"] = [cut(45792 + 4160 * i, [T2]) for i in range(4)]
    V["sm"] = cut(62432, [64])
    V = S["ssd"] = {}
    V["x"] = cut(0, [9, 1024])
    V["bc"] = cut(36864, [4, T2])
    V["bt"] = cut(53504, [9, 256])
    V["dt"] = cut(62720, [9, 16])
    V["xin"] = cut(63296, [T2 + 8])
    V["cv"] = cut(67488, [T2])
    V["zin"] = [cut(4160 * i, [T2]) for i in range(2)]
    ar2 = at("arena2", [2 * 8 * T2], F32, free0 - 2 * 8 * T2 * 4)
    Q = S["scan"] = {}
    pos = 0
    for name, num, width in (("state", 2, 512), ("gt", 2, 1024), ("m", 2, 1024), ("cbm", 2, 128),
                             ("xd", 2, 512), ("xs", 2, 512), ("tx", 2, 512), ("y", 2, 1024),
                             ("ad", 2, 16), ("ex", 2, 48), ("ddt", 2, 16)):
        Q[name] = []
        for _ in range(num):
            Q[name].append(ar2[:, pos:pos + width])
            pos += width
    Q["aneg"] = ar2[:, pos:pos + 16]
    V = S["odd"] = {}
    V["ot"] = cut(0, [8, T2])
    V["q"], V["k"], V["vr"] = (cut(33280 + 4160 * i, [T2]) for i in range(3))
    V["q"], V["k"] = [V["q"], cut3(0, [T2])], [V["k"], cut3(4160, [T2])]
    V["gb"] = cut3(8320, [T2])
    V["vt"] = [cut(45760, [9, 128]), cut3(12480, [9, 128])]
    pos = 50368
    for name, num in (("sp", 3), ("e", 2), ("w", 2), ("acc", 3)):
        V[name] = [cut(pos + 1408 * i, [352]) for i in range(num)]
        pos += 1408 * num
    S["ps"] = ctx.enter_context(nc.psum_tensor("ps", [128, 4096], F32))
    return S


def build(nc, A):
    from contextlib import ExitStack
    with ExitStack() as ctx:
        S = layout(nc, ctx)
        _, W = emit(nc, A, S, None)
        P, _ = emit(nc, A, S, W.asked)
        names = list(Prog.ENG) + sorted(P.dman)
        sems = {n: ctx.enter_context(nc.semaphore("s_" + n)) for n in names}
        block = ctx.enter_context(nc.Block())

        def play(eng, key):
            for item in P.q[key]:
                if item[0] == "wait":
                    eng.wait_ge(sems[item[1]], item[2])
                else:
                    ins = item[1](eng)
                    if item[2] is not None:
                        ins.then_inc(sems[item[2]], item[3])

        @block.tensor
        def _(eng):
            play(eng, "pe")

        @block.scalar
        def _(eng):
            play(eng, "act")

        @block.vector
        def _(eng):
            play(eng, "dve")

        @block.gpsimd
        def _(eng):
            play(eng, "pool")

        @block.sync
        def _(eng):
            play(eng, "sp")


def _tiles(w):
    K, N = w.shape
    return w.reshape(K // 128, 128, N // 128, 128).transpose(2, 1, 0, 3).reshape(N // 128, 128, -1)


def _pairs(w):
    return w.reshape(2, 128, 2, 512).transpose(2, 1, 0, 3).reshape(2, 128, 1024)


def _pack(I):
    U = {}

    def put(prefix, arr):
        for i, a in enumerate(arr):
            U[f"{prefix}.{i}"] = a

    for f in (1, 2):
        put(f"G{f}", _tiles(I[f"ffn{f}_w_gate"][0]))
        put(f"U{f}", _tiles(I[f"ffn{f}_w_up"][0]))
        wd = I[f"ffn{f}_w_down"][0]
        for b in range(11):
            put(f"D{f}.{b}", _pairs(wd[256 * b:256 * b + 256]))
    w = I["w_in"][0]
    w = np.concatenate([w[:, 0:1536], w[:, 1544:3080], w[:, 1536:1544], np.zeros((D, 120), w.dtype)], axis=1)
    put("IN", _tiles(w))
    put("OUT", _tiles(I["w_out"][0]))
    w = I["even_w_in_2"][0]
    w = np.concatenate([w, np.zeros((D, 112), w.dtype)], axis=1)
    put("E", _tiles(w))
    for g in range(4):
        wa = I["lru_w_a_2"][0, g].reshape(2, 128, 256).transpose(1, 0, 2).reshape(128, 512)
        wx = I["lru_w_x_2"][0, g].reshape(2, 128, 256).transpose(1, 0, 2).reshape(128, 512)
        U[f"L.{g}"] = np.concatenate([wa, wx], axis=1)
        put(f"EO.{g}", _pairs(I["even_w_out_2"][0][256 * g:256 * g + 256]))
    put("EB", _tiles(I["even_w_out_2"][0][1024:]))
    put("Q", _tiles(I["odd_w_in_2"][0]))
    put("QO", _tiles(I["odd_w_out_2"][0]))
    return np.stack([U[n] for n in UNITS])


def _vectors(I):
    out = np.zeros((128, NVEC), np.float32)

    def fm(a):
        return a.reshape(-1, 128).T

    for n in ("ffn1_pre_g", "ffn1_post_g", "mix_pre_g", "mix_post_g", "ffn2_pre_g", "ffn2_post_g",
              "even_norm_2", "odd_norm_2", "final_norm_2", "lru_conv_b_2", "lru_b_a_2", "lru_b_x_2",
              "lru_lambda_2", "ssd_conv_b_2", "ssd_norm_2"):
        a = fm(I[n].reshape(-1))
        out[:, VEC[n]:VEC[n] + a.shape[1]] = a
    for n, w in (("lru_conv_w_2", 8), ("ssd_conv_w_2", 12)):
        for k in range(4):
            out[:, VEC[n] + k * w:VEC[n] + (k + 1) * w] = fm(I[n][0, k])
    out[0:8, VEC["fox_forget_b"]] = I["fox_forget_b"][0]
    out[0:16, VEC["ssd_dt_bias_2"]] = I["ssd_dt_bias_2"][0]
    for n, w in (("ssd_a_log_2", 16), ("ssd_d_2", 16)):
        out[:, VEC[n]:VEC[n] + w] = I[n].reshape(1, w)
    return out


def _mats():
    p = np.arange(128)
    i, j = p[:, None], p[None, :]
    M = {"ident": i == j, "ones": i >= 0 * j, "triu": i <= j, "low": i > j}
    M = {k: a.astype(np.float32) for k, a in M.items()}
    M["ntri"] = -(i >= j).astype(np.float32)
    M["nones"] = -np.ones((128, 128), np.float32)
    rot = np.zeros((128, 128), np.float32)
    for b in (0, 64):
        for a in range(8):
            rot[b + a + 8, b + a] = -1.0
            rot[b + a, b + a + 8] = 1.0
    M["rot"] = rot
    M["cmask"] = np.where(j > i, NEG, 0.0).astype(np.float32)
    M["smask"] = np.where(i >= j, NEG, 0.0).astype(np.float32)
    return [np.concatenate([M[n] for n in names], axis=1) for names in (MATS, MATS2, ("cmask", "smask"))]


def _rope():
    inv = (np.float32(500000.0) ** (-np.arange(0, 16, 2, dtype=np.float32) / np.float32(16))).astype(np.float32)
    ang = np.arange(T1, dtype=np.float32)[None, :] * inv[:, None]
    c, s = np.ones((128, T1), np.float32), np.zeros((128, T1), np.float32)
    for b in (0, 8, 64, 72):
        c[b:b + 8], s[b:b + 8] = np.cos(ang), np.sin(ang)
    return np.stack([c, s], axis=1)


def kernel(**inputs):
    import concourse.bacc as _bacc
    from concourse.bass_utils import run_bass_kernel_spmd as _run

    I = {k: np.asarray(a) for k, a in inputs.items()}
    fm = lambda a: np.ascontiguousarray(a.T.reshape(8, 128, -1).transpose(1, 0, 2))
    lam = np.concatenate([I[f"diff_lambda_{n}"].reshape(-1) for n in ("q1", "k1", "q2", "k2")]
                         + [I["diff_subln_g"].reshape(-1)])
    arrays = {
        "in_x_dram": fm(I["x"][0]),
        "in_meta_dram": fm(I["meta_2"]),
        "in_w_dram": _pack(I),
        "in_vec_dram": _vectors(I),
        "in_lam_dram": np.ascontiguousarray(np.broadcast_to(lam[None, :], (128, 384))),
        "in_mat_dram": _mats()[0],
        "in_mat2_dram": _mats()[1],
        "in_masks_dram": _mats()[2],
        "in_rope_dram": _rope(),
    }
    nc = _bacc.Bacc("TRN2", target_bir_lowering=False, num_devices=1)
    A = {}
    for name, a in arrays.items():
        A[name[3:-5]] = nc.dram_tensor(name, a.shape, mybir.dt.from_np(a.dtype), kind="ExternalInput").ap()
    A["out"] = nc.dram_tensor("out_0_dram", (128, 8, T1), mybir.dt.float32, kind="ExternalOutput").ap()
    A["zs"] = nc.dram_tensor("zs_scratch", (8, 128, T2), mybir.dt.float32).ap()
    A["gs"] = nc.dram_tensor("gs_scratch", (8, 128, T2), mybir.dt.float32).ap()
    A["rs"] = nc.dram_tensor("rs_scratch", (128, 8, T2), mybir.dt.float32).ap()
    build(nc, A)
    r = _run(nc, [arrays], core_ids=[0])
    got = r.results[0]["out_0_dram"]
    return np.ascontiguousarray(got.transpose(1, 0, 2).reshape(D, T1).T[None])
```

```python
import math

import concourse.bass as bass
from concourse import mybir
import numpy as np

D = 1024
T1 = 1024
META = 16
T2 = T1 + META
FF = 2816
EPS = 1e-6
NEG = -1e30
FFN_CHUNKS = [(0, 512), (512, 1024)]
CHUNKS = [(0, 352), (352, 704), (704, 1040)]

UNITS = []
for _f in (1, 2):
    UNITS += [f"G{_f}.{j}" for j in range(22)]
    UNITS += [f"U{_f}.{j}" for j in range(22)]
    UNITS += [f"D{_f}.{b}.{c}" for b in range(11) for c in range(2)]
UNITS += [f"IN.{i}" for i in range(25)]
UNITS += [f"OUT.{i}" for i in range(8)]
UNITS += [f"E.{i}" for i in range(37)]
UNITS += [f"L.{g}" for g in range(4)]
UNITS += [f"EO.{g}.{c}" for g in range(4) for c in range(2)]
UNITS += [f"EB.{i}" for i in range(8)]
UNITS += [f"Q.{i}" for i in range(32)]
UNITS += [f"QO.{i}" for i in range(8)]
UNIT_AT = {name: n for n, name in enumerate(UNITS)}

VEC = {}
_n = 0
for _name, _w in [("ffn1_pre_g", 8), ("ffn1_post_g", 8), ("mix_pre_g", 8), ("mix_post_g", 8),
                  ("ffn2_pre_g", 8), ("ffn2_post_g", 8), ("even_norm_2", 8), ("odd_norm_2", 8),
                  ("final_norm_2", 8), ("lru_conv_w_2", 32), ("lru_conv_b_2", 8), ("lru_b_a_2", 8),
                  ("lru_b_x_2", 8), ("lru_lambda_2", 8), ("ssd_conv_w_2", 48), ("ssd_conv_b_2", 12),
                  ("ssd_norm_2", 8), ("fox_forget_b", 1), ("ssd_dt_bias_2", 1),
                  ("ssd_a_log_2", 16), ("ssd_d_2", 16)]:
    VEC[_name] = _n
    _n += _w
NVEC = _n
MATS = ["ident", "ones", "rot"]
MATS2 = ["triu", "low", "ntri", "nones"]


class Prog:

    ENG = ("pe", "act", "dve", "pool", "sp")

    def __init__(self):
        self.q = {e: [] for e in self.ENG}
        self.n = {e: 0 for e in self.ENG}
        self.waited = {}
        self.dman = {}

    def wait(self, eng, toks):
        for t in toks:
            if t is None:
                continue
            if isinstance(t, list):
                self.wait(eng, t)
                continue
            sem, v = t
            if self.waited.get((eng, sem), 0) < v:
                self.waited[(eng, sem)] = v
                self.q[eng].append(("wait", sem, v))

    def do(self, eng, fn, *toks):
        self.wait(eng, toks)
        self.n[eng] += 1
        self.q[eng].append(("ins", fn, eng, 1))
        return (eng, self.n[eng])

    def act(self, fn, *toks):
        return self.do("act", fn, *toks)

    def dve(self, fn, *toks):
        return self.do("dve", fn, *toks)

    def pool(self, fn, *toks):
        return self.do("pool", fn, *toks)

    def act_raw(self, fn):
        self.q["act"].append(("ins", fn, None, 0))

    def pe(self, fns, *toks):
        self.wait("pe", toks)
        for fn in fns[:-1]:
            self.q["pe"].append(("ins", fn, None, 0))
        self.n["pe"] += 1
        self.q["pe"].append(("ins", fns[-1], "pe", 1))
        return ("pe", self.n["pe"])

    def dma(self, eng, sem, fn, *toks):
        self.wait(eng, toks)
        self.dman[sem] = self.dman.get(sem, 0) + 16
        self.q[eng].append(("ins", fn, sem, 16))
        return (sem, self.dman[sem])


class Weights:

    NRAW, NSPL = 2, 3

    def __init__(self, P, order, dram, raw, hi, lo, COPY, SUB):
        self.P, self.order, self.dram = P, order, dram
        self.raw, self.hi, self.lo = raw, hi, lo
        self.COPY, self.SUB = COPY, SUB
        self.asked = []
        self.eager = False
        self.nload = self.nsplit = 0
        self.loaded, self.parted, self.free = {}, {}, {}

    def _load(self, i):
        s = i % self.NRAW
        src = self.dram[UNIT_AT[self.order[i]]]
        dst = self.raw[s][:, :]
        self.loaded[i] = self.P.dma("sp", f"w{s}", lambda e: e.dma_start(dst, src),
                                    self.parted.get(i - self.NRAW))

    def _split(self, i):
        s, r = i % self.NSPL, i % self.NRAW
        raw, hi, lo, COPY, SUB = self.raw[r], self.hi[s], self.lo[s], self.COPY, self.SUB
        n = {"D": 1024, "L": 1024}.get(self.order[i][0], 1024)
        a = self.P.act(lambda e: e.activation(hi[:, 0:n], raw[:, 0:n], COPY),
                       self.loaded[i], self.free.get(i - self.NSPL))
        b = self.P.pool(lambda e: e.tensor_tensor(lo[:, 0:n], raw[:, 0:n], hi[:, 0:n], SUB),
                        self.loaded[i], self.free.get(i - self.NSPL), a)
        self.parted[i] = [a, b]

    def get(self, name):
        i = len(self.asked)
        self.asked.append(name)
        if self.order is None:
            return i, self.hi[0], self.lo[0], []
        assert self.order[i] == name
        while self.nsplit <= min(i + 1, len(self.order) - 1):
            while self.nload <= min(self.nsplit + 1, len(self.order) - 1):
                if self.nload >= self.NRAW and (self.nload - self.NRAW) not in self.parted:
                    break
                self._load(self.nload)
                self.nload += 1
            self._split(self.nsplit)
            self.nsplit += 1
        while self.nload < len(self.order) and (self.nload - self.NRAW) in self.parted:
            self._load(self.nload)
            self.nload += 1
        return i, self.hi[i % self.NSPL], self.lo[i % self.NSPL], self.parted[i]

    def done(self, i, tok):
        self.free[i] = tok
        j = self.nsplit
        if not self.eager or self.order is None or j >= len(self.order) or j > len(self.asked) + 1:
            return
        if j - self.NSPL in self.free:
            while self.nload <= j:
                self._load(self.nload)
                self.nload += 1
            self._split(j)
            self.nsplit += 1


def emit(nc, A, S, order):
    ALU = mybir.AluOpType
    ACT = mybir.ActivationFunctionType
    AX = mybir.AxisListType
    P = Prog()
    W = Weights(P, order, A["w"], S["raw"], S["whi"], S["wlo"], ACT.Copy, ALU.subtract)
    PS = S["ps"]
    bankfree = {b: [] for b in range(8)}
    RES, XH, XL = S["res"], S["xh"], S["xl"]
    TT = S["t"]
    vec, mat = S["vec"], S["mat"]


    def v(name, i=0):
        c = VEC[name] + i
        return vec[:, c:c + 1]

    def m(name):
        if name in MATS2:
            i = MATS2.index(name)
            return S["mat2"][:, i * 128:(i + 1) * 128]
        i = MATS.index(name)
        return mat[:, i * 128:(i + 1) * 128]

    def bank(b, n=512, p0=0, p1=128):
        return PS[p0:p1, b * 512:b * 512 + n]

    def load(eng, sem, dst, src, *toks):
        return P.dma(eng, sem, lambda e: e.dma_start(dst, src), *toks)

    tc = [load("act", "cst", vec[:, :], A["vec"]), load("act", "cst", mat[:, :], A["mat"]),
          load("act", "cst", TT[0][:, 0:256], A["masks"])]
    tc = tc[-1]
    idb, cmb, smb = S["idb"], S["cmb"], S["smb"]
    tb = [P.dve(lambda e: e.tensor_copy(idb[:, :], m("ident")), tc),
          P.dve(lambda e: e.tensor_copy(cmb[:, :], TT[0][:, 0:128]), tc),
          P.dve(lambda e: e.tensor_copy(smb[:, :], TT[0][:, 128:256]), tc)][-1]

    def mm3(out, whi, wlo, xhi, xlo, first, last):
        return [lambda e: e.matmul(out, whi, xhi, start=first, stop=False),
                lambda e: e.matmul(out, wlo, xhi, start=False, stop=False),
                lambda e: e.matmul(out, whi, xlo, start=False, stop=last)]

    def group(b, n, parts, *toks):
        assert b not in statbusy
        P.wait("pe", [bankfree[b]])
        by = [t for t in toks if isinstance(t, KToks)]
        P.wait("pe", [t for t in toks if not isinstance(t, KToks)])
        for k, (wh, wl, xh, xl) in enumerate(parts):
            t = P.pe(mm3(bank(b, n), wh, wl, xh, xl, k == 0, k == len(parts) - 1),
                     *[q[k] for q in by])
        bankfree[b] = [t]
        tick(len(parts) // 2 + 1)
        return t

    def unit8(wh, wl, c0, c1, XHt=None, XLt=None, K=8):
        XHt, XLt = XHt or XH, XLt or XL
        return [(wh[:, k * 128:(k + 1) * 128], wl[:, k * 128:(k + 1) * 128],
                 XHt[:, k, c0:c1], XLt[:, k, c0:c1]) for k in range(K)]

    def act_(out, in_, func, **kw):
        return lambda e: e.activation(out, in_, func, **kw)

    def tt_(out, a, b, op):
        return lambda e: e.tensor_tensor(out, a, b, op)

    def ts_(out, a, s1, s2, op0, op1=ALU.bypass):
        return lambda e: e.tensor_scalar(out, a, s1, s2, op0, op1)

    def stt_(out, a, s1, b, op0, op1):
        return lambda e: e.scalar_tensor_tensor(out, a, s1, b, op0, op1)

    def cp_(out, a):
        return lambda e: e.tensor_copy(out, a)

    def mm_(out, lhsT, rhs, start=True, stop=True, skip=False):
        return lambda e: e.matmul(out, lhsT, rhs, start=start, stop=stop, skip_group_check=skip)

    def tr_(out, in_, n=128):
        return lambda e: e.transpose(out, in_, m("ident")[0:n, 0:n])

    def exp_ln_tables():
        P.act_raw(lambda e: e.preload_act_table_set("natural_log_exp_and_others"))

    tfree = {i: [] for i in range(8)}
    tfree[0] = [tb]

    def stats(src, KT, c0, c1, srctoks, p, dim, factor, busy):
        n = c1 - c0
        bk, rs = 2 + p, 2 + 2 * p
        R, V = TT[rs][:, 0:n], TT[5][:, 0:n]
        busy.add(bk)
        for k in range(KT):
            s = (0, 1, 6)[sq_[0] % 3]
            sq_[0] += 1
            SQ = TT[s][:, 0:n]
            a = P.act(act_(SQ, src(k, c0, c1), ACT.Square), tfree[s], srctoks[k])
            g = P.pe([mm_(bank(bk, n), m("ones"), SQ, k == 0, k == KT - 1, True)],
                     a, bankfree[bk] if k == 0 else None, tc)
            tfree[s] = [g]
            yield
        d = P.dve(ts_(V, bank(bk, n), 1.0 / dim, EPS, ALU.mult, ALU.add), g, tfree[5])
        bankfree[bk] = [d]
        busy.discard(bk)
        a = P.act(act_(R, V, ACT.Ln), d, tfree[rs])
        a = P.act(act_(R, R, ACT.Exp, scale=-0.5), a)
        d = P.dve(tt_(V, R, V, ALU.mult), a)
        d = P.dve(stt_(V, V, -0.5 * factor, R, ALU.mult, ALU.mult), d)
        d = P.dve(stt_(R, V, 1.5 * factor, R, ALU.add, ALU.mult), d)
        tfree[5] = [d]
        tfree[rs] = [d]
        yield d

    sq_ = [0]
    tm_ = [0]
    statbusy = set()

    def tmp_slot(n):
        s = (3, 7)[tm_[0] % 2]
        tm_[0] += 1
        return s, TT[s][:, 0:n]

    def chain(p, dst, srctoks, post, pre, KT=8, dim=D, k0=0):
        rs = 2 + 2 * p
        if post is not None:
            acc, gname, factor, c0, c1 = post
            n = c1 - c0
            R = TT[rs][:, 0:n]
            for tr in stats(acc, KT, c0, c1, srctoks, p, D, factor, statbusy):
                yield
            ready = []
            for k in range(KT):
                s, tmp = tmp_slot(n)
                d = P.dve(stt_(tmp, acc(k, c0, c1), v(gname, k), R, ALU.mult, ALU.mult), tr, tfree[s])
                tfree[rs] = [d]
                yk = RES[:, k, META + c0:META + c1]
                d = (P.pool if k % 2 else P.dve)(tt_(yk, yk, tmp, ALU.add), d, resback[0])
                tfree[s] = [d]
                ready.append([d])
                yield
            srctoks = ready
        src, gname, c0, c1 = pre
        n = c1 - c0
        R = TT[rs][:, 0:n]
        for tr in stats(src, KT, c0, c1, srctoks, p, dim, 1.0, statbusy):
            yield
        for k in range(KT):
            s, tmp = tmp_slot(n)
            d = P.dve(stt_(tmp, src(k, c0, c1), v(gname, k0 + k), R, ALU.mult, ALU.mult), tr, tfree[s], tc)
            tfree[rs] = [d]
            xh, xl = XH[:, k0 + k, c0:c1], XL[:, k0 + k, c0:c1]
            a = P.act(act_(xh, tmp, ACT.Copy), d, xfree_[0])
            q = (P.dve if k % 2 else P.pool)(tt_(xl, tmp, xh, ALU.subtract), a, xfree_[0])
            tfree[s] = [q]
            dst.append([a, q, d])
            yield

    xfree_ = [[]]
    resback = [None]

    def spill(xt):
        xt.all()
        return P.dma("pool", "spill", lambda e: e.dma_start(A["rs"], RES[:, :, :]),
                     [(q, P.n[q]) for q in ("dve", "pool", "act")], ("meta", 16))

    def restore_tile(f, *toks):
        return P.dma("pool", f"back{f}", lambda e: e.dma_start(RES[:, f, :], A["rs"][:, f, :]), *toks)
    LAG = 10

    class KToks(list):
        pass

    class Chains:

        def __init__(self, gens, outs, per=1):
            self.gens, self.outs, self.per = gens, outs, per
            self.steps = [0] * len(gens)
            self.over = [False] * len(gens)
            self.open = len(gens)

        def step(self, i):
            if i >= self.open or (i >= 2 and not self.over[i - 2]) or self.over[i]:
                return False
            try:
                next(self.gens[i])
                self.steps[i] += 1
            except StopIteration:
                self.over[i] = True
            return True

        def advance(self):
            for i in range(len(self.gens)):
                if not self.over[i]:
                    done = self.step(i)
                    if i + 1 < len(self.gens) and self.steps[i] > LAG:
                        self.step(i + 1)
                    return done
            return False

        def __getitem__(self, c):
            last = self.per * (c + 1) - 1
            while not self.over[last]:
                assert self.advance()
            out = KToks()
            for i in range(self.per * c, last + 1):
                out += self.outs[i]
            return out

        def all(self):
            return [self[c] for c in range(len(self.gens) // self.per)]

    background = []

    def tick(n=1):
        for _ in range(n):
            while background and all(background[0].over):
                background.pop(0)
            if background:
                background[0].advance()

    def chains(specs, xfree, per=1, **kw):
        xfree_[0] = xfree
        outs = [[] for _ in specs]
        gens = [chain(i % 2, outs[i], s[0], s[1], s[2], **dict(kw, **(s[3] if len(s) > 3 else {})))
                for i, s in enumerate(specs)]
        c = Chains(gens, outs, per)
        background.append(c)
        return c

    res_src = lambda k, a, b: RES[:, k, META + a:META + b]
    h_src = lambda k, a, b: RES[:, k, a:b]

    def ffn(f, xt, nxt):
        ACC, H_H, H_L = S["acc"], S["hh"], S["hl"]
        T = FFN_CHUNKS
        hfree = {s: [] for s in range(4)}
        hready = {}
        acctok = [[None] * 8, [None] * 8]
        nb = [0]

        def gate_up(j):
            ig, gh, gl, gt = W.get(f"G{f}.{j}")
            iu, uh, ul, ut = W.get(f"U{f}.{j}")
            s = j % 4
            for c, (c0, c1) in enumerate(T):
                b = 2 * ((2 * j + c) % 2)
                tg = group(b, 512, unit8(gh, gl, c0, c1), gt, xt[c])
                tu = group(b + 1, 512, unit8(uh, ul, c0, c1), ut)
                ta, tb_, = (0, 1) if c == 0 else (2, 3)
                ea, eb = TT[ta][:, :], TT[tb_][:, :]
                g_, u_ = bank(b), bank(b + 1)
                hh, hl = H_H[:, s, c0:c1], H_L[:, s, c0:c1]
                d1 = P.act(lambda e, ea=ea, g_=g_: e.activation(ea, g_, ACT.Silu), tg, tfree[ta])
                d2 = P.dve(lambda e, ea=ea, eb=eb, u_=u_: e.tensor_tensor(eb, u_, ea, ALU.mult),
                           d1, tu, tfree[tb_])
                bankfree[b], bankfree[b + 1] = [d1], [d2]
                a = P.act(lambda e, hh=hh, eb=eb: e.activation(hh, eb, ACT.Copy), d2, hfree[s])
                p = P.pool(lambda e, hh=hh, hl=hl, eb=eb: e.tensor_tensor(hl, eb, hh, ALU.subtract), a)
                tfree[ta], tfree[tb_] = [d2], [p]
                hready[j, c] = [a, p]
            W.done(ig, tg)
            W.done(iu, tu)

        def down_group(b, c, ft, un):
            iw, wh, wl, wt = un
            c0, c1 = T[c]
            pb = 4 + nb[0] % 4
            nb[0] += 1
            parts = []
            for k in range(2):
                o = k * 512 + ft % 4 * 128
                s = (2 * b + k) % 4
                parts.append((wh[:, o:o + 128], wl[:, o:o + 128], H_H[:, s, c0:c1], H_L[:, s, c0:c1]))
            t = group(pb, 512, parts, wt, hready[2 * b, c], hready[2 * b + 1, c])
            acc, pp = ACC[:, ft, c0:c1], bank(pb)
            d = P.dve(cp_(acc, pp) if b == 0 else tt_(acc, acc, pp, ALU.add), t)
            bankfree[pb] = [d]
            acctok[c][ft] = [d]
            return t

        def down(b):
            for h in range(2):
                un = W.get(f"D{f}.{b}.{h}")
                for fi in range(4):
                    for c in range(2):
                        t = down_group(b, c, 4 * h + fi, un)
                W.done(un[0], t)
            for k in range(2):
                hfree[(2 * b + k) % 4] = [t]

        for b in range(11):
            gate_up(2 * b)
            if b:
                down(b - 1)
            gate_up(2 * b + 1)
        xdone = ("pe", P.n["pe"])
        un = [W.get(f"D{f}.10.{h}") for h in range(2)]
        for ft in range(8):
            down_group(10, 0, ft, un[ft // 4])
        exp_ln_tables()
        out = nxt(lambda k, a, b: ACC[:, k, a:b], f"ffn{f}_post_g", 0.5, acctok, [xdone])
        out.open = 1
        for ft in range(8):
            t = down_group(10, 1, ft, un[ft // 4])
            if ft == 3:
                W.done(un[0][0], t)
        W.done(un[1][0], t)
        out.open = len(out.gens)
        return out

    def to_first(gpre):
        def make(acc, gpost, factor, acctok, xfree):
            return chains([(acctok[c], (acc, gpost, factor, c0, c1), (res_src, gpre, c0, c1))
                           for c, (c0, c1) in enumerate(FFN_CHUNKS)], xfree)
        return make

    def to_second(acc, gpost, factor, acctok, xfree):
        return chains([(acctok[min(c, 1)], (acc, gpost, factor, max(c0 - META, 0), c1 - META),
                        (h_src, "even_norm_2", c0, c1)) for c, (c0, c1) in enumerate(CHUNKS)], xfree)

    def softplus(out, tmp, src, srctok, tmpfree, outfree):
        d = P.dve(ts_(tmp, src, 40.0, None, ALU.min), srctok, tmpfree)
        a = P.act(act_(tmp, tmp, ACT.Exp), d)
        a = P.act(act_(tmp, tmp, ACT.Ln, bias=1.0), a)
        return P.dve(tt_(out, src, tmp, ALU.max), a, outfree)

    def mixer(xt, nxt):
        M = S["mix"]
        OT, OTM = S["ot"], M["otm"]
        NC8, COS, SIN = M["nc8"], M["cos"], M["sin"]
        PT, PP, SM, LAM = M["pt"], M["p"], M["sm"], M["lam"]
        T = FFN_CHUNKS
        exp_ln_tables()
        tlam = load("sp", "lam", LAM[:, :], A["lam"])
        SUBG = LAM[:, 256:384]
        sm = lambda i, n=1: SM[:, i:i + n]
        d = []
        for i in range(2):
            q, k = LAM[:, 128 * i:128 * i + 64], LAM[:, 128 * i + 64:128 * i + 128]
            d1 = P.dve(lambda e, q=q, k=k, i=i: e.scalar_tensor_tensor(
                q, q, 1.0, k, ALU.mult, ALU.mult, accum_out=sm(i)), tlam)
            d.append(P.act(act_(sm(i), sm(i), ACT.Exp), d1))
        d1 = P.dve(tt_(sm(0), sm(0), sm(1), ALU.subtract), d)
        tnl = P.dve(ts_(sm(0), sm(0), 0.2, -1.0, ALU.add, ALU.mult), d1)
        tsg = P.dve(ts_(SUBG, SUBG, 0.8, None, ALU.mult), tlam)
        NLAM = sm(0)
        i24, wh, wl, wt = W.get("IN.24")
        tg = []
        for c, (c0, c1) in enumerate(T):
            tg.append(group(c, 512, unit8(wh, wl, c0, c1), wt, xt[c]))
        W.done(i24, tg[1])
        z8 = PT[0][0:8, 0:1024]
        e8 = PT[1][0:8, 0:1024]
        fb = v("fox_forget_b")[0:8, :]
        for c, (c0, c1) in enumerate(T):
            d = P.dve(ts_(z8[:, c0:c1], bank(c, 512, 0, 8), fb, -1.0, ALU.add, ALU.mult), tg[c], tc,
                      tfree[6], tfree[7])
            bankfree[c] = [d]
        CT = sm(64, 64)
        dz8 = d
        pfree = [tfree[0] + tfree[1], tfree[2] + tfree[3]]
        otmfree = [None, None]
        smfree = {}
        pend = []
        late_tr = []
        tiles = {}
        last = {}
        tsp = spill(xt)

        def project(t):
            s = t % 2
            QT, KT_, VT, NCB = M["q"][s], M["k"][s], M["vt"][s], M["ncb"][s]
            VR, RT = M["vr"], M["rt"]
            o, u = (0 if t < 4 else 12), t % 4
            free = [last.get(("s", t - 2)), last.get(("v", t - 2)), tsp]
            tl = {}
            if t == 4:
                last["rope"] = load("pool", "rope", M["cs"][:, :, :], A["rope"], ("dve", P.n["dve"]),
                                    last.get(("s", 2)))
            trope = last.get("rope")
            for which, dst, scale in (("q", QT, 0.125), ("k", KT_, 1.0), ("v", VR, 1.0)):
                iw, wh, wl, wt = W.get(f"IN.{o + 4 * 'qkv'.index(which) + u}")
                fr = last.get("vr") if which == "v" else free
                toks = []
                for c, (c0, c1) in enumerate(T):
                    P.wait("pe", [bankfree[7], wt, xt[c]])
                    parts = unit8(wh, wl, c0, c1)
                    for k, (a, b, x, y) in enumerate(parts):
                        tk = P.pe(mm3(bank(7), a, b, x, y, k == 0, k == 7))
                        if k < 7:
                            yield
                    a = P.act(act_(dst[:, c0:c1], bank(7), ACT.Copy, scale=scale), tk, fr, tsp)
                    bankfree[7] = [a]
                    toks.append(a)
                    yield
                W.done(iw, tk)
                if t >= 4 and which != "v":
                    for c, (c0, c1) in enumerate(T):
                        X, tmp = dst[:, c0:c1], RT[:, c0:c1]
                        tr = P.pe([mm_(bank(7), m("rot"), X)], toks[c], bankfree[7])
                        d1 = P.dve(tt_(tmp, bank(7), SIN[:, c0:c1], ALU.mult), tr, trope, tsp)
                        bankfree[7] = [d1]
                        d2 = P.pool(tt_(X, X, COS[:, c0:c1], ALU.mult), toks[c], tr, trope)
                        toks[c] = P.dve(tt_(X, X, tmp, ALU.add), d1, d2)
                        yield
                tl[which] = toks
            for h in range(2):
                tp = P.pe([tr_(PS[:, 3584 + 128 * k:3712 + 128 * k], VR[:, 512 * h + 128 * k:512 * h + 128 * k + 128])
                           for k in range(4)], tl["v"], bankfree[7], tc)
                a = P.act(act_(VT[:, 4 * h:4 * h + 4, :], bank(7).rearrange("p (a b) -> p a b", a=4),
                               ACT.Copy), tp, free)
                bankfree[7] = [a]
                yield
            last["vr"] = tp
            tl["v"] = a
            if t < 4:
                tl["nc"] = []
                for i in range(2):
                    h = 2 * t + i
                    sel = m("ident")[0:8, h:h + 1].to_broadcast([8, 128])
                    for c, (c0, c1) in enumerate(T):
                        tp = P.pe([mm_(bank(7), sel, NC8[0:8, c0:c1])], bankfree[7], dn)
                        dd = P.dve(cp_(NCB[i][:, c0:c1], bank(7)), tp, tsp)
                        bankfree[7] = [dd]
                        tl["nc"].append(dd)
                        yield
            tiles[t] = tl

        def stage_a(n, t, qb, i):
            nk = 128 * (qb + 1)
            pb = n % 2
            b0 = 2 * pb
            QT, KT_, NCB, state = M["q"][t % 2], M["k"][t % 2], M["ncb"][t % 2], tiles[t]
            fns = []
            for c0 in range(0, nk, 512):
                c1 = min(nk, c0 + 512)
                o = PS[:, b0 * 512 + c0:b0 * 512 + c1]
                fns.append(mm_(o, QT[64 * i:64 * i + 64, 128 * qb:128 * qb + 128],
                               KT_[64 * i:64 * i + 64, c0:c1], True, c1 != nk))
            fns.append(mm_(PS[:, b0 * 512 + nk - 128:b0 * 512 + nk], idb[:, :], cmb[:, :], False, True))
            ts = P.pe(fns, state["q"], state["k"], bankfree[b0], bankfree[b0 + 1], tb)
            last["s", t] = ts
            pp = PP[pb][:, 0:nk]
            src = PS[:, b0 * 512:b0 * 512 + nk]
            j = 4 * (n % 4)
            mx, bias, rs, ri = sm(8 + j), sm(9 + j), sm(10 + j), sm(11 + j)
            if t < 4:
                nc_ = NCB[i][:, 0:nk]
                d = P.dve(lambda e, sc=src: e.tensor_tensor_reduce(
                    out=pp, in0=sc, in1=nc_, scale=1.0, scalar=-3e38, op0=ALU.add, op1=ALU.max,
                    accum_out=mx), ts, pfree[pb], state["nc"], smfree.get(n % 4))
                bankfree[b0] = bankfree[b0 + 1] = [d]
                src = pp
                c = CT[:, 8 * qb + 2 * t + i:8 * qb + 2 * t + i + 1]
                d = P.dve(tt_(mx, mx, c, ALU.subtract), d, dct)
                db = P.dve(stt_(bias, mx, -1.0, c, ALU.mult, ALU.subtract), d)
            else:
                d = P.dve(lambda e: e.tensor_reduce(mx, src, AX.X, ALU.max), ts, smfree.get(n % 4))
                db = P.dve(ts_(bias, mx, -1.0, None, ALU.mult), d)
            a = P.act(act_(pp, src, ACT.Exp, bias=bias, accum_out=rs), db, pfree[pb])
            if t >= 4:
                bankfree[b0] = bankfree[b0 + 1] = [a]
            dr = P.dve(lambda e: e.reciprocal(ri, rs), a)
            return a, dr

        def stage_b(n, t, qb, i, ta):
            nk = 128 * (qb + 1)
            pb = n % 2
            fns = [tr_(PS[:, 2048 + 128 * k:2176 + 128 * k], PP[pb][:, 128 * k:128 * k + 128])
                   for k in range(qb + 1)]
            tp = P.pe(fns, ta, bankfree[4], bankfree[5], tc)
            pfree[pb] = [tp]
            s = n % 2
            dst, src = PT[s][:, 0:nk], PS[:, 2048:2048 + nk]
            te = P.act(act_(dst, src, ACT.Copy), tp, ptfree[s]) if n % 2 else \
                P.dve(cp_(dst, src), tp, ptfree[s])
            bankfree[4] = bankfree[5] = [te]
            return te

        def stage_c(n, t, qb, i, te, dr):
            s = n % 2
            w = 64 if t < 4 else 128
            o = i * 64 if t < 4 else 0
            out = PS[:, 3072:3072 + w]
            VT, OT2 = M["vt"][t % 2], OTM[n // 2 % 2]
            fns = [mm_(out, PT[s][:, 128 * k:128 * k + 128], VT[:, k, o:o + w], k == 0, k == qb)
                   for k in range(qb + 1)]
            tp = P.pe(fns, te, bankfree[6], tiles[t]["v"])
            ptfree[s] = [tp]
            last["v", t] = tp
            j = 4 * (n % 4)
            rs, ri = sm(10 + j), sm(11 + j)
            of = otmfree[n // 2 % 2]
            if t < 4:
                d = P.dve(ts_(OT2[:, o:o + w], out, ri, None, ALU.mult), tp, dr, of)
            elif i == 0:
                d = P.dve(ts_(OT2[:, :], out, ri, None, ALU.mult), tp, dr, of)
                last["o1"] = d
            else:
                d = P.dve(tt_(ri, ri, NLAM, ALU.mult), dr, tnl)
                d = P.dve(stt_(OT2[:, :], out, ri, OT2[:, :], ALU.mult, ALU.add), tp, d, last["o1"])
            bankfree[6] = [d]
            smfree[n % 4] = [d]
            if i == 0:
                return
            if t >= 4:
                x, y, z, sq = sm(28), sm(29), sm(30), M["sq"]
                d = P.dve(lambda e: e.scalar_tensor_tensor(sq, OT2[:, :], 1.0, OT2[:, :], ALU.mult,
                                                           ALU.mult, accum_out=x), d)
                d = P.dve(ts_(x, x, 1.0 / 128, EPS, ALU.mult, ALU.add), d)
                a = P.act(act_(y, x, ACT.Ln), d)
                a = P.act(act_(y, y, ACT.Exp, scale=-0.5), a)
                d = P.dve(tt_(z, y, y, ALU.mult), a)
                d = P.dve(tt_(z, z, x, ALU.mult), d)
                d = P.dve(ts_(z, z, -0.5, 1.5, ALU.mult, ALU.add), d)
                d = P.dve(tt_(y, y, z, ALU.mult), d)
                d = P.dve(stt_(OT2[:, :], OT2[:, :], y, SUBG, ALU.mult, ALU.mult), d, tsg)
            late_tr.append((n, t, qb, d))

        def stage_d(n, t, qb, d):
            OT2 = OTM[n // 2 % 2]
            tp = P.pe([tr_(PS[:, 3328:3456], OT2[:, :])], d, bankfree[6], tc)
            otmfree[n // 2 % 2] = tp
            a = P.act(act_(OT[:, t, 128 * qb:128 * qb + 128], PS[:, 3328:3456], ACT.Copy), tp)
            bankfree[6] = bankfree[6] + [a]
            last["ot"] = a

        fill = [None]

        def work(n):
            for _ in range(n):
                if fill[0] is not None and next(fill[0], "end") == "end":
                    fill[0] = None

        def step(item, w=0):
            tr = late_tr[:]
            del late_tr[:]
            late = [p for p in pend if p[3] is not None]
            todo = [p for p in pend if p[3] is None][:1]
            front = item is not None and item[1] < 4
            for back in (not front, front):
                if back:
                    for p in todo:
                        p[3] = stage_b(*p[0], p[1])
                else:
                    if item is not None:
                        ta, dr = stage_a(*item)
                        pend.append([item, ta, dr, None])
                    for x in tr:
                        stage_d(*x)
                work(w // 2)
            for p in late[:1]:
                stage_c(*p[0], p[3], p[2])
                pend.remove(p)

        first = project(0)
        for _ in range(16):
            next(first)
        d = softplus(z8, e8, z8, dz8, tfree[4] + tfree[5], None)
        dz = P.dve(lambda e: e.memset(e8, 0.0), d)
        dn = P.dve(lambda e: e.tensor_tensor_scan(NC8[0:8, :], z8, e8, 0.0, ALU.add, ALU.add), dz, d)
        ptfree = [[dn], [dn]]
        for _ in range(32):
            next(first)
        tct = P.pe([mm_(PS[:, 8 * b:8 * b + 8], NC8[0:8, 128 * b:128 * b + 128], m("ident")[0:8, 0:8])
                    for b in range(8)], dn, bankfree[0])
        dct = P.dve(cp_(CT, PS[:, 0:64]), tct)
        bankfree[0] = [dct]
        for _ in first:
            pass
        n = 0
        for t in range(8):
            fill[0] = project(t + 1) if t < 7 else None
            for qb in range(8):
                for i in range(2):
                    step((n, t, qb, i), 4)
                    n += 1
            work(1000)
        xdone = [("pe", P.n["pe"])]
        while pend or late_tr:
            step(None)
        aend = [(q, P.n[q]) for q in ("pe", "dve", "act", "pool")]
        resback[0] = [restore_tile(f, aend) for f in range(8)]
        state = {"ot": last["ot"]}
        tfree[0] = tfree[1] = list(pfree[0])
        tfree[2] = tfree[3] = list(pfree[1])
        tfree[6] = tfree[7] = list(ptfree[0])
        tfree[4] = tfree[5] = list(ptfree[1])
        toks = []
        for k in range(8):
            for c, (c0, c1) in enumerate(T):
                x, xh, xl = OT[:, k, c0:c1], XH[:, k, c0:c1], XL[:, k, c0:c1]
                a = P.act(act_(xh, x, ACT.Copy), state["ot"], xdone)
                p = P.dve(tt_(xl, x, xh, ALU.subtract), a)
                toks.append([a, p])
        osplit = toks[-1]
        by_c = [KToks(toks[c::2]) for c in range(2)]
        acctok = [[None] * 8, [None] * 8]
        S_acc = S["acc"]
        out = nxt(lambda k, a, b: S_acc[:, k, a:b], "mix_post_g", 1.0, acctok, None)
        out.open = 0
        for f in range(8):
            iw, wh, wl, wt = W.get(f"OUT.{f}")
            for c, (c0, c1) in enumerate(T):
                b = (2 * f + c) % 8
                t = group(b, 512, unit8(wh, wl, c0, c1), wt, by_c[c])
                d = P.dve(cp_(S_acc[:, f, c0:c1], bank(b)), t, osplit)
                bankfree[b] = [d]
                acctok[c][f] = [d]
                if f == 7:
                    xfree_[0] = [t]
                    out.open = c + 1
            W.done(iw, t)
        return out

    def evac3(unit, fn, xt, b0, *toks):
        iw, wh, wl, wt = W.get(unit)
        for c, (c0, c1) in enumerate(CHUNKS):
            b = b0 + c
            t = group(b, c1 - c0, unit8(wh, wl, c0, c1), wt, xt[c], *toks)
            bankfree[b] = [fn(c, c0, c1, bank(b, c1 - c0), t)]
        W.done(iw, t)

    def conv4(out, x, wname, nw, bname, tile, srctoks, free):
        d = P.dve(ts_(out, x[:, 0:T2], v(wname, tile), v(bname, tile), ALU.mult, ALU.add), srctoks, free)
        for k in range(1, 4):
            d = P.dve(stt_(out, x[:, k:k + T2], v(wname, nw * k + tile), out, ALU.mult, ALU.add), d)
        return d

    def even(xt):
        V = S["lru"]
        XIN, U, TB = V["xin"], V["u"], V["tb"]
        UH, UL, YH, YL = S["uh"], S["ul"], S["yh"], S["yl"]
        W.eager = True
        pe0 = [("pe", P.n["pe"])]
        sm = V["sm"]
        AC, N8 = sm[:, 32:40], sm[:, 40:48]

        def decay(lru_t):
            L, E1, Z, Z2, AC, N8 = [sm[:, 8 * i:8 * i + 8] for i in range(6)]
            lam = vec[:, VEC["lru_lambda_2"]:VEC["lru_lambda_2"] + 8]
            d = P.dve(ts_(L, lam, -1.0, None, ALU.mult), tc, lru_t)
            d = P.dve(tt_(E1, L, lam, ALU.min), d)
            a = P.act(act_(E1, E1, ACT.Exp), d)
            d = P.dve(ts_(Z, E1, 2.0, None, ALU.add), a)
            d = P.dve(lambda e: e.reciprocal(Z, Z), d)
            d = P.dve(tt_(Z, Z, E1, ALU.mult), d)
            d = P.dve(tt_(Z2, Z, Z, ALU.mult), d)
            d = P.dve(ts_(AC, Z2, 1.0 / 17, 1.0 / 15, ALU.mult, ALU.add), d)
            for q in (13, 11, 9, 7, 5, 3, 1):
                d = P.dve(tt_(AC, AC, Z2, ALU.mult), d)
                d = P.dve(ts_(AC, AC, 1.0 / q, None, ALU.add), d)
            d = P.dve(tt_(AC, AC, Z, ALU.mult), d)
            d = P.dve(ts_(L, L, 0.0, 8.0, ALU.max, ALU.mult), d)
            d = P.dve(stt_(AC, AC, 16.0, L, ALU.mult, ALU.add), d)
            ts8 = P.dve(ts_(N8, AC, -1.0, None, ALU.mult), d)
            return ts8
        S8 = AC
        ts8 = None
        tz = [P.pool(lambda e: e.memset(XIN[0][:, 0:3], 0.0), pe0), None]
        tms = []
        restok = None
        gfree = {0: [], 1: []}
        R_, I_, A_, L_ = TB
        xinfree, ufree = [[], []], [[], []]
        uhfree, yfree = [], []
        tbfree = {0: [], 1: [], 2: [], 3: []}
        ynb = [0]
        uts, lw, sts, yts, ends = {}, {}, {}, {}, []
        G = [V["g"], XIN[0][:, 3:3 + T2]]

        def conv_in(g):
            nonlocal ts8, restok, tbfree
            uts[g] = []
            for ti in range(2):
                tile = 2 * g + ti
                toks = []

                def to_xin(c, c0, c1, b, t):
                    a = P.act(act_(XIN[ti][:, 3 + c0:3 + c1], b, ACT.Copy), t, xinfree[ti], tz[ti])
                    toks.append(a)
                    return a
                if ti and ts8 is None:
                    xt.all()
                    lru_t = [tfree[i] for i in range(8)]
                    tz[1] = P.pool(lambda e: e.memset(XIN[1][:, 0:3], 0.0), lru_t)
                    restok = [("dve", P.n["dve"]), ("pool", P.n["pool"])]
                    tms.append(load("act", "mat2", S["mat2"][:, :], A["mat2"], restok))
                    tbfree = {i: [lru_t] for i in range(4)}
                    gfree[0] = [lru_t]
                    ts8 = decay(lru_t)
                evac3(f"E.{tile}", to_xin, xt, 3 * ti)
                d = conv4(U[ti], XIN[ti], "lru_conv_w_2", 8, "lru_conv_b_2", tile, toks, ufree[ti])
                xinfree[ti] = [d]
                if ti == 0:
                    gfree[1] = [d]
                a = P.act(act_(UH[:, ti, :], U[ti], ACT.Copy), d, uhfree)
                p = P.pool(tt_(UL[:, ti, :], U[ti], UH[:, ti, :], ALU.subtract), a)
                uts[g] += [a, p]

        def gate(g, tj):
            toks = []
            G_ = G[tj]

            def to_g(c, c0, c1, b, t):
                a = P.act(act_(G_[:, c0:c1], b, ACT.Sigmoid), t, gfree[tj])
                d = P.dve(tt_(G_[:, c0:c1], b, G_[:, c0:c1], ALU.mult), a)
                toks.append(d)
                return d
            evac3(f"E.{8 + 2 * g + tj}", to_g, xt, 0)
            sts[tj] = toks

        def recur(g, tj):
            tile = 2 * g + tj
            if tj == 0:
                lw[g] = W.get(f"L.{g}")
            il, lh, ll, lt = lw[g]
            st = {0: [], 1: []}
            for which, dst, bname in ((0, R_, "lru_b_a_2"), (1, I_, "lru_b_x_2")):
                for c, (c0, c1) in enumerate(CHUNKS):
                    b = 3 * (1 - which) + c
                    parts = []
                    for ki in range(2):
                        o = which * 512 + ki * 256 + tj * 128
                        parts.append((lh[:, o:o + 128], ll[:, o:o + 128],
                                      UH[:, ki, c0:c1], UL[:, ki, c0:c1]))
                    t = group(b, c1 - c0, parts, lt, uts[g])
                    a = P.act(act_(dst[:, c0:c1], bank(b, c1 - c0), ACT.Sigmoid,
                                   bias=v(bname, tile)), t, tbfree[which])
                    bankfree[b] = [a]
                    st[which].append(a)
            uhfree[:] = [t]
            if tj == 1:
                W.done(il, t)
            s8, n8 = S8[:, tile:tile + 1], N8[:, tile:tile + 1]
            at = P.act(act_(L_, R_, ACT.Tanh, scale=s8), st[0], ts8, tbfree[3])
            exp_ln_tables()
            aa = P.act(act_(A_, R_, ACT.Exp, scale=n8), ts8, tbfree[2])
            d = P.dve(ts_(L_, L_, 1e-18, None, ALU.max), at)
            a1 = P.act(act_(R_, L_, ACT.Ln, scale=2.0), d, aa)
            a2 = P.act(act_(L_, L_, ACT.Ln, bias=1.0), a1)
            d = P.dve(tt_(R_, R_, L_, ALU.subtract), a1, a2)
            a3 = P.act(act_(R_, R_, ACT.Exp, scale=0.5), d)
            d = P.pool(tt_(I_, I_, U[tj], ALU.mult), st[1], uts[g])
            ufree[tj] = [d]
            d = P.dve(tt_(I_, I_, R_, ALU.mult), d, a3)
            tbfree[0] = [d]
            d = P.dve(lambda e: e.tensor_tensor_scan(L_, A_, I_, 0.0, ALU.mult, ALU.add), d, aa)
            tbfree[1] = tbfree[2] = [d]
            d = P.dve(tt_(L_, L_, G[tj], ALU.mult), d, sts[tj])
            gfree[tj] = [d]
            if tj:
                xinfree[0] = [d]
            a = P.act(act_(YH[:, tj, :], L_, ACT.Copy), d, yfree)
            p = P.pool(tt_(YL[:, tj, :], L_, YH[:, tj, :], ALU.subtract), a)
            tbfree[3] = [p]
            yts.setdefault(g, []).extend([a, p])

        def out_rows(g):
            nonlocal yfree
            for hh in range(2):
                iw, wh, wl, wt = W.get(f"EO.{g}.{hh}")
                for fi in range(4):
                    f = 4 * hh + fi
                    for c, (c0, c1) in enumerate(CHUNKS):
                        b = 6 + ynb[0] % 2
                        ynb[0] += 1
                        parts = [(wh[:, k * 512 + fi * 128:k * 512 + fi * 128 + 128],
                                  wl[:, k * 512 + fi * 128:k * 512 + fi * 128 + 128],
                                  YH[:, k, c0:c1], YL[:, k, c0:c1]) for k in range(2)]
                        t = group(b, c1 - c0, parts, wt, yts[g])
                        r = RES[:, f, c0:c1]
                        d = P.dve(tt_(r, r, bank(b, c1 - c0), ALU.add), t, restok)
                        bankfree[b] = [d]
                W.done(iw, t)
            yfree = [t]
            ends[:] = [d, t]

        for g in range(4):
            conv_in(g)
            if g:
                out_rows(g - 1)
            gate(g, 0)
            recur(g, 0)
            gate(g, 1)
            recur(g, 1)
        zb = [0]

        def z_unit(k, bufs, b0):
            def to_z(c, c0, c1, b, t):
                s = zb[0] % 2
                zb[0] += 1
                z = bufs[s][:, 0:c1 - c0]
                a = P.act(act_(z, b, ACT.Silu), t, zfree[s])
                zfree[s] = [load("pool", f"zs{s}", A["zs"][k][:, c0:c1], z, a)]
                return a
            evac3(f"E.{16 + k}", to_z, xt, b0)

        zfree = [[], []]
        z_unit(0, V["zb"], 3)
        z_unit(1, V["zb"], 0)
        zfree0 = zfree[0] + zfree[1]
        out_rows(3)
        d, t = ends
        a, p = yts[3][-2:]
        tm2 = tms[0]
        lru_end = [d, t, a, p, zfree0, ("pool", P.n["pool"]), ("act", P.n["act"])]
        tsp = P.dma("pool", "spill", lambda e: e.dma_start(A["rs"], RES[:, :, :]), d)
        V = S["ssd"]
        X, BC, BT, DT = V["x"], V["bc"], V["bt"], V["dt"]
        ZB = V["zb"]
        XINs, CVs = [V["xin"], V["xin2"]], [V["cv"], V["cv2"]]
        tz = [P.pool(lambda e: e.memset(XINs[0][:, 0:3], 0.0), lru_end),
              P.pool(lambda e: e.memset(XINs[1][:, 0:3], 0.0), lru_end, tsp)]
        cvfree, xinfree = [list(lru_end), [tsp]], [list(lru_end), [tsp]]
        nblk = 9
        blk = [(128 * c, min(128, T2 - 128 * c)) for c in range(nblk)]
        xtok = None
        held = []

        def flush():
            nonlocal xtok
            k, src, a = held.pop(0)
            for part in range(3):
                bs = blk[4 * part:4 * part + 4]
                b = 6 + part % 2
                t = P.pe([tr_(PS[0:n, b * 512 + 128 * j:b * 512 + 128 * j + 128], src[:, t0:t0 + n])
                          for j, (t0, n) in enumerate(bs)], a, bankfree[b], tc)
                n = bs[0][1]
                o = BT[0:n, 4 * part:4 * part + len(bs), (k - 8) * 128:(k - 7) * 128] if k >= 8 else \
                    X[0:n, 4 * part:4 * part + len(bs), k * 128:(k + 1) * 128]
                i_ = PS[0:n, b * 512:b * 512 + 128 * len(bs)].rearrange("p (a b) -> p a b", a=len(bs))
                xtok = P.dve(cp_(o, i_), t, lru_end)
                bankfree[b] = [xtok]
            if k < 8:
                cvfree[k % 2] = [t]

        zfree = [[tsp], [tsp]]
        zat = {3: 2, 5: 3, 7: 4, 9: 5, 10: 6, 11: 7}
        for k in range(12):
            toks = []
            X_, C_ = XINs[k % 2], CVs[k % 2]

            def to_x(c, c0, c1, b, t):
                a = P.act(act_(X_[:, 3 + c0:3 + c1], b, ACT.Copy), t, xinfree[k % 2], tz[k % 2])
                toks.append(a)
                return a
            evac3(f"E.{24 + k}", to_x, xt, 0)
            if held:
                flush()
            d = conv4(C_, X_, "ssd_conv_w_2", 12, "ssd_conv_b_2", k, toks, cvfree[k % 2])
            xinfree[k % 2] = [d]
            dst = C_ if k < 8 else BC[:, k - 8, :]
            a = P.act(act_(dst, C_, ACT.Silu), d, lru_end)
            cvfree[k % 2] = [a]
            if k in zat:
                z_unit(zat[k], ZB, 3)
            if k < 10:
                held.append((k, dst, a))
        while held:
            flush()
        zdone = zfree[0] + zfree[1]
        xinfree, cvfree = xinfree[0], cvfree[0] + cvfree[1]
        bctok = a
        exp_ln_tables()
        dtf = XINs[0][0:16, 0:T2]
        db = v("ssd_dt_bias_2")[0:16, :]
        toks = []

        def to_dt(c, c0, c1, b, t):
            d = P.dve(ts_(dtf[:, c0:c1], b[0:16, :], db, None, ALU.add), t, xinfree)
            toks.append(d)
            return d
        evac3("E.36", to_dt, xt, 0)
        xdone = [("pe", P.n["pe"])]
        d = toks
        t = P.pe([mm_(PS[0:n, 1536 + 16 * c:1552 + 16 * c], dtf[:, t0:t0 + n], m("ident")[0:16, 0:16])
                  for c, (t0, n) in enumerate(blk)], d, bankfree[3])
        dz = P.dve(lambda e: e.memset(DT[:, 8, :], 0.0), lru_end)
        DX, DE, DW, DR = [S["scan"]["y"][0][:, 144 * i:144 * i + 144] for i in range(4)]
        dx = P.dve(lambda e: e.memset(DX, 0.0), xdone)
        dx = P.dve(cp_(DX[:, 0:128], PS[:, 1536:1664]), t, dx)
        dx = P.dve(cp_(DX[0:16, 128:144], PS[0:16, 1664:1680]), t, dx)
        bankfree[3] = [dx]
        d = P.dve(ts_(DE, DX, 40.0, None, ALU.min), dx)
        a = P.act(act_(DE, DE, ACT.Exp), d)
        d = P.dve(ts_(DW, DE, 1.0, None, ALU.add), a)
        a = P.act(act_(DR, DW, ACT.Ln), d)
        d = P.dve(ts_(DW, DW, -1.0, 1e-30, ALU.add, ALU.max), a)
        d = P.dve(lambda e: e.reciprocal(DW, DW), d)
        d = P.dve(tt_(DR, DR, DW, ALU.mult), d)
        d = P.dve(tt_(DR, DR, DE, ALU.mult), d)
        d = P.dve(ts_(DW, DE, -1.0, 1.0, ALU.mult, ALU.add), d)
        d = P.dve(tt_(DW, DW, DE, ALU.mult), d)
        d = P.dve(tt_(DR, DR, DW, ALU.max), d)
        d = P.dve(tt_(DR, DR, DX, ALU.max), d)
        dd = [P.dve(cp_(DT[:, 0:8, :], DR[:, 0:128].rearrange("p (a b) -> p a b", a=8)), d, lru_end),
              P.dve(cp_(DT[0:16, 8, :], DR[0:16, 128:144]), d, dz)]
        dtt = dd[1]
        Q = S["scan"]
        ANEG = Q["aneg"]
        a = P.act(act_(ANEG, vec[:, VEC["ssd_a_log_2"]:VEC["ssd_a_log_2"] + 16], ACT.Exp), xdone)
        ta = P.dve(ts_(ANEG, ANEG, -1.0, None, ALU.mult), a)
        AD, EX, DDT = Q["ad"], Q["ex"], Q["ddt"]
        DTf = V["dt"].rearrange("p a b -> p (a b)")
        tad = P.dve(tt_(AD.rearrange("p (a b) -> p a b", a=9), DT[:, :, :],
                        ANEG.unsqueeze(1).to_broadcast([128, 9, 16]), ALU.mult), ta, dtt)
        t = P.pe([mm_(PS[:, 0:144], m("triu"), AD), mm_(PS[:, 144:288], m("low"), AD),
                  mm_(PS[:, 288:432], m("ones"), AD)], tad, bankfree[0], tm2)
        tex = P.act(act_(EX, PS[:, 0:432], ACT.Exp), t)
        bankfree[0] = [tex]
        tddt = P.dve(tt_(DDT, DTf, EX[:, 144:288], ALU.mult), tex)
        DD = vec[:, VEC["ssd_d_2"]:VEC["ssd_d_2"] + 16]
        ST = Q["state"]
        YT = RES
        sttok = [None, None]
        stread = [None, None]
        fr = {}

        def bc3(ap, w):
            p, h = ap.shape
            return ap.unsqueeze(2).to_broadcast([p, h, w])

        def bh(ap, h):
            p, w = ap.shape
            return ap.unsqueeze(1).to_broadcast([p, h, w])

        def r3(ap, h):
            return ap.rearrange("p (a b) -> p a b", a=h)

        ytok = None

        def front(c, g):
            t0, n = blk[c]
            GT, M_, CBM, XD, XS, TX = (Q[q][g] for q in ("gt", "m", "cbm", "xd", "xs", "tx"))
            hs, ha = slice(8 * g, 8 * g + 8), slice(16 * c + 8 * g, 16 * c + 8 * g + 8)
            xg = r3(X[0:n, c, 512 * g:512 * g + 512], 8)
            gt3 = r3(GT[0:n, 0:8 * n], 8)
            p = P.pool(tt_(gt3, bh(m("triu")[0:n, 0:n], 8), bc3(AD[0:n, ha], n), ALU.mult),
                       tad, fr.get(("gt", g)), tm2)
            w = 4 * n
            tcb = P.pe([mm_(PS[0:n, 64:64 + n], BC[:, g, t0:t0 + n], BC[:, 2 + g, t0:t0 + n])],
                       bctok, bankfree[0])
            dc = P.dve(tt_(CBM[0:n, 0:n], PS[0:n, 64:64 + n], m("triu")[0:n, 0:n], ALU.mult),
                       tcb, fr.get(("cbm", g)), tm2)
            bankfree[0] = bankfree[0] + [dc]
            t = P.pe([mm_(PS[0:n, 512:512 + w], m("low")[0:n, 0:n], GT[0:n, 0:w]),
                      mm_(PS[0:n, 1024:1024 + w], m("low")[0:n, 0:n], GT[0:n, w:2 * w])],
                     p, bankfree[1], bankfree[2])
            fr[("gt", g)] = [t]
            a = None
            for q in range(2):
                a = P.act(act_(M_[0:n, q * w:q * w + w], PS[0:n, 512 + 512 * q:512 + 512 * q + w], ACT.Exp),
                          t, fr.get(("m", g)))
            bankfree[1] = bankfree[2] = [a]
            ps_ = P.pool(tt_(r3(XS[0:n, :], 8), xg, bc3(DT[0:n, c, hs], 64), ALU.mult),
                         xtok, dtt, fr.get(("xs", g)))
            pd_ = P.pool(tt_(r3(XD[0:n, :], 8), xg, bc3(DDT[0:n, ha], 64), ALU.mult),
                         tddt, fr.get(("xd", g)))
            px_ = P.pool(tt_(r3(TX[0:n, :], 8), xg, bc3(DD[0:n, hs], 64), ALU.mult),
                         fr.get(("tx", g)))
            m3 = r3(M_[0:n, 0:8 * n], 8)
            dm = P.dve(tt_(m3, m3, bh(CBM[0:n, 0:n], 8), ALU.mult), a, dc)
            fr[("cbm", g)] = [dm]
            if g:
                fr["x", c] = [px_]
            return ps_, pd_, px_, dm

        def back_(c, g, toks):
            nonlocal ytok
            ps_, pd_, px_, dm = toks
            t0, n = blk[c]
            s2 = c % 2
            Y = Q["y"][s2]
            M_, XD, XS, TX = (Q[q][g] for q in ("m", "xd", "xs", "tx"))
            hs = slice(8 * g, 8 * g + 8)
            e0, e2 = 16 * c + 8 * g, 288 + 16 * c + 8 * g
            if c:
                to = P.pe([mm_(PS[0:n, 2048:2560], BC[:, 2 + g, t0:t0 + n], ST[g])],
                          sttok[g], bankfree[4])
            ty = P.pe([mm_(PS[0:n, 1536 + 64 * h:1600 + 64 * h], M_[0:n, h * n:h * n + n],
                           XS[0:n, 64 * h:64 * h + 64]) for h in range(8)], dm, ps_, bankfree[3])
            fr[("m", g)] = [ty]
            fr[("xs", g)] = [ty]
            if c < nblk - 1:
                tb_ = P.pe([mm_(PS[:, 2560:3072], BT[0:n, c, 128 * g:128 * g + 128], XD[0:n, :])],
                           pd_, xtok, bankfree[5])
                fr[("xd", g)] = [tb_]
                if c:
                    d = P.dve(tt_(r3(ST[g], 8), r3(ST[g], 8), bc3(EX[:, e2:e2 + 8], 64),
                                  ALU.mult), to, tex, sttok[g])
                    d = P.dve(tt_(ST[g], ST[g], PS[:, 2560:3072], ALU.add), d, tb_)
                else:
                    d = P.dve(cp_(ST[g], PS[:, 2560:3072]), tb_, xdone)
                bankfree[5] = [d]
                sttok[g] = d
            yv = Y[0:n, 512 * g:512 * g + 512]
            if c:
                d = P.dve(tt_(r3(yv, 8), r3(PS[0:n, 2048:2560], 8), bc3(EX[0:n, e0:e0 + 8], 64), ALU.mult),
                          to, tex, fr.get(("y", s2)))
                bankfree[4] = [d]
                d = P.dve(tt_(yv, yv, PS[0:n, 1536:2048], ALU.add), ty, d)
                bankfree[3] = [d]
                d = P.dve(tt_(yv, yv, TX[0:n, :], ALU.add), px_, d)
            else:
                d = P.dve(tt_(yv, TX[0:n, :], PS[0:n, 1536:2048], ALU.add), ty, px_, fr.get(("y", s2)))
                bankfree[3] = [d]
            fr[("tx", g)] = [d]
            if g == 0:
                fr["y0"] = d
                return
            late.append((c, [d, fr["y0"]]))

        def turn(c, ydone):
            nonlocal ytok
            t0, n = blk[c]
            Y = Q["y"][c % 2]
            for half in range(2):
                b = 6 + half
                t = P.pe([tr_(PS[:, b * 512 + 128 * j:b * 512 + 128 * j + n],
                              Y[0:n, 512 * half + 128 * j:512 * half + 128 * j + 128], n) for j in range(4)],
                         ydone, bankfree[b], tc)
                src = PS[:, b * 512:b * 512 + 512].rearrange("p (a b) -> p a b", a=4)[:, :, 0:n]
                ytok = P.act(act_(YT[:, 4 * half:4 * half + 4, t0:t0 + n], src, ACT.Copy), t, tsp, zdone, xtok)
                bankfree[b] = [ytok]
            fr[("y", c % 2)] = [t]

        zin, tz_ = V["zin"], []

        def zload(k):
            tz_.append(load("sp", f"zin{k}", zin[k], A["zs"][k], zdone, fr["x", k], fr["x", k + 1]))

        late = []
        order_ = [(c, g) for c in range(nblk) for g in range(2)]
        prev = None
        for item in order_ + [None]:
            now = (item, front(*item)) if item else None
            if item and item[1] and item[0]:
                zload(item[0] - 1)
            if late:
                turn(*late.pop(0))
            if prev:
                back_(*prev[0], prev[1])
            prev = now
        turn(*late.pop(0))
        scan_end = [("pe", P.n["pe"]), ("dve", P.n["dve"]), ("pool", P.n["pool"]), ("act", P.n["act"])]
        for i in range(8):
            tfree[i] = list(scan_end)
        exp_ln_tables()
        gt = []
        for k in range(8):
            gt.append((P.pool if k % 3 == 2 else P.dve)(tt_(YT[:, k, :], YT[:, k, :], zin[k], ALU.mult),
                                                        tz_[k], ytok))
        specs = []
        for c0, c1 in CHUNKS:
            for grp in range(2):
                specs.append((gt[4 * grp:4 * grp + 4], None,
                              (lambda k, a, b, grp=grp: YT[:, 4 * grp + k, a:b], "ssd_norm_2", c0, c1),
                              dict(k0=4 * grp)))
        yn = chains(specs, scan_end, per=2, KT=4, dim=512)
        back = {}

        def restore(f):
            if not back:
                y2 = yn[2]
                for k in range(8):
                    back[k] = P.dma("pool", f"back{k}", lambda e, k=k: e.dma_start(RES[:, k, :], A["rs"][:, k, :]),
                                    y2[k], tsp)
            return back[f]
        out = add_gemm("EB", yn, restore, "odd_norm_2")
        W.eager = False
        return out

    def add_gemm(prefix, yn, restok, gname):
        nb = 0
        toks = [[None] * 8 for _ in CHUNKS]
        late = {}
        if gname:
            out = chains([(toks[c], None, (h_src, gname, c0, c1)) for c, (c0, c1) in enumerate(CHUNKS)], None)
            out.open = 0
        for f in range(8):
            iw, wh, wl, wt = W.get(f"{prefix}.{f}")
            for c, (c0, c1) in enumerate(CHUNKS):
                b = nb % 8
                nb += 1
                t = group(b, c1 - c0, unit8(wh, wl, c0, c1), wt, yn[c])
                late[c] = (b, t)
                if c < 2 and restok is not None and f == 0:
                    continue
                for cc, (bb, tt) in sorted(late.items()):
                    r = RES[:, f, CHUNKS[cc][0]:CHUNKS[cc][1]]
                    d = P.dve(tt_(r, r, bank(bb, CHUNKS[cc][1] - CHUNKS[cc][0]), ALU.add), tt,
                              restok(f) if restok else None)
                    bankfree[bb] = [d]
                    toks[cc][f] = [d]
                late = {}
                if f == 7 and gname:
                    xfree_[0] = [t]
                    out.open = c + 1
            W.done(iw, t)
        return out if gname else toks

    def odd(xt):
        V = S["odd"]
        OT, VR, GB = V["ot"], V["vr"], V["gb"]
        SPB, EB_, WB, AB = V["sp"], V["e"], V["w"], V["acc"]
        blk = [(128 * c, min(128, T2 - 128 * c)) for c in range(9)]
        pe0 = [("pe", P.n["pe"])]
        gdone = None
        for k in range(8):
            toks = []
            dst = (VR, V["q"][0])[k % 2]

            def to_g(c, c0, c1, b, t):
                a = P.act(act_(dst[:, c0:c1], b, ACT.Silu), t, pe0 if k < 2 else gst[k % 2])
                toks.append(a)
                return a
            if k == 0:
                gst = [None, None]
            evac3(f"Q.{24 + k}", to_g, xt, 3 * (k % 2))
            gdone = P.dma("pool", f"gs{k % 2}", lambda e, k=k, dst=dst: e.dma_start(A["gs"][k], dst), toks)
            gst[k % 2] = [gdone]
        exp_ln_tables()
        tsp = spill(xt)
        SPH, SPL, NTRI = V["sph"], V["spl"], V["ntri"]
        tconst = P.dve(cp_(NTRI[:, :], m("ntri")), tsp)
        state = {}
        free = {("sph", s): [tsp] for s in range(4)}
        free.update({("acc", s): [tsp] for s in range(4)})
        pend = []
        last = {"vr": gst[0], ("z", -2): gst[1]}
        tiles = {}

        def stage_a(it):
            n, t, i, ci, kb, top = it
            c0, c1 = CHUNKS[ci]
            s0, ks = blk[kb]
            a0 = max(c0, s0)
            x0, x1 = a0 - c0, c1 - c0
            b = n % 4
            Q_, K_ = V["q"][t % 2], V["k"][t % 2]
            out = PS[0:ks, b * 512 + x0:b * 512 + x1]
            fns = [mm_(out, K_[64 * i:64 * i + 64, s0:s0 + ks], Q_[64 * i:64 * i + 64, a0:c1],
                       True, False, True)]
            e1 = min(c1, s0 + 128)
            if s0 < c1 and e1 > a0:
                fns.append(mm_(PS[0:ks, b * 512 + x0:b * 512 + e1 - c0], idb[0:ks, 0:ks],
                               smb[0:ks, a0 - s0:e1 - s0], False, False, True))
            tp = P.pe(fns, bankfree[b], tiles[t]["q"], tiles[t]["k"], tb)
            last["z", t] = tp
            s = n % 3
            ev, sp = EB_[n % 2][0:ks, 0:x1 - x0], SPB[s][0:ks, 0:x1 - x0]
            d = P.dve(ts_(ev, out, 40.0, None, ALU.min), tp, free.get(("e", n % 2)))
            a = P.act(act_(ev, ev, ACT.Exp), d)
            return P.act(act_(ev, ev, ACT.Ln, bias=1.0), a)

        def stage_a2(it, a):
            n, t, i, ci, kb, top = it
            c0, c1 = CHUNKS[ci]
            s0, ks = blk[kb]
            x0, x1 = max(c0, s0) - c0, c1 - c0
            s = n % 3
            out = PS[0:ks, n % 4 * 512 + x0:n % 4 * 512 + x1]
            ev, sp = EB_[n % 2][0:ks, 0:x1 - x0], SPB[s][0:ks, 0:x1 - x0]
            d = P.dve(tt_(sp, out, ev, ALU.max), a, free.get(("sp", s)))
            free[("e", n % 2)] = [d]
            sa = None
            if ks == 128:
                h, l = SPH[:, n % 4, 0:x1 - x0], SPL[:, n % 4, 0:x1 - x0]
                sa = P.act(act_(h, sp, ACT.Copy), d, free.get(("sph", n % 4)))
                free[("sp", s)] = [sa]
            else:
                free[("sp", s)] = []
            cur = state.get("acc")
            if kb:
                ns = (state.get("slot", 0) + 1) % 4
                state["slot"] = ns
                nxt = AB[ns]
                was = [free.get(("acc", ns)), free.get(("accr", ns)), free.get(("accw", ns))]
                if top:
                    dz = P.pool(lambda e: e.memset(nxt[:, 0:c1 - c0], 0.0), *was)
                    p = P.pool(cp_(nxt[0:ks, x0:x1], sp), dz, d)
                else:
                    cs_, ctok = cur[0], cur[1]
                    old = AB[cs_]
                    if ks < 128 or x0 > 0:
                        p = P.pool(cp_(nxt[:, 0:c1 - c0], old[:, 0:c1 - c0]), ctok, *was)
                        p = P.pool(tt_(nxt[0:ks, x0:x1], old[0:ks, x0:x1], sp, ALU.add), p, d)
                    else:
                        p = P.pool(tt_(nxt[:, x0:x1], old[:, x0:x1], sp, ALU.add), ctok, d, *was)
                    free[("accr", cs_)] = free[("accr", cs_)] + [p]
                free[("accw", ns)] = [p]
                free[("accr", ns)] = []
                state["acc"] = (ns, p)
                free[("sp", s)] = free[("sp", s)] + [p]
            return d, sa, cur

        def stage_a3(it, d, sa, cur):
            n, t, i, ci, kb, top = it
            c0, c1 = CHUNKS[ci]
            s0, ks = blk[kb]
            w = c1 - max(c0, s0)
            if ks == 128:
                sb = P.dve(tt_(SPL[:, n % 4, 0:w], SPB[n % 3][:, 0:w], SPH[:, n % 4, 0:w], ALU.subtract), sa,
                           free.get(("sph", n % 4)))
                free["spx", n] = [sa, sb]
                free[("sp", n % 3)] = free[("sp", n % 3)] + [sb]

        def stage_b(it, d, cur):
            n, t, i, ci, kb, top = it
            c0, c1 = CHUNKS[ci]
            s0, ks = blk[kb]
            x0, x1 = max(c0, s0) - c0, c1 - c0
            b = n % 4
            s = n % 3
            out = PS[0:ks, b * 512 + x0:b * 512 + x1]
            if ks == 128:
                fns = [mm_(out, NTRI[:, :], SPH[:, n % 4, 0:x1 - x0], False, False, True),
                       mm_(out, NTRI[:, :], SPL[:, n % 4, 0:x1 - x0], False, top, True)]
                d = free.pop(("spx", n))
            else:
                fns = [mm_(out, m("ntri")[0:ks, 0:ks], SPB[s][0:ks, 0:x1 - x0], False, top, True)]
            tacc = None
            if not top:
                tacc = cur[1]
                fns.append(mm_(out, m("nones")[:, 0:ks], AB[cur[0]][:, x0:x1], False, True, True))
            tp = P.pe(fns, d, tacc, tconst)
            if ks == 128:
                free[("sph", n % 4)] = [tp]
            else:
                free[("sp", s)] = free[("sp", s)] + [tp]
            if not top:
                free[("acc", cur[0])] = [tp]
            w = WB[n % 2][0:ks, 0:x1 - x0]
            a = P.act(act_(w, out, ACT.Exp), tp, free.get(("w", n % 2)))
            bankfree[b] = [a]
            return a

        def stage_c(it, a):
            n, t, i, ci, kb, top = it
            c0, c1 = CHUNKS[ci]
            s0, ks = blk[kb]
            x0, x1 = max(c0, s0) - c0, c1 - c0
            ob = 4 + i
            VT = V["vt"][t % 2]
            out = PS[64 * i:64 * i + 64, ob * 512 + x0:ob * 512 + x1]
            tp = P.pe([mm_(out, VT[0:ks, kb, 64 * i:64 * i + 64], WB[n % 2][0:ks, 0:x1 - x0],
                           top, kb == 0, True)], a, bankfree[ob], tiles[t]["v"])
            free[("w", n % 2)] = [tp]
            last["v", t] = tp
            if kb == 0:
                d = P.dve(cp_(OT[64 * i:64 * i + 64, t, c0:c1], PS[64 * i:64 * i + 64,
                                                                ob * 512:ob * 512 + c1 - c0]), tp)
                bankfree[ob] = [d]
                state["o"] = d
            else:
                bankfree[ob] = []

        fill = [None]

        def work(n):
            for _ in range(n):
                if fill[0] is not None and next(fill[0], "end") == "end":
                    fill[0] = None

        def step(it, w=0):
            pipe.insert(0, None)
            if pipe[2]:
                stage_a3(*pipe[2])
            if pipe[1]:
                pipe[1][1:] = stage_a2(*pipe[1])
            if pipe[3]:
                d, sa, cur = pipe[3][1:]
                pipe[3].append(stage_b(pipe[3][0], d, cur))
            work(w)
            if it is not None:
                pipe[0] = [it, stage_a(it)]
            work(w)
            if pipe[4]:
                stage_c(pipe[4][0], pipe[4][-1])
            pipe.pop()

        pipe = [None] * 5

        osplit = KToks([None] * 8)
        gtok = {}

        def gate(k):
            tl = P.dma("pool", "gin", lambda e: e.dma_start(GB, A["gs"][k]), gst[0], gst[1], tsp,
                       gtok.get(k - 1))
            gtok[k] = P.dve(tt_(OT[:, k, :], OT[:, k, :], GB, ALU.mult), tl, state["o"])

        def split(k):
            a = P.act(act_(XH[:, k, :], OT[:, k, :], ACT.Copy), gtok[k], xdone)
            q = P.pool(tt_(XL[:, k, :], OT[:, k, :], XH[:, k, :], ALU.subtract), a)
            osplit[k] = [a, q]

        def project(t):
            s = t % 2
            QT, KT_, VT = V["q"][s], V["k"][s], V["vt"][s]
            fr = [last.get(("z", t - 2)), last.get(("v", t - 2)), tsp]
            tl = {}
            nb = 0
            for which, dst, scale in (("q", QT, 0.125), ("k", KT_, 1.0), ("v", VR, 1.0)):
                iw, wh, wl, wt = W.get(f"Q.{8 * 'qkv'.index(which) + t}")
                toks = []
                for c, (c0, c1) in enumerate(CHUNKS):
                    b = 6 + nb % 2
                    nb += 1
                    P.wait("pe", [bankfree[b], wt, xt[c]])
                    for k, (a, b_, x, y) in enumerate(unit8(wh, wl, c0, c1)):
                        tk = P.pe(mm3(bank(b, c1 - c0), a, b_, x, y, k == 0, k == 7))
                        if k < 7:
                            yield
                    a = P.act(act_(dst[:, c0:c1], bank(b, c1 - c0), ACT.Copy, scale=scale), tk,
                              last["vr"] if which == "v" else fr)
                    bankfree[b] = [a]
                    toks.append(a)
                    yield
                W.done(iw, tk)
                tl[which] = toks
            if t == 7:
                xdone.append(tk)
            for part in range(3):
                bs = blk[4 * part:4 * part + 4]
                b = 6 + nb % 2
                nb += 1
                tp = P.pe([tr_(PS[0:w, b * 512 + 128 * j:b * 512 + 128 * j + 128], VR[:, t0:t0 + w])
                           for j, (t0, w) in enumerate(bs)], tl["v"], bankfree[b], tc)
                w = bs[0][1]
                i_ = PS[0:w, b * 512:b * 512 + 128 * len(bs)].rearrange("p (a b) -> p a b", a=len(bs))
                dv = P.dve(cp_(VT[0:w, 4 * part:4 * part + len(bs), :], i_), tp, fr)
                bankfree[b] = [dv]
                yield
            last["vr"] = tp
            tl["v"] = dv
            tiles[t] = tl

        xdone = []
        for _ in project(0):
            pass
        n = 0
        for t in range(8):
            m_ = 0
            fill[0] = project(t + 1) if t < 7 else None
            for ci in range(3):
                top = (CHUNKS[ci][1] - 1) // 128
                for i in range(2):
                    for kb in range(top, -1, -1):
                        step((n, t, i, ci, kb, kb == top), 1)
                        n += 1
                        m_ += 1
                        if t and m_ == 6:
                            gate(t - 1)
                        if t == 7 and m_ > 6 and m_ % 4 == 0 and osplit[6] is None:
                            split(sum(s is not None for s in osplit))
            work(1000)
        for _ in range(5):
            step(None)
        gate(7)
        split(7)
        end = [("dve", P.n["dve"]), ("pe", P.n["pe"])]
        back = [restore_tile(f, end) for f in range(8)]
        return add_gemm("QO", [osplit] * 3, lambda f: back[f], None)

    def final(toks):
        exp_ln_tables()
        cuts = [(max(c0, META), c1) for c0, c1 in CHUNKS]

        gens = [stats(h_src, 8, *cuts[ci], toks[ci], ci % 2, D, 1.0, statbusy) for ci in range(3)]

        def squares(ci):
            for _ in range(8):
                next(gens[ci])

        def apply(ci):
            tr = next(gens[ci])
            c0, c1 = cuts[ci]
            rs = 2 + 2 * (ci % 2)
            for k in range(8):
                x = h_src(k, c0, c1)
                d = P.dve(stt_(x, x, v("final_norm_2", k), TT[rs][:, 0:c1 - c0], ALU.mult, ALU.mult), tr)
                tfree[rs] = [d]
                if k % 2:
                    load("sp" if k % 4 == 1 else "act", f"out{ci}{k}", A["out"][:, k - 1:k + 1, c0 - META:c1 - META],
                         RES[:, k - 1:k + 1, c0:c1], d)

        squares(0)
        squares(1)
        apply(0)
        squares(2)
        apply(1)
        apply(2)

    def run():
        tx = [[], []]
        for c, (c0, c1) in enumerate(FFN_CHUNKS):
            for k in range(0, 8, 2):
                t = load(("act", "pool")[k // 2 % 2], f"x{c}{k}", RES[:, k:k + 2, META + c0:META + c1],
                         A["x"][:, k:k + 2, c0:c1])
                tx[c] += [[t], [t]]
        tm = load("act", "meta", RES[:, :, 0:META], A["meta"])
        exp_ln_tables()
        xt = chains([(tx[c], None, (res_src, "ffn1_pre_g", c0, c1)) for c, (c0, c1) in enumerate(FFN_CHUNKS)], [])
        xt = ffn(1, xt, to_first("mix_pre_g"))
        xt = mixer(xt, to_first("ffn2_pre_g"))
        if xt is None:
            return
        P.wait("act", [tm])
        P.wait("dve", [tm])
        xt = ffn(2, xt, to_second)
        xt = even(xt)
        toks = odd(xt)
        final(toks)

    run()
    P.wait("sp", [(sem, v) for sem, v in sorted(P.dman.items())])
    return P, W


def layout(nc, ctx):
    F32, F32R, BF = mybir.dt.float32, mybir.dt.float32r, mybir.dt.bfloat16
    base = 16512
    S = {}

    def at(name, shape, dt, off):
        return nc.alloc_sbuf_tensor_at(name, [128] + shape, dt, offset=off)

    o = base
    S["vec"] = at("vec", [NVEC], F32, o)
    o += (NVEC * 4 + 31) // 32 * 32
    S["mat"] = at("mat", [len(MATS) * 128], F32, o)
    o += len(MATS) * 512
    S["mat2"] = at("mat2", [len(MATS2) * 128], F32, o)
    lam = at("mlam", [384], F32, o)
    otm = at("motm", [128], F32, o + 1536)
    o += len(MATS2) * 512
    for n in ("idb", "cmb", "smb"):
        S[n] = at(n, [128], BF, o)
        o += 256
    S["raw"] = [at(f"raw{i}", [1024], F32, o + 4096 * i) for i in range(2)]
    o += 8192
    S["whi"] = [at(f"whi{i}", [1024], F32R, o + 8192 * i) for i in range(3)]
    S["wlo"] = [at(f"wlo{i}", [1024], F32R, o + 8192 * i + 4096) for i in range(3)]
    o += 24576
    S["res"] = at("res", [8, T2], F32, o)
    o += 8 * T2 * 4
    S["xh"] = at("xh", [8, T2], F32R, o)
    S["xl"] = at("xl", [8, T2], F32R, o + 8 * T2 * 4)
    o += 2 * 8 * T2 * 4
    free0 = o
    arena = at("arena", [(229344 - free0) // 4], F32, free0)

    def cut(off, shape):
        n = 1
        for k in shape:
            n *= k
        ap = arena[:, off // 4:off // 4 + n]
        return ap if len(shape) == 1 else ap.rearrange("p (a b) -> p a b", a=shape[0])

    S["acc"] = cut(0, [8, T1])
    S["hh"] = at("hh", [4, T1], F32R, free0 + 32768)
    S["hl"] = at("hl", [4, T1], F32R, free0 + 49152)
    S["t"] = [cut(off + 2048 * i, [512]) for off in (65536, 57344) for i in range(4)]
    S["ot"] = cut(0, [8, T1])
    M = S["mix"] = {}
    q0 = 32768
    ar3 = at("arena3", [8 * T2], F32, free0 - 3 * 8 * T2 * 4)

    def cut3(off, shape):
        n = 1
        for k in shape:
            n *= k
        ap = ar3[:, off // 4:off // 4 + n]
        return ap if len(shape) == 1 else ap.rearrange("p (a b) -> p a b", a=shape[0])

    M["q"], M["k"] = [cut(q0, [T1]), cut3(0, [T1])], [cut(q0 + 4096, [T1]), cut3(4096, [T1])]
    M["vt"] = [cut(q0 + 8192, [8, 128]), cut3(8192, [8, 128])]
    M["ncb"] = [[cut(q0 + 12288 + 4096 * i, [T1]) for i in range(2)],
                [cut3(16384 + 4096 * i, [T1]) for i in range(2)]]
    M["vr"], M["rt"] = cut3(12288, [T1]), cut3(24576, [T1])
    M["sq"] = cut3(29184, [128])
    M["nc8"] = cut(q0 + 20480, [T1])
    cs = M["cs"] = cut(q0 + 12288, [2, T1])
    M["cos"], M["sin"] = cs[:, 0, :], cs[:, 1, :]
    M["pt"] = [cut(q0 + 24576 + 4096 * i, [T1]) for i in range(2)]
    M["p"] = [cut(q0 + 32768 + 4096 * i, [T1]) for i in range(2)]
    M["otm"], M["lam"] = [otm, cut3(28672, [128])], lam
    M["sm"] = cut(q0 + 40960, [128])
    f = free0
    S["uh"], S["ul"] = at("uh", [2, T2], F32R, f), at("ul", [2, T2], F32R, f + 8320)
    S["yh"], S["yl"] = at("yh", [2, T2], F32R, f + 16640), at("yl", [2, T2], F32R, f + 24960)
    V = S["lru"] = {}
    V["xin"] = [cut(33280, [T2 + 8]), cut(70720, [T2 + 8])]
    V["g"] = cut(66560, [T2])
    V["zb"] = [cut(62688 + 1408 * i, [352]) for i in range(2)]
    V["u"] = [cut(37472 + 4160 * i, [T2]) for i in range(2)]
    V["tb"] = [cut(45792 + 4160 * i, [T2]) for i in range(4)]
    V["sm"] = cut(62432, [64])
    V = S["ssd"] = {}
    V["x"] = cut(0, [9, 1024])
    V["bc"] = cut(36864, [4, T2])
    V["bt"] = cut(53504, [9, 256])
    V["dt"] = cut(62720, [9, 16])
    V["xin"] = cut(63296, [T2 + 8])
    V["cv"] = cut(67488, [T2])
    V["xin2"], V["cv2"] = cut3(0, [T2 + 8]), cut3(4192, [T2])
    V["zb"] = [cut3(8352 + 1408 * i, [352]) for i in range(2)]
    V["zin"] = [cut(4160 * i, [T2]) for i in range(8)]
    ar2 = at("arena2", [2 * 8 * T2], F32, free0 - 2 * 8 * T2 * 4)
    Q = S["scan"] = {}
    pos = 0
    for name, num, width in (("state", 2, 512), ("gt", 2, 1024), ("m", 2, 1024), ("cbm", 2, 128),
                             ("xd", 2, 512), ("xs", 2, 512), ("tx", 2, 512), ("y", 2, 1024),
                             ("ad", 1, 144), ("ex", 1, 432), ("ddt", 1, 144)):
        Q[name] = []
        for _ in range(num):
            Q[name].append(ar2[:, pos:pos + width])
            pos += width
    for name in ("ad", "ex", "ddt"):
        Q[name] = Q[name][0]
    Q["aneg"] = ar2[:, pos:pos + 16]
    V = S["odd"] = {}
    V["ot"] = cut(0, [8, T2])
    V["q"], V["k"], V["vr"] = (cut(33280 + 4160 * i, [T2]) for i in range(3))
    V["q"], V["k"] = [V["q"], cut3(0, [T2])], [V["k"], cut3(4160, [T2])]
    V["gb"] = cut3(8320, [T2])
    r0 = free0 - 3 * 8 * T2 * 4 + 17088
    V["sph"], V["spl"] = at("sph", [4, 352], F32R, r0), at("spl", [4, 352], F32R, r0 + 5632)
    V["ntri"] = at("ntri_r", [128], F32R, free0 + 65536)
    V["vt"] = [cut(45760, [9, 128]), cut3(12480, [9, 128])]
    pos = 50368
    for name, num in (("sp", 3), ("e", 2), ("w", 2)):
        V[name] = [cut(pos + 1408 * i, [352]) for i in range(num)]
        pos += 1408 * num
    V["acc"] = [cut(66560 + 1408 * i, [352]) for i in range(4)]
    S["ps"] = ctx.enter_context(nc.psum_tensor("ps", [128, 4096], F32))
    return S


def build(nc, A):
    from contextlib import ExitStack
    with ExitStack() as ctx:
        S = layout(nc, ctx)
        _, W = emit(nc, A, S, None)
        P, _ = emit(nc, A, S, W.asked)
        names = list(Prog.ENG) + sorted(P.dman)
        sems = {n: ctx.enter_context(nc.semaphore("s_" + n)) for n in names}
        block = ctx.enter_context(nc.Block())

        def play(eng, key):
            for item in P.q[key]:
                if item[0] == "wait":
                    eng.wait_ge(sems[item[1]], item[2])
                else:
                    ins = item[1](eng)
                    if item[2] is not None:
                        ins.then_inc(sems[item[2]], item[3])

        @block.tensor
        def _(eng):
            play(eng, "pe")

        @block.scalar
        def _(eng):
            play(eng, "act")

        @block.vector
        def _(eng):
            play(eng, "dve")

        @block.gpsimd
        def _(eng):
            play(eng, "pool")

        @block.sync
        def _(eng):
            play(eng, "sp")


def _tiles(w):
    K, N = w.shape
    return w.reshape(K // 128, 128, N // 128, 128).transpose(2, 1, 0, 3).reshape(N // 128, 128, -1)


def _pairs(w):
    return w.reshape(2, 128, 2, 512).transpose(2, 1, 0, 3).reshape(2, 128, 1024)


def _pack(I):
    U = {}

    def put(prefix, arr):
        for i, a in enumerate(arr):
            U[f"{prefix}.{i}"] = a

    for f in (1, 2):
        put(f"G{f}", _tiles(I[f"ffn{f}_w_gate"][0]))
        put(f"U{f}", _tiles(I[f"ffn{f}_w_up"][0]))
        wd = I[f"ffn{f}_w_down"][0]
        for b in range(11):
            put(f"D{f}.{b}", _pairs(wd[256 * b:256 * b + 256]))
    w = I["w_in"][0]
    w = np.concatenate([w[:, 0:1536], w[:, 1544:3080], w[:, 1536:1544], np.zeros((D, 120), w.dtype)], axis=1)
    put("IN", _tiles(w))
    put("OUT", _tiles(I["w_out"][0]))
    w = I["even_w_in_2"][0]
    w = np.concatenate([w, np.zeros((D, 112), w.dtype)], axis=1)
    put("E", _tiles(w))
    for g in range(4):
        wa = I["lru_w_a_2"][0, g].reshape(2, 128, 256).transpose(1, 0, 2).reshape(128, 512)
        wx = I["lru_w_x_2"][0, g].reshape(2, 128, 256).transpose(1, 0, 2).reshape(128, 512)
        U[f"L.{g}"] = np.concatenate([wa, wx], axis=1)
        put(f"EO.{g}", _pairs(I["even_w_out_2"][0][256 * g:256 * g + 256]))
    put("EB", _tiles(I["even_w_out_2"][0][1024:]))
    put("Q", _tiles(I["odd_w_in_2"][0]))
    put("QO", _tiles(I["odd_w_out_2"][0]))
    return np.stack([U[n] for n in UNITS])


def _vectors(I):
    out = np.zeros((128, NVEC), np.float32)

    def fm(a):
        return a.reshape(-1, 128).T

    for n in ("ffn1_pre_g", "ffn1_post_g", "mix_pre_g", "mix_post_g", "ffn2_pre_g", "ffn2_post_g",
              "even_norm_2", "odd_norm_2", "final_norm_2", "lru_conv_b_2", "lru_b_a_2", "lru_b_x_2",
              "lru_lambda_2", "ssd_conv_b_2", "ssd_norm_2"):
        a = fm(I[n].reshape(-1))
        out[:, VEC[n]:VEC[n] + a.shape[1]] = a
    for n, w in (("lru_conv_w_2", 8), ("ssd_conv_w_2", 12)):
        for k in range(4):
            out[:, VEC[n] + k * w:VEC[n] + (k + 1) * w] = fm(I[n][0, k])
    out[0:8, VEC["fox_forget_b"]] = I["fox_forget_b"][0]
    out[0:16, VEC["ssd_dt_bias_2"]] = I["ssd_dt_bias_2"][0]
    for n, w in (("ssd_a_log_2", 16), ("ssd_d_2", 16)):
        out[:, VEC[n]:VEC[n] + w] = I[n].reshape(1, w)
    return out


def _mats():
    p = np.arange(128)
    i, j = p[:, None], p[None, :]
    M = {"ident": i == j, "ones": i >= 0 * j, "triu": i <= j, "low": i > j}
    M = {k: a.astype(np.float32) for k, a in M.items()}
    M["ntri"] = -(i >= j).astype(np.float32)
    M["nones"] = -np.ones((128, 128), np.float32)
    rot = np.zeros((128, 128), np.float32)
    for b in (0, 64):
        for a in range(8):
            rot[b + a + 8, b + a] = -1.0
            rot[b + a, b + a + 8] = 1.0
    M["rot"] = rot
    M["cmask"] = np.where(j > i, NEG, 0.0).astype(np.float32)
    M["smask"] = np.where(i >= j, NEG, 0.0).astype(np.float32)
    return [np.concatenate([M[n] for n in names], axis=1) for names in (MATS, MATS2, ("cmask", "smask"))]


def _rope():
    inv = (np.float32(500000.0) ** (-np.arange(0, 16, 2, dtype=np.float32) / np.float32(16))).astype(np.float32)
    ang = np.arange(T1, dtype=np.float32)[None, :] * inv[:, None]
    c, s = np.ones((128, T1), np.float32), np.zeros((128, T1), np.float32)
    for b in (0, 8, 64, 72):
        c[b:b + 8], s[b:b + 8] = np.cos(ang), np.sin(ang)
    return np.stack([c, s], axis=1)


def kernel(**inputs):
    import concourse.bacc as _bacc
    from concourse.bass_utils import run_bass_kernel_spmd as _run

    I = {k: np.asarray(a) for k, a in inputs.items()}
    fm = lambda a: np.ascontiguousarray(a.T.reshape(8, 128, -1).transpose(1, 0, 2))
    lam = np.concatenate([I[f"diff_lambda_{n}"].reshape(-1) for n in ("q1", "k1", "q2", "k2")]
                         + [I["diff_subln_g"].reshape(-1)])
    arrays = {
        "in_x_dram": fm(I["x"][0]),
        "in_meta_dram": fm(I["meta_2"]),
        "in_w_dram": _pack(I),
        "in_vec_dram": _vectors(I),
        "in_lam_dram": np.ascontiguousarray(np.broadcast_to(lam[None, :], (128, 384))),
        "in_mat_dram": _mats()[0],
        "in_mat2_dram": _mats()[1],
        "in_masks_dram": _mats()[2],
        "in_rope_dram": _rope(),
    }
    nc = _bacc.Bacc("TRN2", target_bir_lowering=False, num_devices=1)
    A = {}
    for name, a in arrays.items():
        A[name[3:-5]] = nc.dram_tensor(name, a.shape, mybir.dt.from_np(a.dtype), kind="ExternalInput").ap()
    A["out"] = nc.dram_tensor("out_0_dram", (128, 8, T1), mybir.dt.float32, kind="ExternalOutput").ap()
    A["zs"] = nc.dram_tensor("zs_scratch", (8, 128, T2), mybir.dt.float32).ap()
    A["gs"] = nc.dram_tensor("gs_scratch", (8, 128, T2), mybir.dt.float32).ap()
    A["rs"] = nc.dram_tensor("rs_scratch", (128, 8, T2), mybir.dt.float32).ap()
    build(nc, A)
    r = _run(nc, [arrays], core_ids=[0])
    got = r.results[0]["out_0_dram"]
    return np.ascontiguousarray(got.transpose(1, 0, 2).reshape(D, T1).T[None])
```
